# Optimizing a Trainium2 kernel written in Bass

```python
import math
import jax, jax.numpy as jnp
from jax import lax
import numpy as np

D_MODEL = 1024
BATCH = 1
SEQ = 256
DEPTH = 2

N_Q_HEADS = 8
N_KV_HEADS = 2
HEAD_DIM = 64
Q_GROUP = N_Q_HEADS // N_KV_HEADS
WINDOW = 128
BLOCK = 128
ROPE_THETA = 500000.0
ROT_DIM = HEAD_DIM // 4
ATTN_WIDTH = N_Q_HEADS * HEAD_DIM
KV_WIDTH = N_KV_HEADS * HEAD_DIM
NEG_INF = -1e30
CONV_WIDTH = D_MODEL // 2
CONV_K = 3
SSM_WIDTH = D_MODEL // 2
SSM_GROUP = 16
SSM_GROUPS = SSM_WIDTH // SSM_GROUP
SSM_STATE = 64
DT_MIN = 1e-3
DT_MAX = 1e-1
N_BRANCH = 3
GATE_WIDTH = N_BRANCH * D_MODEL
FFN_HIDDEN = -(-8 * D_MODEL // (3 * 256)) * 256
NORM_EPS = 1e-6

IN_SIZES = (ATTN_WIDTH, KV_WIDTH, KV_WIDTH, CONV_WIDTH, CONV_WIDTH, CONV_WIDTH, SSM_WIDTH, GATE_WIDTH)
IN_COLS = sum(IN_SIZES)
IN_SPLITS = tuple(int(v) for v in np.cumsum(IN_SIZES)[:-1])


def rmsnorm(x, g):
    xf = x.astype(jnp.float32)
    y = xf * lax.rsqrt(jnp.mean(xf * xf, axis=-1, keepdims=True) + NORM_EPS)
    return (y * g.astype(jnp.float32)).astype(x.dtype)

def rope_tables(seq_len):
    pos = jnp.arange(seq_len, dtype=jnp.float32)
    inv_freq = ROPE_THETA ** (-jnp.arange(0, ROT_DIM, 2, dtype=jnp.float32) / ROT_DIM)
    ang = pos[:, None] * inv_freq[None, :]
    return jnp.cos(ang), jnp.sin(ang)

def partial_rope(t, cos, sin):
    half = ROT_DIM // 2
    tf = t.astype(jnp.float32)
    t1, t2, rest = tf[..., :half], tf[..., half:ROT_DIM], tf[..., ROT_DIM:]
    c = cos[None, :, None, :]
    s = sin[None, :, None, :]
    out = jnp.concatenate([t1 * c - t2 * s, t2 * c + t1 * s, rest], axis=-1)
    return out.astype(t.dtype)

def sliding_window_attention(q, k, v, sinks):
    b, l = q.shape[0], q.shape[1]
    nb = l // BLOCK
    qb = q.reshape(b, nb, BLOCK, N_KV_HEADS, Q_GROUP, HEAD_DIM).astype(jnp.float32)

    def band(t):
        tp = jnp.pad(t, ((0, 0), (BLOCK, 0), (0, 0), (0, 0)))
        tp = tp.reshape(b, nb + 1, BLOCK, N_KV_HEADS, HEAD_DIM)
        return jnp.concatenate([tp[:, :-1], tp[:, 1:]], axis=2).astype(jnp.float32)

    kb, vb = band(k), band(v)
    s = jnp.einsum("bnqkgd,bnskd->bnkgqs", qb, kb) * (HEAD_DIM ** -0.5)
    qi = jnp.arange(BLOCK)[:, None]
    kj = jnp.arange(2 * BLOCK)[None, :]
    delta = qi + BLOCK - kj
    band_ok = (delta >= 0) & (delta < WINDOW)
    kpos = jnp.arange(nb)[:, None] * BLOCK - BLOCK + kj
    mask = band_ok[None, :, :] & (kpos >= 0)[:, None, :]
    s = jnp.where(mask[None, :, None, None, :, :], s, NEG_INF)
    sink = sinks.astype(jnp.float32).reshape(N_KV_HEADS, Q_GROUP)[None, None, :, :, None, None]
    m = jnp.maximum(jnp.max(s, axis=-1, keepdims=True), sink)
    p = jnp.exp(s - m)
    denom = jnp.sum(p, axis=-1, keepdims=True) + jnp.exp(sink - m)
    o = jnp.einsum("bnkgqs,bnskd->bnqkgd", p / denom, vb)
    return o.reshape(b, l, ATTN_WIDTH).astype(q.dtype)

def short_conv(z, w):
    l = z.shape[1]
    zp = jnp.pad(z, ((0, 0), (CONV_K - 1, 0), (0, 0)))
    y = w[0] * zp[:, 0:l]
    for j in range(1, CONV_K):
        y = y + w[j] * zp[:, j:j + l]
    return y

def s5_ssm(u, a_re, a_im, b_re, b_im, c_re, c_im, d, log_dt):
    bsz, l = u.shape[0], u.shape[1]
    uf = u.astype(jnp.float32).reshape(bsz, l, SSM_GROUPS, SSM_GROUP)
    lam = lax.complex(a_re.astype(jnp.float32), a_im.astype(jnp.float32))
    dt = jnp.exp(log_dt.astype(jnp.float32))[:, None]
    lam_bar = jnp.exp(lam * dt)
    b_c = lax.complex(b_re.astype(jnp.float32), b_im.astype(jnp.float32))
    b_bar = ((lam_bar - 1.0) / lam)[..., None] * b_c
    bu = jnp.einsum("blgh,gph->blgp", uf.astype(jnp.complex64), b_bar)
    a_elems = jnp.broadcast_to(lam_bar, bu.shape)

    def combine(e1, e2):
        a1, x1 = e1
        a2, x2 = e2
        return a1 * a2, a2 * x1 + x2

    _, states = lax.associative_scan(combine, (a_elems, bu), axis=1)
    c_c = lax.complex(c_re.astype(jnp.float32), c_im.astype(jnp.float32))
    y = jnp.einsum("blgp,ghp->blgh", states, c_c).real
    y = y + d.astype(jnp.float32).reshape(SSM_GROUPS, SSM_GROUP) * uf
    return y.reshape(bsz, l, SSM_WIDTH).astype(u.dtype)

def first_inputs(seed: int = 0) -> dict:
    key = jax.random.key(seed)
    ks = jax.random.split(key, 24)
    L = DEPTH

    def nrm(k, shape, fan_in):
        return jax.random.normal(k, shape, jnp.float32) * (fan_in ** -0.5)

    x = jax.random.normal(ks[0], (BATCH, SEQ, D_MODEL), jnp.float32)
    norm_mix = 1.0 + 0.02 * jax.random.normal(ks[1], (L, D_MODEL), jnp.float32)
    w_in = nrm(ks[2], (L, D_MODEL, IN_COLS), D_MODEL)
    b_gate = 0.02 * jax.random.normal(ks[3], (L, GATE_WIDTH), jnp.float32)
    attn_sinks = 0.5 * jax.random.normal(ks[4], (L, N_Q_HEADS), jnp.float32)
    w_attn_o = nrm(ks[5], (L, ATTN_WIDTH, D_MODEL), ATTN_WIDTH)
    conv_w = nrm(ks[6], (L, CONV_K, CONV_WIDTH), CONV_K)
    w_conv_o = nrm(ks[7], (L, CONV_WIDTH, D_MODEL), CONV_WIDTH)
    ssm_a_re = -0.5 + 0.01 * jax.random.normal(ks[8], (L, SSM_GROUPS, SSM_STATE), jnp.float32)
    ssm_a_im = (math.pi * jnp.arange(SSM_STATE, dtype=jnp.float32))[None, None, :] \
        + 0.01 * jax.random.normal(ks[9], (L, SSM_GROUPS, SSM_STATE), jnp.float32)
    ssm_b_re = nrm(ks[10], (L, SSM_GROUPS, SSM_STATE, SSM_GROUP), 2 * SSM_GROUP)
    ssm_b_im = nrm(ks[11], (L, SSM_GROUPS, SSM_STATE, SSM_GROUP), 2 * SSM_GROUP)
    ssm_c_re = nrm(ks[12], (L, SSM_GROUPS, SSM_GROUP, SSM_STATE), 2 * SSM_STATE)
    ssm_c_im = nrm(ks[13], (L, SSM_GROUPS, SSM_GROUP, SSM_STATE), 2 * SSM_STATE)
    ssm_d = jax.random.normal(ks[14], (L, SSM_WIDTH), jnp.float32)
    ssm_log_dt = jax.random.uniform(ks[15], (L, SSM_GROUPS), jnp.float32,
                                    minval=math.log(DT_MIN), maxval=math.log(DT_MAX))
    w_ssm_glu = nrm(ks[16], (L, SSM_WIDTH, SSM_WIDTH), SSM_WIDTH)
    w_ssm_o = nrm(ks[17], (L, SSM_WIDTH, D_MODEL), SSM_WIDTH)
    w_mix_o = nrm(ks[18], (L, D_MODEL, D_MODEL), D_MODEL)
    norm_ffn = 1.0 + 0.02 * jax.random.normal(ks[19], (L, D_MODEL), jnp.float32)
    w_ffn_in = nrm(ks[20], (L, D_MODEL, 2 * FFN_HIDDEN), D_MODEL)
    w_ffn_out = nrm(ks[21], (L, FFN_HIDDEN, D_MODEL), FFN_HIDDEN)
    norm_final = 1.0 + 0.02 * jax.random.normal(ks[22], (D_MODEL,), jnp.float32)
    return {"x": x, "norm_mix": norm_mix, "w_in": w_in, "b_gate": b_gate,
            "attn_sinks": attn_sinks, "w_attn_o": w_attn_o, "conv_w": conv_w, "w_conv_o": w_conv_o,
            "ssm_a_re": ssm_a_re, "ssm_a_im": ssm_a_im, "ssm_b_re": ssm_b_re, "ssm_b_im": ssm_b_im,
            "ssm_c_re": ssm_c_re, "ssm_c_im": ssm_c_im, "ssm_d": ssm_d, "ssm_log_dt": ssm_log_dt,
            "w_ssm_glu": w_ssm_glu, "w_ssm_o": w_ssm_o, "w_mix_o": w_mix_o, "norm_ffn": norm_ffn,
            "w_ffn_in": w_ffn_in, "w_ffn_out": w_ffn_out, "norm_final": norm_final}

def first_block(x, norm_mix, w_in, b_gate, attn_sinks, w_attn_o, conv_w, w_conv_o,
              ssm_a_re, ssm_a_im, ssm_b_re, ssm_b_im, ssm_c_re, ssm_c_im, ssm_d, ssm_log_dt,
              w_ssm_glu, w_ssm_o, w_mix_o, norm_ffn, w_ffn_in, w_ffn_out, norm_final):
    b, l = x.shape[0], x.shape[1]
    cos, sin = rope_tables(l)
    for i in range(DEPTH):
        h = rmsnorm(x, norm_mix[i])
        proj = h @ w_in[i]
        q, k, v, cb, cc, cx, u, g = jnp.split(proj, IN_SPLITS, axis=-1)
        q = partial_rope(q.reshape(b, l, N_Q_HEADS, HEAD_DIM), cos, sin)
        k = partial_rope(k.reshape(b, l, N_KV_HEADS, HEAD_DIM), cos, sin)
        v = v.reshape(b, l, N_KV_HEADS, HEAD_DIM)
        y_attn = sliding_window_attention(q, k, v, attn_sinks[i]) @ w_attn_o[i]
        y_conv = (cb * short_conv(cc * cx, conv_w[i])) @ w_conv_o[i]
        ys = jax.nn.gelu(s5_ssm(u, ssm_a_re[i], ssm_a_im[i], ssm_b_re[i], ssm_b_im[i],
                                ssm_c_re[i], ssm_c_im[i], ssm_d[i], ssm_log_dt[i]))
        y_ssm = (ys * jax.nn.sigmoid(ys @ w_ssm_glu[i])) @ w_ssm_o[i]
        gates = jax.nn.sigmoid(g + b_gate[i]).reshape(b, l, N_BRANCH, D_MODEL)
        merged = gates[:, :, 0] * y_attn + gates[:, :, 1] * y_conv + gates[:, :, 2] * y_ssm
        x = x + merged @ w_mix_o[i]
        h = rmsnorm(x, norm_ffn[i])
        gt, up = jnp.split(h @ w_ffn_in[i], 2, axis=-1)
        x = x + (jax.nn.silu(gt) * up) @ w_ffn_out[i]
    return rmsnorm(x, norm_final)


EPS = 1e-6
CHUNK = 128

RET_HEADS = 4
RET_DK = 256
RET_DV = 512
RET_QK = RET_HEADS * RET_DK
RET_V = RET_HEADS * RET_DV
ROPE_BASE = 10000.0

SSD_INNER = 2 * D_MODEL
SSD_HEADDIM = 64
SSD_HEADS = SSD_INNER // SSD_HEADDIM
SSD_GROUPS = 4
SSD_HPG = SSD_HEADS // SSD_GROUPS
SSD_STATE = 128
SSD_CONV = 4
SSD_BC = SSD_GROUPS * SSD_STATE
SSD_CONV_CH = SSD_INNER + 2 * SSD_BC

D_FF = -(-8 * D_MODEL // (3 * 256)) * 256

IN_SIZES_2 = (RET_QK, RET_QK, RET_V, RET_V, SSD_INNER, SSD_CONV_CH, SSD_HEADS, D_MODEL, D_MODEL)
D_IN = sum(IN_SIZES_2)


def rmsnorm_2(x, w):
    xf = x.astype(jnp.float32)
    y = xf * lax.rsqrt(jnp.mean(xf * xf, axis=-1, keepdims=True) + EPS)
    return (y * w.astype(jnp.float32)).astype(x.dtype)

def rotary(t, pos):
    half = t.shape[-1] // 2
    inv = ROPE_BASE ** (-jnp.arange(half, dtype=jnp.float32) / half)
    ang = pos.astype(jnp.float32)[:, None] * inv[None, :]
    cos = jnp.cos(ang)[None, :, None, :]
    sin = jnp.sin(ang)[None, :, None, :]
    t1, t2 = t[..., :half], t[..., half:]
    return jnp.concatenate([t1 * cos - t2 * sin, t1 * sin + t2 * cos], axis=-1)

def retention(q, k, v):
    bsz, s = q.shape[0], q.shape[1]
    nc = s // CHUNK
    log_g = jnp.log(1.0 - 2.0 ** (-5.0 - jnp.arange(RET_HEADS, dtype=jnp.float32)))
    idx = jnp.arange(CHUNK, dtype=jnp.float32)
    diff = idx[:, None] - idx[None, :]
    causal = diff >= 0
    intra = jnp.where(causal[None], jnp.exp(log_g[:, None, None] * jnp.maximum(diff, 0.0)[None]), 0.0)
    q_decay = jnp.exp(log_g[:, None] * (idx + 1.0))[None, :, :, None]
    k_decay = jnp.exp(log_g[:, None] * (CHUNK - 1.0 - idx))[None, :, :, None]
    chunk_decay = jnp.exp(log_g * CHUNK)[None, :, None, None]

    def to_chunks(t):
        return t.reshape(bsz, nc, CHUNK, RET_HEADS, t.shape[-1]).transpose(1, 0, 3, 2, 4)

    def step(state, inp):
        qc, kc, vc = inp
        sc = jnp.einsum('bhid,bhjd->bhij', qc, kc) * intra[None]
        y = jnp.einsum('bhij,bhjv->bhiv', sc, vc) + jnp.einsum('bhid,bhdv->bhiv', qc, state) * q_decay
        state = state * chunk_decay + jnp.einsum('bhjd,bhjv->bhdv', kc * k_decay, vc)
        return state, y

    init = jnp.zeros((bsz, RET_HEADS, RET_DK, RET_DV), jnp.float32)
    _, ys = lax.scan(step, init, (to_chunks(q), to_chunks(k), to_chunks(v)))
    return ys.transpose(1, 0, 3, 2, 4).reshape(bsz, s, RET_HEADS, RET_DV)

def ssd_scan(xdt, la, bm, cm):
    bsz, s = xdt.shape[0], xdt.shape[1]
    nc = s // CHUNK
    mask = jnp.tril(jnp.ones((CHUNK, CHUNK), dtype=bool))[None, :, :, None, None]

    def to_chunks(t):
        return jnp.moveaxis(t.reshape((bsz, nc, CHUNK) + t.shape[2:]), 1, 0)

    def step(state, inp):
        xc, lac, bc, cc = inp
        acs = jnp.cumsum(lac, axis=1)
        seg = acs[:, :, None] - acs[:, None, :]
        lmat = jnp.where(mask, jnp.exp(jnp.where(mask, seg, 0.0)), 0.0)
        cb = jnp.einsum('bign,bjgn->bijg', cc, bc)
        y = jnp.einsum('bijgr,bjgrp->bigrp', cb[..., None] * lmat, xc)
        y = y + jnp.einsum('bign,bgrpn->bigrp', cc, state) * jnp.exp(acs)[..., None]
        last = acs[:, -1]
        state = state * jnp.exp(last)[..., None, None] + jnp.einsum(
            'bjgn,bjgrp->bgrpn', bc, xc * jnp.exp(last[:, None] - acs)[..., None])
        return state, y

    init = jnp.zeros((bsz, SSD_GROUPS, SSD_HPG, SSD_HEADDIM, SSD_STATE), jnp.float32)
    _, ys = lax.scan(step, init, (to_chunks(xdt), to_chunks(la), to_chunks(bm), to_chunks(cm)))
    return jnp.moveaxis(ys, 0, 1).reshape(xdt.shape)

def causal_dwconv(x, w, b):
    out = lax.conv_general_dilated(
        x, w[:, None, :], window_strides=(1,), padding=[(SSD_CONV - 1, 0)],
        dimension_numbers=('NWC', 'WIO', 'NWC'), feature_group_count=x.shape[-1])
    return out + b

def hybrid_mixer(h, w_in, ret_out, conv_w, conv_b, dt_bias, a_log, d_skip, ssd_norm_w, ssd_out, w_o):
    bsz, s, _ = h.shape
    u = h @ w_in
    q, k, v, g_ret, z, xbc, dt, gate_ret, gate_ssd = jnp.split(u, list(np.cumsum(IN_SIZES_2)[:-1]), axis=-1)
    pos = jnp.arange(s)

    qf = rotary(q.astype(jnp.float32).reshape(bsz, s, RET_HEADS, RET_DK), pos)
    kf = rotary(k.astype(jnp.float32).reshape(bsz, s, RET_HEADS, RET_DK), pos) * (RET_DK ** -0.5)
    vf = v.astype(jnp.float32).reshape(bsz, s, RET_HEADS, RET_DV)
    yr = retention(qf, kf, vf)
    yr = yr * lax.rsqrt(jnp.mean(yr * yr, axis=-1, keepdims=True) + EPS)
    yr = (jax.nn.silu(g_ret.astype(jnp.float32)) * yr.reshape(bsz, s, RET_V)).astype(h.dtype)
    o_ret = yr @ ret_out

    xbc = jax.nn.silu(causal_dwconv(xbc, conv_w, conv_b))
    xs, bm, cm = jnp.split(xbc, [SSD_INNER, SSD_INNER + SSD_BC], axis=-1)
    xs = xs.astype(jnp.float32).reshape(bsz, s, SSD_GROUPS, SSD_HPG, SSD_HEADDIM)
    bm = bm.astype(jnp.float32).reshape(bsz, s, SSD_GROUPS, SSD_STATE)
    cm = cm.astype(jnp.float32).reshape(bsz, s, SSD_GROUPS, SSD_STATE)
    dtp = jax.nn.softplus(dt.astype(jnp.float32) + dt_bias.astype(jnp.float32))
    dtp = dtp.reshape(bsz, s, SSD_GROUPS, SSD_HPG)
    a = -jnp.exp(a_log.astype(jnp.float32)).reshape(SSD_GROUPS, SSD_HPG)
    ys = ssd_scan(xs * dtp[..., None], dtp * a, bm, cm)
    ys = ys + d_skip.astype(jnp.float32).reshape(SSD_GROUPS, SSD_HPG)[:, :, None] * xs
    ys = ys.reshape(bsz, s, SSD_INNER) * jax.nn.silu(z.astype(jnp.float32))
    ysg = ys.reshape(bsz, s, SSD_GROUPS, SSD_INNER // SSD_GROUPS)
    ysg = ysg * lax.rsqrt(jnp.mean(ysg * ysg, axis=-1, keepdims=True) + EPS)
    ys = (ysg.reshape(bsz, s, SSD_INNER) * ssd_norm_w.astype(jnp.float32)).astype(h.dtype)
    o_ssd = ys @ ssd_out

    merged = jax.nn.sigmoid(gate_ret) * o_ret + jax.nn.sigmoid(gate_ssd) * o_ssd
    return merged @ w_o

def swiglu(h, w_gate_up, w_down):
    gu = h @ w_gate_up
    gate, up = jnp.split(gu, [D_FF], axis=-1)
    return (jax.nn.silu(gate) * up) @ w_down

def second_inputs(seed: int = 0) -> dict:
    key = jax.random.key(seed)
    ks = jax.random.split(key, 20)
    f32 = jnp.float32

    def nrm(k, shape, fan_in):
        return jax.random.normal(k, shape, f32) * (fan_in ** -0.5)

    def gain(k, shape):
        return 1.0 + 0.02 * jax.random.normal(k, shape, f32)

    dt0 = jnp.exp(jax.random.uniform(ks[6], (DEPTH, SSD_HEADS), f32, math.log(1e-3), math.log(1e-1)))
    dt_bias = dt0 + jnp.log(-jnp.expm1(-dt0))
    a_log = jnp.log(jax.random.uniform(ks[7], (DEPTH, SSD_HEADS), f32, 1.0, 16.0))
    return {
        "x": jax.random.normal(ks[0], (BATCH, SEQ, D_MODEL), f32),
        "norm_mix_w": gain(ks[1], (DEPTH, D_MODEL)),
        "w_in": nrm(ks[2], (DEPTH, D_MODEL, D_IN), D_MODEL),
        "ret_out": nrm(ks[3], (DEPTH, RET_V, D_MODEL), RET_V),
        "conv_w": nrm(ks[4], (DEPTH, SSD_CONV, SSD_CONV_CH), SSD_CONV),
        "conv_b": 0.02 * jax.random.normal(ks[5], (DEPTH, SSD_CONV_CH), f32),
        "dt_bias": dt_bias,
        "a_log": a_log,
        "d_skip": gain(ks[8], (DEPTH, SSD_HEADS)),
        "ssd_norm_w": gain(ks[9], (DEPTH, SSD_INNER)),
        "ssd_out": nrm(ks[10], (DEPTH, SSD_INNER, D_MODEL), SSD_INNER),
        "w_o": nrm(ks[11], (DEPTH, D_MODEL, D_MODEL), D_MODEL),
        "norm_ffn_w": gain(ks[12], (DEPTH, D_MODEL)),
        "w_gate_up": nrm(ks[13], (DEPTH, D_MODEL, 2 * D_FF), D_MODEL),
        "w_down": nrm(ks[14], (DEPTH, D_FF, D_MODEL), D_FF),
        "final_norm_w": gain(ks[15], (D_MODEL,)),
    }

def second_block(x, norm_mix_w, w_in, ret_out, conv_w, conv_b, dt_bias, a_log, d_skip, ssd_norm_w,
              ssd_out, w_o, norm_ffn_w, w_gate_up, w_down, final_norm_w):
    h = x
    for l in range(DEPTH):
        h = h + hybrid_mixer(rmsnorm_2(h, norm_mix_w[l]), w_in[l], ret_out[l], conv_w[l], conv_b[l],
                             dt_bias[l], a_log[l], d_skip[l], ssd_norm_w[l], ssd_out[l], w_o[l])
        h = h + swiglu(rmsnorm_2(h, norm_ffn_w[l]), w_gate_up[l], w_down[l])
    return rmsnorm_2(h, final_norm_w)


def setup_inputs(seed=0):
    out = dict(first_inputs(seed))
    for name, value in second_inputs(seed + 1).items():
        if name != "x":
            out[name + "_2"] = value
    return out


def reference(
    x, norm_mix, w_in, b_gate, attn_sinks, w_attn_o, conv_w, w_conv_o, ssm_a_re, ssm_a_im,
    ssm_b_re, ssm_b_im, ssm_c_re, ssm_c_im, ssm_d, ssm_log_dt, w_ssm_glu, w_ssm_o, w_mix_o,
    norm_ffn, w_ffn_in, w_ffn_out, norm_final, norm_mix_w_2, w_in_2, ret_out_2, conv_w_2,
    conv_b_2, dt_bias_2, a_log_2, d_skip_2, ssd_norm_w_2, ssd_out_2, w_o_2, norm_ffn_w_2,
    w_gate_up_2, w_down_2, final_norm_w_2,
):
    x = first_block(
        x, norm_mix, w_in, b_gate, attn_sinks, w_attn_o, conv_w, w_conv_o, ssm_a_re, ssm_a_im,
        ssm_b_re, ssm_b_im, ssm_c_re, ssm_c_im, ssm_d, ssm_log_dt, w_ssm_glu, w_ssm_o, w_mix_o,
        norm_ffn, w_ffn_in, w_ffn_out, norm_final,
    )
    return second_block(
        x, norm_mix_w_2, w_in_2, ret_out_2, conv_w_2, conv_b_2, dt_bias_2, a_log_2, d_skip_2,
        ssd_norm_w_2, ssd_out_2, w_o_2, norm_ffn_w_2, w_gate_up_2, w_down_2, final_norm_w_2,
    )


_drawn_inputs = setup_inputs


def setup_inputs(seed=0):
    import zlib

    import numpy as np

    out = dict(_drawn_inputs(seed))
    spreads = {}
    factors = {'b_gate': 5.222,
     'attn_sinks': 2.931,
     'ssm_a_re': 8.0,
     'ssm_b_re': 3.067,
     'ssm_b_im': 3.123,
     'ssm_c_re': 3.103,
     'ssm_c_im': 3.126,
     'conv_b_2': 2.879,
     'd_skip_2': 5.741,
     'ssd_norm_w_2': 3.835,
     'norm_ffn_w_2': 2.796,
     'final_norm_w_2': 2.89}
    for name, (base, spread) in spreads.items():
        noise = np.random.default_rng([zlib.crc32(name.encode()), seed]).standard_normal(out[name].shape)
        drawn = base * np.exp(spread * noise) if base else spread * noise
        out[name] = __import__('jax').numpy.asarray(drawn.astype(out[name].dtype))
    for name, factor in factors.items():
        out[name] = (out[name] * factor).astype(out[name].dtype)
    return out
```

```python
from contextlib import ExitStack

import concourse.bass as bass
from concourse import mybir

ALU = mybir.AluOpType
ACT = mybir.ActivationFunctionType
AX_X = mybir.AxisListType.X
F32 = mybir.dt.float32
F32R = mybir.dt.float32r

P = 128
T = 256
D = 1024
KD = D // P
DEPTH = 2
EPS = 1e-6
SLAB = 1024
RING = 4
AHEAD = 3
LO_V = 384
FF = 22

HEADS, KV_HEADS, HD = 8, 2, 64
ROT = 16
N1 = 512 // P
CH = 64
NCH = T // CH
PAIRS = 16
PC = 32

U0, Q0, K0, V0, C0, G0 = 0, 4, 8, 9, 10, 22
CO0, AO0, GL0, SO0, MX0, FI0 = 46, 50, 54, 56, 60, 68
FO_S1, FO_T1 = 112, 112
S1, T1 = 136, 120
Q20, K20, V20, X20, GR20, Z20 = 0, 8, 16, 32, 56, 72
RO_S, RO_T, SO_S, SO_T = 88, 88, 112, 104
WO_S, WO_T, FI_S2, FI_T2, FO_S2, FO_T2 = 136, 120, 144, 128, 188, 172
S2, T2 = 212, 180
TOTAL = DEPTH * (S1 + S2)

RH = 4
SH, SP_, SG = 32, 64, 4
NI = 16
XB = 24
TRI = 3 * P

P1 = {}
_at = 0
for _name, _n in (("g_mix", KD), ("g_ffn", KD), ("b_gate", 24), ("conv_w", 3 * N1), ("d", N1),
                  ("sink", HEADS), ("a_re", PAIRS), ("a_im", PAIRS), ("log_dt", PAIRS),
                  ("b_re", N1 * P), ("b_im", N1 * P), ("c_re", PAIRS * PC), ("c_im", PAIRS * PC)):
    P1[_name] = (_at, _at + _n)
    _at += _n
P1_N = _at
P2 = {}
_at = 0
for _name, _n in (("g_mix", KD), ("g_ffn", KD), ("conv_w", 4 * XB), ("conv_b", XB), ("dt_b", SH),
                  ("a_log", SH), ("d_skip", NI), ("norm", NI), ("w_dt", KD * SH)):
    P2[_name] = (_at, _at + _n)
    _at += _n
P2_N = _at
C1 = {}
_at = 0
for _name, _n in (("ones_d", P), ("ones_i", P), ("ident", P), ("g_mid", KD), ("g_final", KD),
                  ("rope_c", T), ("rope_s", T), ("rope_r", P), ("mask", TRI)):
    C1[_name] = (_at, _at + _n)
    _at += _n
C1_N = _at
C2 = {}
_at = 0
for _name, _n in (("cos", T), ("sin", T), ("tri", TRI)):
    C2[_name] = (_at, _at + _n)
    _at += _n
C2_N = _at

V_STEPS1 = 74
V_STEPS2 = 170

TWO_PI = 6.283185307179586
TWO_PI_1 = 6.28125
TWO_PI_2 = 0.0019350051879882812
TWO_PI_3 = TWO_PI - TWO_PI_1 - TWO_PI_2
ROUND = 12582912.0
HALF_PI = 1.5707963267948966
PI_F = 3.1415925


def tasks1():
    side = [("rope", b) for b in range(5)]
    for c in range(NCH):
        side += [("rot", c), ("none",), ("rot2", c), ("none",)]
        if c == 1:
            side.append(("softnorm",))
        side += [("scan", c), ("none",), ("turn", c), ("none",)]
        if c == 0:
            side += [("scores", h) for h in range(HEADS)] + [("softmax",)]
        side += [("ssm_y", c), ("none",)]
    side.append(("gelu",))
    for h in range(HEADS):
        side += [("pt", h)] + ([("pv", h - 1)] if h else [])
    side.append(("pv", HEADS - 1))
    first = {4: [("prep",)], 5: [("prep_c",)], **{6 + k: [("double", k)] for k in range(6)}, 12: [("carry",)]}
    out = []
    for i in range(C0):
        out += first.pop(i, []) + [("slab", i)]
    per = -(-len(side) // (CO0 - C0 - 4))
    for i in range(C0, CO0):
        out += first.pop(i, []) + [("slab", i)]
        if i >= C0 + 4:
            out += side[:per]
            side = side[per:]
    return out + side + [("slab", i) for i in range(CO0, FI0)]


def tasks2():
    out = [("slab", i) for i in range(X20)]
    out.insert(V20 + 2, ("dt",))
    out.insert(V20 + 8, ("dt_sums",))
    ret = [t for h in range(RH) for t in (("ret_s", h), ("ret_y", h), ("ret_m", h))]
    for n in range(XB):
        out.append(("slab", X20 + n))
        if n % 2 == 1:
            out.append(ret.pop(0))
    out.append(("ret_rs",))
    pairs = [t for b in range(NI) for t in ([("pair", b)] + ([("pair_y", b - 1)] if b else []))] + [("pair_y", NI - 1)]
    for b in range(NI):
        out.append(("slab", GR20 + b))
        if b < SG:
            out += [("xdt", 2 * b), ("xdt", 2 * b + 1), ("cb", b)]
        else:
            out += pairs[:2]
            pairs = pairs[2:]
    for b in range(NI):
        out.append(("slab", Z20 + b))
        out += pairs[:2]
        pairs = pairs[2:]
        if b % 4 == 0 and b >= 4:
            out.append(("z_m", b // 4 - 1))
    out += [("slab", RO_S), ("slab", RO_S + 1), ("z_m", SG - 1), ("z_rs",)]
    norms = [("z_norm", b) for b in range(NI)]
    for i in range(RO_S + 2, FI_S2):
        out += [("slab", i)] + norms[:1]
        norms = norms[1:]
    return out


def hybrid_kernel(nc, weights, x_t, p1_d, p2_d, c1_d, c2_d, decay_d, out_t):
    with ExitStack() as ctx:
        top = [16512]

        def place(name, shape, dtype=F32, at=None):
            n = 4
            for v in shape[1:]:
                n *= v
            if at is None:
                at = top[0]
                top[0] += -(-n // 32) * 32
            assert at + n <= nc.sbuf_usable_end, (name, at + n)
            return nc.alloc_sbuf_tensor_at(name, shape, dtype, offset=at)

        w_raw = place("w_raw", [P, RING, SLAB])
        w_hi = place("w_hi", [P, RING, SLAB], F32R)
        w_lo = place("w_lo", [P, RING, SLAB], F32R)
        x = place("x", [P, KD, T])
        h_hi = place("h_hi", [P, KD, T], F32R)
        h_lo = place("h_lo", [P, KD, T], F32R)
        work_at = top[0]
        work = place("work", [P, KD, T])
        norm_at = top[0]
        root = place("root", [P, T])
        rinv = place("rinv", [P, T])
        rtmp = place("rtmp", [P, T])
        zpad_at = top[0]
        zpad = place("zpad", [P, 8 + T])
        sel = place("sel", [P, P], F32R)
        c1_at = top[0]
        c1 = place("c1", [P, C1_N])
        p_at = top[0]
        p1 = place("p1", [P, P1_N])
        arena = top[0]

        def in_arena(name, at, shape, dtype=F32):
            return place(name, shape, dtype, arena + at)

        f_hi = in_arena("f_hi", 0, [P, FF, T], F32R)
        f_lo = in_arena("f_lo", 22528, [P, FF, T], F32R)
        f_act = in_arena("f_act", 45056, [P, 2, T])
        f_prod = in_arena("f_prod", 47104, [P, 2, T])
        gate = in_arena("gate", 0, [P, 24, T])
        u = in_arena("u", 24576, [P, N1, T])
        qk = in_arena("qk", 28672, [P, 5, T])
        vrow = in_arena("vrow", 33792, [P, 2, P])
        turn = in_arena("turn", 34816, [P, 2, PAIRS, CH])
        decay = in_arena("decay", 43008, [P, PAIRS, CH])
        zs = in_arena("zs", 47104, [P, 2, PAIRS, CH])
        tm = in_arena("tm", 55296, [P, 2, PAIRS * CH])
        xst = in_arena("xst", 63488, [P, 2, PAIRS, CH])
        cab = in_arena("cab", 71680, [P, 2, PAIRS, PC])
        prob = in_arena("prob", 75776, [P, HEADS, TRI])
        probt = in_arena("probt", 88064, [P, 2, TRI])
        o_hi = in_arena("o_hi", 91136, [P, N1, T], F32R)
        o_lo = in_arena("o_lo", 95232, [P, N1, T], F32R)
        ccx = in_arena("ccx", 99328, [P, 2, T])
        cy = in_arena("cy", 101376, [P, 2, T])
        branch = in_arena("branch", 75776, [P, 2, 2 * T])
        cv_hi = in_arena("cv_hi", 103424, [P, N1, T], F32R)
        cv_lo = in_arena("cv_lo", 107520, [P, N1, T], F32R)
        ysg = in_arena("ysg", 55296, [P, N1, T])
        ys_hi = in_arena("ys_hi", 59392, [P, N1, T], F32R)
        ys_lo = in_arena("ys_lo", 47104, [P, N1, T], F32R)
        glu = in_arena("glu", 51200, [P, 2, 2 * T])
        yv = in_arena("yv", 34816, [P, N1, T])
        yv_hi = in_arena("yv_hi", 38912, [P, N1, T], F32R)
        yv_lo = in_arena("yv_lo", 43008, [P, N1, T], F32R)
        tiny = place("tiny", [P, 40, PAIRS], at=work_at)
        soft = place("soft", [P, 10, 2, HEADS], at=work_at + 4096)
        qt = in_arena("qt", 0, [P, 2 * RH, T])
        kt = in_arena("kt", 8192, [P, 2 * RH, T])
        vr = in_arena("vr", 16384, [P, 2, NI * P])
        r_hi = in_arena("r_hi", 0, [P, NI, T], F32R)
        r_lo = in_arena("r_lo", 16384, [P, NI, T], F32R)
        m_hi = in_arena("m_hi", 0, [P, KD, T], F32R)
        m_lo = in_arena("m_lo", 8192, [P, KD, T], F32R)
        rp = in_arena("rp", 32768, [P, 2, TRI])
        rdec = in_arena("rdec", 35840, [P, RH, TRI])
        lseg = in_arena("lseg", 41984, [P, 2, TRI])
        xs = in_arena("xs", 45056, [P, NI, T])
        xdt = in_arena("xdt", 61440, [P, 2, NI * P])
        sq2 = in_arena("sq2", 61440, [P, 4, T])
        sqz = in_arena("sqz", 35840, [P, 4, T])
        s_hi = in_arena("s_hi", 61440, [P, NI, T], F32R)
        yr = in_arena("yr", 77824, [P, NI, T])
        s_lo = in_arena("s_lo", 77824, [P, NI, T], F32R)
        mt = in_arena("mt", 94208, [P, 2, TRI])
        wdt_hi = in_arena("wdt_hi", 94208, [P, KD, SH], F32R)
        wdt_lo = in_arena("wdt_lo", 95232, [P, KD, SH], F32R)
        nt = in_arena("nt", 65536, [P, 4, T])
        cv = in_arena("cv", 97280, [P, 2, T])
        ms = in_arena("ms", 99328, [P, 4, T])
        rr = in_arena("rr", 103424, [P, 4, T])
        sg = in_arena("sg", 107520, [P, 2, T])
        pr = in_arena("pr", 109568, [P, 2, T])
        dts = place("dts", [P, 12, 2, SH], at=norm_at)
        bc = place("bc", [P, 2, SG, T], at=work_at)
        c2 = place("c2", [P, C2_N], at=c1_at + 4 * C1["rope_c"][0])
        p2 = place("p2", [P, P2_N], at=p_at)
        at_hi = place("at_hi", [P, T], F32R, at=zpad_at + 32)
        at_lo = place("at_lo", [P, T], F32R, at=p_at + 4 * P2["w_dt"][0])
        cbm = place("cbm", [P, SG, TRI], at=p_at + 4 * P2_N)
        above = place("above", [P, P], F32R, at=c1_at + 4 * (C1["rope_c"][0] + C2_N))
        assert P2_N + SG * TRI <= P1_N and C2_N + P <= C1_N - C1["rope_c"][0]

        def par1(name, a=0, b=None):
            lo, hi = P1[name]
            return p1[:, lo + a:hi if b is None else lo + b]

        def par2(name, a=0, b=None):
            lo, hi = P2[name]
            return p2[:, lo + a:hi if b is None else lo + b]

        def con1(name):
            return c1[:, C1[name][0]:C1[name][1]]

        def con2(name):
            return c2[:, C2[name][0]:C2[name][1]]

        acc = [ctx.enter_context(nc.psum_tensor(f"acc{i}", [P, 512], F32)) for i in range(4)]
        mid = [ctx.enter_context(nc.psum_tensor(f"mid{i}", [P, 512], F32)) for i in range(4)]

        def sem(name):
            return ctx.enter_context(nc.semaphore(name))

        landed = [sem(f"landed{i}") for i in range(RING)]
        hi_done = sem("hi_done")
        lo_v = sem("lo_v")
        lo_g = sem("lo_g")
        used = sem("used")
        out = [sem(f"out{i}") for i in range(4)]
        consts = sem("consts")
        consts2 = sem("consts2")
        decays = sem("decays")
        params = sem("params")
        sel_ok = sem("sel_ok")
        v_above = sem("v_above")
        pad_ok = sem("pad_ok")
        stored = sem("stored")
        sq_ok = sem("sq_ok")
        mean_ok = sem("mean_ok")
        root_ok = sem("root_ok")
        hf_ok = sem("hf_ok")
        hhi_ok = sem("hhi_ok")
        h_ok = sem("h_ok")
        ff_hi = sem("ff_hi")
        ff_lo = sem("ff_lo")
        v_norm = sem("v_norm")
        dve_step = sem("dve_step")
        dve_step2 = sem("dve_step2")
        a_prep = sem("a_prep")
        v_prep = sem("v_prep")
        pe_rope = sem("pe_rope")
        v_rope = sem("v_rope")
        pe_bu = sem("pe_bu")
        v_rot = sem("v_rot")
        v_x = sem("v_x")
        pe_y = sem("pe_y")
        v_y = sem("v_y")
        a_gelu = sem("a_gelu")
        v_yslo = sem("v_yslo")
        pe_s = sem("pe_s")
        v_mask = sem("v_mask")
        v_max = sem("v_max")
        a_exp = sem("a_exp")
        v_p = sem("v_p")
        pe_t = sem("pe_t")
        a_pt = sem("a_pt")
        pe_pv = sem("pe_pv")
        a_ohi = sem("a_ohi")
        v_olo = sem("v_olo")
        a_chi = sem("a_chi")
        v_clo = sem("v_clo")
        v_yv = sem("v_yv")
        a_yvhi = sem("a_yvhi")
        v_yvlo = sem("v_yvlo")
        v_mg = sem("v_mg")
        a_mhi = sem("a_mhi")
        v_mlo = sem("v_mlo")
        a_cv = sem("a_cv")
        a_xs = sem("a_xs")
        pe_rs = sem("pe_rs")
        v_rp = sem("v_rp")
        pe_ry = sem("pe_ry")
        a_yr = sem("a_yr")
        pe_rm = sem("pe_rm")
        v_rm = sem("v_rm")
        a_root2 = sem("a_root2")
        v_qk = sem("v_qk")
        a_dt = sem("a_dt")
        v_dt = sem("v_dt")
        pe_dt = sem("pe_dt")
        pe_xt = sem("pe_xt")
        v_xdt = sem("v_xdt")
        pe_cb = sem("pe_cb")
        v_cb = sem("v_cb")
        pe_bc = sem("pe_bc")
        a_l = sem("a_l")
        v_m = sem("v_m")
        pe_y2 = sem("pe_y2")
        v_ys = sem("v_ys")
        v_flo = sem("v_flo")
        v_z = sem("v_z")
        a_zsq = sem("a_zsq")
        pe_zm = sem("pe_zm")
        v_zm = sem("v_zm")
        v_slo = sem("v_slo")
        v_mlo2 = sem("v_mlo2")

        block = ctx.enter_context(nc.Block())

        class Layer:

            def __init__(self, second, n):
                self.n = n
                self.slab = n * S2 + DEPTH * S1 if second else n * S1
                self.four = n * (T2 // 4) + DEPTH * (T1 // 4) if second else n * (T1 // 4)
                self.norm = n * 2 + (2 * DEPTH + 1 if second else 0)
                self.split = n * 2 + (2 * DEPTH if second else 0)
                self.ffn = n * FF + (DEPTH * FF if second else 0)

        def wait_used(eng, at, i):
            eng.wait_ge(used, at.slab + (i + 1 + RING))

        def wait_out(eng, at, t):
            eng.wait_ge(out[t % 4], at.four + (t // 4 + 3))

        class Middle:
            norm = 2 * DEPTH
            four = DEPTH * (T1 // 4)

        def ffn_layout(second):
            return (FI_S2, FI_T2, FO_S2, FO_T2) if second else (FI0, FI0, FO_S1, FO_T1)

        class Later:

            def __init__(self, at, it, slabs, tiles, ffn=0):
                self.n, self.norm, self.split = at.n, at.norm, at.split
                self.slab = at.slab + it * slabs
                self.four = at.four + it * (tiles // 4)
                self.ffn = at.ffn + it * ffn

        @block.sync
        def _(sp):
            def load(s, slot):
                sp.dma_start(w_raw[:, slot, :], weights[bass.ds(s, 1)].rearrange("a p n -> p (a n)")
                             ).then_inc(landed[slot], 16)

            for slot in range(RING):
                load(slot, slot)
            with sp.Fori(1, TOTAL // RING + 1) as it:
                for slot in range(RING):
                    sp.wait_ge(lo_v, it * RING + (slot + 1 - RING))
                    sp.wait_ge(lo_g, it * RING + (slot + 1 - RING))
                    load(it * RING + slot, slot)
            for j in range(4):
                sp.wait_ge(hf_ok, 4 * (4 * DEPTH + 1) + j + 1)
                sp.dma_start(out_t.rearrange("(k p) t -> p k t", p=P)[:, 2 * j:2 * j + 2, :],
                             work[:, 2 * j:2 * j + 2, :]).then_inc(stored, 16)
            sp.wait_ge(stored, 64)
            for slot in range(RING):
                sp.wait_ge(landed[slot], 16 * (TOTAL // RING + 1))

        @block.gpsimd
        def _(pool):
            nc.gpsimd.memset(zpad[:, 0:8], 0.0).then_inc(pad_ok, 1)
            with pool.Fori(0, TOTAL // RING) as it:
                for slot in range(RING):
                    pool.wait_ge(hi_done, it * RING + (slot + 1))
                    nc.gpsimd.tensor_tensor(w_lo[:, slot, LO_V:], w_raw[:, slot, LO_V:],
                                            w_hi[:, slot, LO_V:].bitcast(F32), ALU.subtract).then_inc(lo_g, 1)
            for slot in range(AHEAD):
                pool.wait_ge(hi_done, TOTAL + slot + 1)
                nc.gpsimd.tensor_tensor(w_lo[:, slot, LO_V:], w_raw[:, slot, LO_V:],
                                        w_hi[:, slot, LO_V:].bitcast(F32), ALU.subtract).then_inc(lo_g, 1)

        @block.tensor
        def _(pe):
            mm = nc.tensor.matmul

            def norm(at, which):
                for b in range(KD):
                    pe.wait_ge(sq_ok, (at.norm + which) * KD + (b + 1))
                    last = mm(mid[0][:, 0:T], con1("ones_d"), work[:, b, :], start=b == 0, stop=b == KD - 1)
                last.then_inc(mean_ok, 1)

            def weights_of(at, i):
                pe.wait_ge(lo_v, at.slab + (i + 1))
                pe.wait_ge(lo_g, at.slab + (i + 1))

            def bank(at, t):
                pe.wait_ge(out[t % 4], at.four + (t // 4 + 2))

            def products(at, i, dst, col, width, ks, hi, lo, first=True, last=True, need=None):
                slot = i % RING
                for j, k in enumerate(ks):
                    if need is not None:
                        need(k)
                    a = j * width + col
                    wh, wl = w_hi[:, slot, a:a + P], w_lo[:, slot, a:a + P]
                    mm(dst, wh, hi[:, k, :], start=first and j == 0, stop=False)
                    mm(dst, wh, lo[:, k, :], start=False, stop=False)
                    done = mm(dst, wl, hi[:, k, :], start=False, stop=last and j == len(ks) - 1)
                return done

            def slab_k8(at, i, t, need=None, hi=h_hi, lo=h_lo):
                weights_of(at, i)
                bank(at, t)
                products(at, i, acc[t % 4][:, 0:T], 0, P, range(KD), hi, lo, need=need).then_inc(used, 1)

            def slab_k4(at, i, t, hi, lo):
                weights_of(at, i)
                bank(at, t)
                for b in range(2):
                    done = products(at, i, acc[t % 4][:, b * T:(b + 1) * T], b * P, 2 * P, range(4), hi, lo)
                done.then_inc(used, 1)

            def slabs_long(at, i, t, n, blocks, hi, lo, need=None):
                bank(at, t)
                for m in range(n):
                    weights_of(at, i + m)
                    ks = range(m * KD, min(m * KD + KD, blocks))
                    products(at, i + m, acc[t % 4][:, 0:T], 0, P, ks, hi, lo, m == 0, m == n - 1, need).then_inc(used, 1)

            def slab_rows(at, i, t):
                weights_of(at, i)
                bank(at, t)
                slot = i % RING
                for r in range(2):
                    dst = acc[t % 4][:, r * P:(r + 1) * P]
                    for k in range(KD):
                        wh, wl = w_hi[:, slot, k * P:(k + 1) * P], w_lo[:, slot, k * P:(k + 1) * P]
                        hh, hl = h_hi[:, k, r * P:(r + 1) * P], h_lo[:, k, r * P:(r + 1) * P]
                        mm(dst, hh, wh, start=k == 0, stop=False)
                        mm(dst, hh, wl, start=False, stop=False)
                        done = mm(dst, hl, wh, start=False, stop=k == KD - 1)
                done.then_inc(used, 1)

            def normed(at, which):
                return lambda k: pe.wait_ge(h_ok, (at.split + which) * 4 + (k // 2 + 1))

            def ffn(at, second):
                si, ti, so, to = ffn_layout(second)
                need = normed(at, 1)
                with pe.Fori(0, FF // 2) as it:
                    now = Later(at, it, 4, 4)
                    for j in range(4):
                        slab_k8(now, si + j, ti + j, need if j == 0 else None)
                def act_ready(k):
                    pe.wait_ge(ff_lo, at.ffn + (k + 1))

                with pe.Fori(0, 2) as it:
                    now = Later(at, it, 12, 4)
                    for n in range(4):
                        slabs_long(now, so + 3 * n, to + n, 3, FF, f_hi, f_lo, act_ready if n == 0 else None)

            def s5_in(at, c):
                if c == 0:
                    pe.wait_ge(v_rope, at.n * 5 + 5)
                    for t in range(4):
                        wait_out(pe, at, U0 + t)
                else:
                    pe.wait_ge(v_y, at.n * 4 + c)
                    pe.wait_ge(v_mask, at.n * 8 + 8)
                for part, name in ((0, "b_re"), (1, "b_im")):
                    for blk in range(N1):
                        for q in range(4):
                            rows = slice(PC * q, PC * q + PC)
                            b = p1[rows, P1[name][0] + blk * P:P1[name][0] + (blk + 1) * P]
                            dst = mid[q][:, (part * N1 + blk) * CH:(part * N1 + blk + 1) * CH]
                            last = mm(dst, b, u[rows, blk, c * CH:(c + 1) * CH], start=True, stop=True,
                                      tile_position=(PC * q, 0))
                last.then_inc(pe_bu, 1)

            def s5_out(at, c):
                pe.wait_ge(v_x, at.n * 4 + (c + 1))
                if c == 0:
                    pe.wait_ge(v_prep, at.n * 3 + 3)
                for blk in range(N1):
                    for q in range(4):
                        pair = blk * 4 + q
                        dst = mid[2][PC * q:PC * q + PC, blk * CH:(blk + 1) * CH]
                        mm(dst, cab[:, 0, pair, :], xst[:, 0, pair, :], start=True, stop=False, tile_position=(0, PC * q))
                        last = mm(dst, cab[:, 1, pair, :], xst[:, 1, pair, :], start=False, stop=True,
                                  tile_position=(0, PC * q))
                last.then_inc(pe_y, 1)

            def rope(at, b):
                wait_out(pe, at, Q0 + b)
                if b >= 2:
                    pe.wait_ge(v_rope, at.n * 5 + (b - 1))
                mm(mid[2 + b % 2][:, 0:T], con1("rope_r"), qk[:, b, :],
                   start=True, stop=True).then_inc(pe_rope, 1)

            def scores(at, h):
                a, g = h // 2, h % 2
                if h == 0:
                    pe.wait_ge(v_rot, at.n * 4 + 1)
                else:
                    pe.wait_ge(v_mask, at.n * 8 + h)
                rows = slice(HD * g, HD * g + HD)
                mm(mid[3][:, 0:P], qk[rows, a, 0:P], qk[rows, 4, 0:P], start=True, stop=True)
                mm(mid[3][:, P:TRI], qk[rows, a, P:T], qk[rows, 4, :], start=True, stop=True).then_inc(pe_s, 1)

            def turn_probs(at, h):
                if h == 0:
                    pe.wait_ge(v_p, at.n + 1)
                else:
                    pe.wait_ge(a_pt, at.n * 8 + h)
                for j in range(3):
                    last = nc.tensor.transpose(mid[3][:, j * P:(j + 1) * P], prob[:, h, j * P:(j + 1) * P], con1("ident"))
                last.then_inc(pe_t, 1)

            def values(at, h):
                a, g = h // 2, h % 2
                pe.wait_ge(a_pt, at.n * 8 + (h + 1))
                if h == 0:
                    wait_out(pe, at, V0)
                    pe.wait_ge(v_y, at.n * 4 + 4)
                if g == 0 and a > 0:
                    pe.wait_ge(v_olo, at.n * 4 + a)
                rows = slice(HD * g, HD * g + HD)
                mm(mid[2][rows, T:2 * T], vrow[:, 0, rows], probt[:, h % 2, 0:T], start=True, stop=False,
                   tile_position=(0, HD * g))
                mm(mid[2][rows, T + P:2 * T], vrow[:, 1, rows], probt[:, h % 2, T:TRI], start=False, stop=True,
                   tile_position=(0, HD * g)).then_inc(pe_pv, 1)

            def first_slab(at, i):
                if i == 0:
                    slab_k8(at, i, i, normed(at, 0))
                elif i == V0:
                    slab_rows(at, i, i)
                elif i < CO0:
                    slab_k8(at, i, i)
                elif i < AO0:
                    if i == CO0:
                        pe.wait_ge(v_clo, at.n * 4 + 4)
                    slab_k4(at, i, i, cv_hi, cv_lo)
                elif i < GL0:
                    if i == AO0:
                        pe.wait_ge(v_olo, at.n * 4 + 4)
                    slab_k4(at, i, i, o_hi, o_lo)
                elif i < SO0:
                    if i == GL0:
                        pe.wait_ge(v_yslo, at.n + 1)
                    slab_k4(at, i, i, ys_hi, ys_lo)
                elif i < MX0:
                    if i == SO0:
                        pe.wait_ge(v_yvlo, at.n * 2 + 2)
                    slab_k4(at, i, i, yv_hi, yv_lo)
                else:
                    slab_k8(at, i, i, (lambda k: pe.wait_ge(v_mlo, at.n * 4 + (k // 2 + 1))) if i == MX0 else None)

            pe.sem_inc(used, RING)
            for t in range(4):
                pe.sem_inc(out[t], 2)
            pe.wait_ge(consts, 16 * 2)
            with pe.Fori(0, DEPTH) as n:
                at = Layer(False, n)
                norm(at, 0)
                for task in tasks1():
                    if task[0] == "slab":
                        first_slab(at, task[1])
                    elif task[0] == "rope":
                        rope(at, task[1])
                    elif task[0] == "rot":
                        s5_in(at, task[1])
                    elif task[0] == "ssm_y":
                        s5_out(at, task[1])
                    elif task[0] == "scores":
                        scores(at, task[1])
                    elif task[0] == "pt":
                        turn_probs(at, task[1])
                    elif task[0] == "pv":
                        values(at, task[1])
                norm(at, 1)
                ffn(at, False)

            def ret_scores(at, h):
                if h == 0:
                    pe.wait_ge(v_qk, at.n * 8 + 8)
                else:
                    pe.wait_ge(v_rp, at.n * 4 + h)
                for d in range(2):
                    mm(mid[2][:, 0:T], kt[:, 2 * h + d, 0:P], qt[:, 2 * h + d, :], start=d == 0, stop=d == 1)
                for d in range(2):
                    last = mm(mid[2][:, T:TRI], kt[:, 2 * h + d, P:T], qt[:, 2 * h + d, P:T], start=d == 0, stop=d == 1)
                last.then_inc(pe_rs, 1)

            def ret_values(at, h):
                pe.wait_ge(v_rp, at.n * 4 + (h + 1))
                if h == 0:
                    for t in range(V20 + 12, V20 + 16):
                        wait_out(pe, at, t)
                for e in range(4):
                    a = (h * 4 + e) * P
                    dst = mid[e // 2]
                    c = (e % 2) * T
                    mm(dst[:, c:c + T], vr[:, 0, a:a + P], rp[:, h % 2, 0:T], start=True, stop=False)
                    last = mm(dst[:, c + P:c + T], vr[:, 1, a:a + P], rp[:, h % 2, T:TRI], start=False, stop=True)
                last.then_inc(pe_ry, 1)

            def ret_mean(at, h):
                pe.wait_ge(a_yr, at.n * 16 + (4 * h + 4))
                if h:
                    pe.wait_ge(v_rm, at.n * 4 + h)
                for e in range(4):
                    last = mm(mid[3][:, 0:T], con1("ones_i"), sq2[:, e, :], start=e == 0, stop=e == 3)
                last.then_inc(pe_rm, 1)

            def dt(at):
                pe.wait_ge(v_dt, at.n * 4 + 1)
                for r in range(2):
                    dst = mid[0][:, r * SH:(r + 1) * SH]
                    for k in range(KD):
                        hh, hl = h_hi[:, k, r * P:(r + 1) * P], h_lo[:, k, r * P:(r + 1) * P]
                        mm(dst, hh, wdt_hi[:, k, :], start=k == 0, stop=False)
                        mm(dst, hh, wdt_lo[:, k, :], start=False, stop=False)
                        last = mm(dst, hl, wdt_hi[:, k, :], start=False, stop=k == KD - 1)
                last.then_inc(pe_dt, 1)

            def dt_sums(at):
                pe.wait_ge(v_dt, at.n * 4 + 3)
                tri = con2("tri")
                la = dts[:, 8, :, :]
                a0 = 2 * SH
                mm(mid[0][:, a0:a0 + SH], tri[:, 0:P], la[:, 0, :], start=True, stop=True)
                mm(mid[0][:, a0 + SH:a0 + 2 * SH], tri[:, P:T], la[:, 0, :], start=True, stop=False)
                mm(mid[0][:, a0 + SH:a0 + 2 * SH], tri[:, T:TRI], la[:, 1, :], start=False, stop=True)
                mm(mid[0][0:SH, P:P + T], la[:, 0, :], tri[:, 0:T], start=True, stop=False)
                mm(mid[0][0:SH, T:P + T], la[:, 1, :], tri[:, T:TRI], start=False, stop=True).then_inc(pe_dt, 1)

            def turn_xs(at, m):
                pe.wait_ge(a_xs, at.n * XB + (2 * m + 2))
                if m >= 2:
                    pe.wait_ge(v_xdt, at.n * 8 + (m - 1))
                elif m == 1:
                    pe.wait_ge(v_rp, at.n * 4 + 4)
                for b in range(2):
                    for r in range(2):
                        c = (2 * b + r) * P
                        last = nc.tensor.transpose(mid[1 + m % 2][:, c:c + P], xs[:, 2 * m + b, r * P:(r + 1) * P],
                                                   con1("ident"))
                last.then_inc(pe_xt, 1)

            def c_times_b(at, g):
                if g == 0:
                    pe.wait_ge(a_xs, at.n * XB + XB)
                    pe.wait_ge(a_yr, at.n * 16 + 16)
                else:
                    pe.wait_ge(v_cb, at.n * 4 + g)
                mm(mid[0][:, 0:T], bc[:, 0, g, 0:P], bc[:, 1, g, :], start=True, stop=True)
                mm(mid[0][:, T:TRI], bc[:, 0, g, P:T], bc[:, 1, g, P:T], start=True, stop=True).then_inc(pe_cb, 1)

            def sums_of_pair(at, b):
                if b:
                    pe.wait_ge(a_l, at.n * 16 + b)
                else:
                    pe.wait_ge(v_cb, at.n * 4 + 4)
                    pe.wait_ge(v_xdt, at.n * 8 + 8)
                    pe.wait_ge(v_dt, at.n * 4 + 4)
                for n in range(2):
                    pick = sel[0:SH, 2 * b + n:2 * b + n + 1].to_broadcast([SH, P])
                    for lo, hi, t in ((0, T, 0), (T, TRI, P)):
                        dst = mid[n][:, lo:hi]
                        mm(dst, pick, at_hi[0:SH, t:T], start=True, stop=False)
                        mm(dst, pick, at_lo[0:SH, t:T], start=False, stop=False)
                        last = mm(mid[n][:, lo:lo + P], sel[:, :], above[:, :], start=False, stop=True)
                last.then_inc(pe_bc, 1)

            def ssd_values(at, b):
                pe.wait_ge(v_m, at.n * 16 + (b + 1))
                if b >= 2:
                    pe.wait_ge(v_ys, at.n * 16 + (b - 1))
                dst = mid[2 + b % 2]
                for n in range(2):
                    h = 2 * b + n
                    rows = slice(SP_ * n, SP_ * n + SP_)
                    mm(dst[rows, 0:T], xdt[:, 0, h * SP_:(h + 1) * SP_], mt[:, n, 0:T], start=True, stop=False,
                       tile_position=(0, SP_ * n))
                    last = mm(dst[rows, P:T], xdt[:, 1, h * SP_:(h + 1) * SP_], mt[:, n, T:TRI],
                              start=False, stop=True, tile_position=(0, SP_ * n))
                last.then_inc(pe_y2, 1)

            def ssd_mean(at, g):
                pe.wait_ge(a_zsq, at.n * 16 + (4 * g + 4))
                if g:
                    pe.wait_ge(v_zm, at.n * 4 + g)
                else:
                    pe.wait_ge(v_ys, at.n * 16 + 16)
                for e in range(4):
                    last = mm(mid[3][:, 0:T], con1("ones_i"), sqz[:, e, :], start=e == 0, stop=e == 3)
                last.then_inc(pe_zm, 1)

            def second_slab(at, i):
                if i == 0:
                    slab_k8(at, i, i, normed(at, 0))
                elif V20 <= i < X20:
                    slab_rows(at, i, i)
                elif i < RO_S:
                    slab_k8(at, i, i)
                elif i < WO_S:
                    s0, t0, hi, lo, ready, per = ((RO_S, RO_T, r_hi, r_lo, v_flo, NI) if i < SO_S
                                                  else (SO_S, SO_T, s_hi, s_lo, v_slo, NI))
                    n, part = (i - s0) // 3, (i - s0) % 3
                    if part == 0:
                        slab_k8(at, i, t0 + 2 * n)
                    elif part == 1:
                        slabs_long(at, i, t0 + 2 * n + 1, 2, NI, hi, lo,
                                   (lambda k: pe.wait_ge(ready, at.n * per + (k + 1))) if n == 0 else None)
                else:
                    slab_k8(at, i, WO_T + i - WO_S,
                            (lambda k: pe.wait_ge(v_mlo2, at.n * 8 + (k + 1))) if i == WO_S else None, m_hi, m_lo)

            norm(Middle(), 0)
            pe.wait_ge(sel_ok, 1)
            pe.wait_ge(v_above, 1)
            pe.wait_ge(consts2, 16)
            with pe.Fori(0, DEPTH) as n:
                at = Layer(True, n)
                norm(at, 0)
                for task in tasks2():
                    if task[0] == "slab":
                        second_slab(at, task[1])
                    elif task[0] == "ret_s":
                        ret_scores(at, task[1])
                    elif task[0] == "ret_y":
                        ret_values(at, task[1])
                    elif task[0] == "ret_m":
                        ret_mean(at, task[1])
                    elif task[0] == "dt":
                        dt(at)
                    elif task[0] == "dt_sums":
                        dt_sums(at)
                    elif task[0] == "xdt":
                        turn_xs(at, task[1])
                    elif task[0] == "cb":
                        c_times_b(at, task[1])
                    elif task[0] == "pair":
                        sums_of_pair(at, task[1])
                    elif task[0] == "pair_y":
                        ssd_values(at, task[1])
                    elif task[0] == "z_m":
                        ssd_mean(at, task[1])
                norm(at, 1)
                ffn(at, True)
            norm(Layer(True, DEPTH), 0)

        def wait_x(eng, at, second, which, b):
            if which == 0:
                eng.wait_ge(out[b % 4], at.four + (b // 4 + 1))
            else:
                wait_out(eng, at, (WO_T if second else MX0) + b)

        @block.scalar
        def _(act):
            def split(at, i):
                slot = i % RING
                act.wait_ge(landed[slot], (at.slab // RING + (i // RING + 1)) * 16)
                act.wait_ge(used, at.slab + (i + 1))
                nc.scalar.copy(w_hi[:, slot, :], w_raw[:, slot, :]).then_inc(hi_done, 1)

            def evac(at, i, t, dst, src, func=ACT.Copy, **kw):
                wait_used(act, at, i)
                nc.scalar.activation(dst, src, func, **kw).then_inc(out[t % 4], 1)

            def norm(at, second, which, last=False):
                for b in range(KD):
                    wait_x(act, at, second, which, b)
                    nc.scalar.activation(work[:, b, :], x[:, b, :], ACT.Square).then_inc(sq_ok, 1)
                act.wait_ge(mean_ok, at.norm + (which + 1))
                nc.scalar.activation(root[:, :], mid[0][:, 0:T], ACT.Sqrt, bias=EPS).then_inc(root_ok, 1)
                if last:
                    return
                for j in range(4):
                    act.wait_ge(hf_ok, (at.norm + which) * 4 + (j + 1))
                    nc.scalar.copy(h_hi[:, 2 * j:2 * j + 2, :], work[:, 2 * j:2 * j + 2, :]).then_inc(hhi_ok, 1)

            def ffn(at, second):
                si, ti, so, to = ffn_layout(second)
                with act.Fori(0, FF // 2) as it:
                    now = Later(at, it, 4, 4, 2)
                    for b in range(2):
                        split(now, si + 2 * b + AHEAD)
                        wait_out(act, now, ti + 2 * b - 3)
                        evac(now, si + 2 * b, ti + 2 * b, f_act[:, b, :], acc[(ti + 2 * b) % 4][:, 0:T], ACT.Silu)
                        split(now, si + 2 * b + 1 + AHEAD)
                with act.Fori(0, 2) as it:
                    now = Later(at, it, 12, 4)
                    for j in range(12):
                        split(now, so + j + AHEAD)

            def prep(at):
                act.wait_ge(h_ok, at.split * 4 + 4)
                nc.scalar.activation(tiny[:, 0, :], par1("log_dt"), ACT.Exp).then_inc(a_prep, 1)
                act.wait_ge(v_prep, at.n * 3 + 1)
                nc.scalar.activation(tiny[:, 2, :], tiny[:, 1, :], ACT.Exp).then_inc(a_prep, 1)
                act.wait_ge(v_prep, at.n * 3 + 2)
                nc.scalar.activation(turn[:, 1, :, 0], tiny[:, 5, :], ACT.Sin).then_inc(a_prep, 1)
                nc.scalar.activation(turn[:, 0, :, 0], tiny[:, 6, :], ACT.Sin, bias=HALF_PI).then_inc(a_prep, 1)

            def softmax(at):
                act.wait_ge(v_max, at.n + 1)
                nc.scalar.activation(soft[:, 5, :, :], soft[:, 4, :, :], ACT.Exp)
                for h in range(HEADS):
                    for r, (a, b) in enumerate(((0, P), (P, TRI))):
                        last = nc.scalar.activation(prob[:, h, a:b], prob[:, h, a:b], ACT.Exp, bias=soft[:, 3, r, h:h + 1],
                                                    accum_out=soft[:, 6, r, h:h + 1])
                last.then_inc(a_exp, 1)

            def gelu(at):
                act.wait_ge(v_y, at.n * 4 + 4)
                nc.scalar.activation(ysg[:, :, :], u[:, :, :], ACT.Gelu_apprx_tanh).then_inc(a_gelu, 1)
                act.wait_ge(a_gelu, at.n * 2 + 1)
                nc.scalar.copy(ys_hi[:, :, :], ysg[:, :, :]).then_inc(a_gelu, 1)

            def probs(at, h):
                act.wait_ge(pe_t, at.n * 8 + (h + 1))
                if h >= 2:
                    act.wait_ge(pe_pv, at.n * 8 + (h - 1))
                nc.scalar.copy(probt[:, h % 2, :], mid[3][:, 0:TRI]).then_inc(a_pt, 1)

            def attended(at, a):
                act.wait_ge(pe_pv, at.n * 8 + (2 * a + 2))
                nc.scalar.copy(o_hi[:, a, :], mid[2][:, T:2 * T]).then_inc(a_ohi, 1)

            def first_slab(at, i):
                split(at, i + AHEAD)
                bank = acc[i % 4]
                if i < Q0:
                    evac(at, i, i, u[:, i, :], bank[:, 0:T])
                elif i < V0:
                    evac(at, i, i, qk[:, i - Q0, :], bank[:, 0:T])
                elif i == V0:
                    evac(at, i, i, vrow[:, :, :], bank[:, 0:T])
                elif i < G0:
                    b, part = (i - C0) // 3, (i - C0) % 3
                    if part == 0:
                        if b >= 2:
                            wait_out(act, at, i - 4)
                        evac(at, i, i, ccx[:, b % 2, :], bank[:, 0:T])
                    if part == 2:
                        wait_out(act, at, i)
                        nc.scalar.copy(cv_hi[:, b, :], cy[:, b % 2, :]).then_inc(a_chi, 1)
                elif i < CO0:
                    evac(at, i, i, gate[:, i - G0, :], bank[:, 0:T], ACT.Sigmoid, bias=par1("b_gate", i - G0, i - G0 + 1))
                elif GL0 <= i < SO0:
                    evac(at, i, i, glu[:, i - GL0, :], bank[:, :], ACT.Sigmoid)
                    act.wait_ge(v_yv, at.n * 2 + (i - GL0 + 1))
                    a = 2 * (i - GL0)
                    nc.scalar.copy(yv_hi[:, a:a + 2, :], yv[:, a:a + 2, :]).then_inc(a_yvhi, 1)
                elif SO0 <= i < MX0:
                    act.wait_ge(v_mg, at.n * 4 + (i - SO0 + 1))
                    a = 2 * (i - SO0)
                    nc.scalar.copy(h_hi[:, a:a + 2, :], work[:, a:a + 2, :]).then_inc(a_mhi, 1)

            act.dma_start(x[:, :, :], x_t.rearrange("(k p) t -> p k t", p=P)).then_inc(consts, 16)
            act.dma_start(c1[:, :], c1_d).then_inc(consts, 16)
            start = Layer(False, 0)
            for slot in range(AHEAD):
                split(start, slot)
            act.wait_ge(consts, 32)
            nc.scalar.copy(sel[:, :], con1("ident")).then_inc(sel_ok, 1)
            with act.Fori(0, DEPTH) as n:
                at = Layer(False, n)
                wait_x(act, at, False, 0, KD - 1)
                act.dma_start(p1[:, :], p1_d[bass.ds(n, 1)].rearrange("a p n -> p (a n)")).then_inc(params, 16)
                norm(at, False, 0)
                act.wait_ge(params, n * 16 + 16)
                for task in tasks1():
                    if task[0] == "slab":
                        first_slab(at, task[1])
                    elif task[0] == "prep":
                        prep(at)
                    elif task[0] == "softmax":
                        softmax(at)
                    elif task[0] == "gelu":
                        gelu(at)
                    elif task[0] == "pt":
                        probs(at, task[1])
                    elif task[0] == "pv" and task[1] % 2:
                        attended(at, task[1] // 2)
                norm(at, False, 1)
                ffn(at, False)

            def conv_silu(at, b):
                wait_out(act, at, X20 + b)
                dst = xs[:, b, :] if b < NI else bc[:, (b - NI) // SG, b % SG, :]
                nc.scalar.activation(dst, cv[:, b % 2, :], ACT.Silu).then_inc(a_xs, 1)

            def ret_out(at, h):
                act.wait_ge(pe_ry, at.n * 4 + (h + 1))
                for e in range(2):
                    nc.scalar.copy(yr[:, 4 * h + 2 * e:4 * h + 2 * e + 2, :], mid[e][:, :]).then_inc(a_yr, 1)
                    nc.scalar.activation(sq2[:, 2 * e:2 * e + 2, :], mid[e][:, :], ACT.Square).then_inc(a_yr, 1)

            def roots(at, which, ready, count):
                act.wait_ge(ready, at.n * count + count)
                nc.scalar.activation(rr[:, :, :], ms[:, :, :], ACT.Sqrt).then_inc(a_root2, 1)

            def dt(at):
                act.wait_ge(v_dt, at.n * 4 + 2)
                nc.scalar.activation(dts[:, 2, :, :], dts[:, 1, :, :], ACT.Exp, scale=-1.0).then_inc(a_dt, 1)
                nc.scalar.activation(dts[:, 7, 0, :], par2("a_log"), ACT.Exp).then_inc(a_dt, 1)

            def dt_sums(at):
                act.wait_ge(pe_dt, at.n * 2 + 2)
                nc.scalar.copy(at_hi[0:SH, :], mid[0][0:SH, P:P + T]).then_inc(a_dt, 1)

            def pair(at, b):
                act.wait_ge(pe_bc, at.n * 16 + (b + 1))
                if b:
                    act.wait_ge(v_m, at.n * 16 + b)
                else:
                    act.wait_ge(v_dt, at.n * 4 + 4)
                for n in range(2):
                    h = 2 * b + n
                    nc.scalar.activation(lseg[:, n, 0:T], mid[n][:, 0:T], ACT.Exp, bias=dts[:, 9, 0, h:h + 1])
                    last = nc.scalar.activation(lseg[:, n, T:TRI], mid[n][:, T:TRI], ACT.Exp, bias=dts[:, 9, 1, h:h + 1])
                last.then_inc(a_l, 1)

            def z_square(at, b):
                act.wait_ge(v_z, at.n * 16 + (b + 1))
                if b >= 4:
                    act.wait_ge(pe_zm, at.n * 4 + b // 4)
                nc.scalar.activation(sqz[:, b % 4, :], xs[:, b, :], ACT.Square).then_inc(a_zsq, 1)

            def second_slab(at, i):
                split(at, i + AHEAD)
                if V20 <= i < X20:
                    j = (i - V20) * P
                    evac(at, i, i, vr[:, :, j:j + P], acc[i % 4][:, 0:T].rearrange("p (r c) -> p r c", r=2))
                elif X20 <= i < GR20:
                    b = i - X20
                    evac_conv = par2("conv_w", 3 * XB + b, 3 * XB + b + 1)
                    wait_used(act, at, i)
                    if b >= 2:
                        act.wait_ge(a_xs, at.n * XB + (b - 1))
                    nc.scalar.activation(cv[:, b % 2, :], acc[i % 4][:, 0:T], ACT.Identity, scale=evac_conv,
                                         bias=par2("conv_b", b, b + 1)).then_inc(a_cv, 1)
                    if b:
                        conv_silu(at, b - 1)
                    if b == XB - 1:
                        conv_silu(at, b)
                elif GR20 <= i < Z20:
                    b = i - GR20
                    if b >= 2:
                        act.wait_ge(v_flo, at.n * 16 + (b - 1))
                    evac(at, i, i, sg[:, b % 2, :], acc[i % 4][:, 0:T], ACT.Silu)
                elif Z20 <= i < RO_S:
                    b = i - Z20
                    if b >= 2:
                        act.wait_ge(v_z, at.n * 16 + (b - 1))
                    else:
                        act.wait_ge(v_flo, at.n * 16 + (15 + b))
                    evac(at, i, i, sg[:, b % 2, :], acc[i % 4][:, 0:T], ACT.Silu)
                    if b:
                        z_square(at, b - 1)
                    if b == NI - 1:
                        z_square(at, b)
                elif RO_S <= i < WO_S:
                    s0, t0 = (RO_S, RO_T) if i < SO_S else (SO_S, SO_T)
                    n, part = (i - s0) // 3, (i - s0) % 3
                    if part == 0:
                        t = t0 + 2 * n
                        if t >= RO_T + 4:
                            wait_out(act, at, t - 3)
                        else:
                            act.wait_ge(v_z, at.n * 16 + (15 + n))
                        evac(at, i, t, sg[:, n % 2, :], acc[t % 4][:, 0:T], ACT.Sigmoid)

            norm(Middle(), True, 0, last=True)
            act.dma_start(c2[:, :], c2_d).then_inc(consts2, 16)
            act.wait_ge(hf_ok, 4 * (2 * DEPTH + 1))
            with act.Fori(0, DEPTH) as n:
                at = Layer(True, n)
                wait_x(act, at, True, 0, KD - 1)
                act.dma_start(p2[:, :], p2_d[bass.ds(n, 1)].rearrange("a p n -> p (a n)")).then_inc(params, 16)
                act.dma_start(rdec[:, :, :], decay_d).then_inc(decays, 16)
                norm(at, True, 0)
                act.wait_ge(params, n * 16 + (DEPTH * 16 + 16))
                nc.scalar.copy(wdt_hi[:, :, :], par2("w_dt").rearrange("p (k h) -> p k h", k=KD)).then_inc(a_dt, 1)
                for task in tasks2():
                    if task[0] == "slab":
                        second_slab(at, task[1])
                    elif task[0] == "ret_y":
                        ret_out(at, task[1])
                    elif task[0] == "ret_rs":
                        roots(at, 0, v_rm, 4)
                    elif task[0] == "dt":
                        dt(at)
                    elif task[0] == "dt_sums":
                        dt_sums(at)
                    elif task[0] == "pair":
                        pair(at, task[1])
                    elif task[0] == "z_rs":
                        roots(at, 1, v_zm, 4)
                norm(at, True, 1)
                ffn(at, True)
            norm(Layer(True, DEPTH), True, 0, last=True)

        @block.vector
        def _(dve):
            tt, ts, stt = nc.vector.tensor_tensor, nc.vector.tensor_scalar, nc.vector.scalar_tensor_tensor
            copy = nc.vector.tensor_copy
            ADD, SUB, MUL, MAX, MIN = ALU.add, ALU.subtract, ALU.mult, ALU.max, ALU.min

            class Steps:

                def __init__(self, base):
                    self.base, self.n = base, 0
                    self.turned_back = self.scanned = None

                def next(self):
                    self.n += 1
                    return self.base + self.n

            def split(at, i):
                slot = i % RING
                dve.wait_ge(hi_done, at.slab + (i + 1))
                tt(w_lo[:, slot, 0:LO_V], w_raw[:, slot, 0:LO_V], w_hi[:, slot, 0:LO_V].bitcast(F32), SUB).then_inc(lo_v, 1)

            def norm(at, which, gain, dst, last=False):
                step = (at.norm + which) * 5
                dve.wait_ge(root_ok, at.norm + (which + 1))
                nc.vector.reciprocal(rinv[:, :], root[:, :]).then_inc(v_norm, 1)
                dve.wait_ge(v_norm, step + 1)
                stt(rtmp[:, :], mid[0][:, 0:T], EPS, rinv[:, :], ADD, MUL).then_inc(v_norm, 1)
                dve.wait_ge(v_norm, step + 2)
                tt(rtmp[:, :], rtmp[:, :], rinv[:, :], MUL).then_inc(v_norm, 1)
                dve.wait_ge(v_norm, step + 3)
                ts(rtmp[:, :], rtmp[:, :], -0.5, 1.5, MUL, ADD).then_inc(v_norm, 1)
                dve.wait_ge(v_norm, step + 4)
                tt(rinv[:, :], rinv[:, :], rtmp[:, :], MUL).then_inc(v_norm, 1)
                dve.wait_ge(v_norm, step + 5)
                for j in range(4):
                    stt(dst[:, 2 * j, :], x[:, 2 * j, :], gain[:, 2 * j:2 * j + 1], rinv[:, :], MUL, MUL)
                    stt(dst[:, 2 * j + 1, :], x[:, 2 * j + 1, :], gain[:, 2 * j + 1:2 * j + 2], rinv[:, :], MUL, MUL).then_inc(hf_ok, 1)
                if last:
                    return
                for j in range(4):
                    dve.wait_ge(hhi_ok, (at.split + which) * 4 + (j + 1))
                    a = slice(2 * j, 2 * j + 2)
                    tt(h_lo[:, a, :], work[:, a, :], h_hi[:, a, :].bitcast(F32), SUB).then_inc(h_ok, 1)

            def ffn(at, second):
                si, ti, so, to = ffn_layout(second)
                with dve.Fori(0, FF // 2) as it:
                    now = Later(at, it, 4, 4, 2)
                    for b in range(2):
                        gate_slab, t = si + 2 * b, ti + 2 * b + 1
                        split(now, gate_slab + AHEAD)
                        split(now, gate_slab + 1 + AHEAD)
                        wait_used(dve, now, gate_slab + 1)
                        wait_out(dve, now, t - 1)
                        tt(f_prod[:, b, :], f_act[:, b, :], acc[t % 4][:, 0:T], MUL).then_inc(out[t % 4], 1)
                        wait_out(dve, now, t)
                        k = bass.ds(it * 2 + b, 1)
                        copy(f_hi[:, k, :], f_prod[:, b:b + 1, :]).then_inc(ff_hi, 1)
                        dve.wait_ge(ff_hi, now.ffn + (b + 1))
                        tt(f_lo[:, k, :], f_prod[:, b:b + 1, :], f_hi[:, k, :].bitcast(F32), SUB).then_inc(ff_lo, 1)
                with dve.Fori(0, 2) as it:
                    now = Later(at, it, 12, 4)
                    for n in range(4):
                        for m in range(3):
                            split(now, so + 3 * n + m + AHEAD)
                        wait_used(dve, now, so + 3 * n + 2)
                        k = bass.ds(it * 4 + n, 1)
                        bank = acc[(to + n) % 4][:, 0:T].unsqueeze(1)
                        tt(x[:, k, :], x[:, k, :], bank, ADD).then_inc(out[(to + n) % 4], 1)

            def prep(at, own):
                a_re, a_im = par1("a_re"), par1("a_im")
                dve.wait_ge(a_prep, at.n * 4 + 1)
                tt(tiny[:, 1, :], a_re, tiny[:, 0, :], MUL).then_inc(v_prep, 1)
                tt(tiny[:, 3, :], a_im, tiny[:, 0, :], MUL).then_inc(dve_step, 1)
                dve.wait_ge(dve_step, own.next())
                ts(tiny[:, 4, :], tiny[:, 3, :], 1.0 / TWO_PI, ROUND, MUL, ADD).then_inc(dve_step, 1)
                dve.wait_ge(dve_step, own.next())
                ts(tiny[:, 7, :], tiny[:, 4, :], -ROUND, None, ADD).then_inc(dve_step, 1)
                a = 3
                for part, b in ((TWO_PI_1, 8), (TWO_PI_2, 9), (TWO_PI_3, 10)):
                    dve.wait_ge(dve_step, own.next())
                    stt(tiny[:, b, :], tiny[:, 7, :], -part, tiny[:, a, :], MUL, ADD).then_inc(dve_step, 1)
                    a = b
                dve.wait_ge(dve_step, own.next())
                ts(tiny[:, 5, :], tiny[:, 10, :], PI_F, -PI_F, MIN, MAX).then_inc(dve_step, 1)
                dve.wait_ge(dve_step, own.next())
                stt(tiny[:, 6, :], tiny[:, 5, :], -1.0, tiny[:, 5, :], MUL, MIN).then_inc(v_prep, 1)

            def prep_c(at, own):
                a_re, a_im, r = par1("a_re"), par1("a_im"), tiny[:, 2, :]
                dve.wait_ge(a_prep, at.n * 4 + 4)
                tt(tiny[:, 11, :], r, turn[:, 0, :, 0], MUL)
                tt(tiny[:, 12, :], r, turn[:, 1, :, 0], MUL)
                tt(tiny[:, 13, :], a_re, a_re, MUL)
                tt(tiny[:, 14, :], a_im, a_im, MUL)
                nc.vector.memset(decay[:, :, 0:1], 0.0)
                copy(decay[:, :, 1:CH], r.unsqueeze(2).to_broadcast([P, PAIRS, CH - 1])).then_inc(dve_step, 1)
                dve.wait_ge(dve_step, own.next())
                ts(tiny[:, 15, :], tiny[:, 11, :], -1.0, None, ADD)
                tt(tiny[:, 16, :], tiny[:, 13, :], tiny[:, 14, :], ADD).then_inc(dve_step, 1)
                dve.wait_ge(dve_step, own.next())
                nc.vector.reciprocal(tiny[:, 17, :], tiny[:, 16, :])
                tt(tiny[:, 18, :], tiny[:, 15, :], a_re, MUL)
                tt(tiny[:, 19, :], tiny[:, 12, :], a_im, MUL)
                tt(tiny[:, 20, :], tiny[:, 12, :], a_re, MUL)
                tt(tiny[:, 21, :], tiny[:, 15, :], a_im, MUL).then_inc(dve_step, 1)
                dve.wait_ge(dve_step, own.next())
                tt(tiny[:, 22, :], tiny[:, 18, :], tiny[:, 19, :], ADD)
                tt(tiny[:, 23, :], tiny[:, 20, :], tiny[:, 21, :], SUB).then_inc(dve_step, 1)
                dve.wait_ge(dve_step, own.next())
                tt(tiny[:, 24, :], tiny[:, 22, :], tiny[:, 17, :], MUL)
                tt(tiny[:, 25, :], tiny[:, 23, :], tiny[:, 17, :], MUL).then_inc(dve_step, 1)
                dve.wait_ge(dve_step, own.next())
                c_re = par1("c_re").rearrange("p (a c) -> p a c", a=PAIRS)
                c_im = par1("c_im").rearrange("p (a c) -> p a c", a=PAIRS)
                f_re = tiny[:, 24, :].unsqueeze(2).to_broadcast([P, PAIRS, PC])
                f_im = tiny[:, 25, :].unsqueeze(2).to_broadcast([P, PAIRS, PC])
                t0 = tm[:, 0, 0:PAIRS * PC].rearrange("p (a c) -> p a c", a=PAIRS)
                t1 = tm[:, 1, 0:PAIRS * PC].rearrange("p (a c) -> p a c", a=PAIRS)
                tt(cab[:, 0, :, :], c_re, f_re, MUL)
                tt(t0, c_im, f_im, MUL)
                tt(cab[:, 1, :, :], c_re, f_im, MUL)
                tt(t1, c_im, f_re, MUL).then_inc(dve_step, 1)
                dve.wait_ge(dve_step, own.next())
                tt(cab[:, 0, :, :], cab[:, 0, :, :], t0, SUB)
                stt(cab[:, 1, :, :], cab[:, 1, :, :], -1.0, t1, MUL, SUB).then_inc(v_prep, 1)

            def double(at, own, k):
                n = 1 << k
                if k == 0:
                    dve.wait_ge(v_prep, at.n * 3 + 3)
                cos, sin = turn[:, 0, :, 0:n], turn[:, 1, :, 0:n]
                cos_n = turn[:, 0, :, n - 1:n].to_broadcast([P, PAIRS, n])
                sin_n = turn[:, 1, :, n - 1:n].to_broadcast([P, PAIRS, n])
                t0 = tm[:, 0, 0:PAIRS * n].rearrange("p (a c) -> p a c", a=PAIRS)
                t1 = tm[:, 1, 0:PAIRS * n].rearrange("p (a c) -> p a c", a=PAIRS)
                tt(turn[:, 0, :, n:2 * n], cos, cos_n, MUL)
                tt(t0, sin, sin_n, MUL)
                tt(turn[:, 1, :, n:2 * n], sin, cos_n, MUL)
                tt(t1, cos, sin_n, MUL).then_inc(dve_step, 1)
                dve.wait_ge(dve_step, own.next())
                tt(turn[:, 0, :, n:2 * n], turn[:, 0, :, n:2 * n], t0, SUB)
                tt(turn[:, 1, :, n:2 * n], turn[:, 1, :, n:2 * n], t1, ADD).then_inc(dve_step, 1)
                dve.wait_ge(dve_step, own.next())

            def carry_factors(at, own):
                tt(tiny[:, 26, :], tiny[:, 2, :], turn[:, 0, :, CH - 1], MUL)
                tt(tiny[:, 27, :], tiny[:, 2, :], turn[:, 1, :, CH - 1], MUL).then_inc(dve_step, 1)
                dve.wait_ge(dve_step, own.next())

            def rope(at, own, b):
                dve.wait_ge(pe_rope, at.n * 5 + (b + 1))
                tt(prob[:, b, 0:T], mid[2 + b % 2][:, 0:T], con1("rope_s"), MUL)
                tt(qk[:, b, :], qk[:, b, :], con1("rope_c"), MUL).then_inc(dve_step, 1)
                dve.wait_ge(dve_step, own.next())
                tt(qk[:, b, :], qk[:, b, :], prob[:, b, 0:T], ADD).then_inc(v_rope, 1)

            def rot(at, own, c, first):
                dve.wait_ge(pe_bu, at.n * 4 + (c + 1))
                for q in (0, 1) if first else (2, 3):
                    bu = mid[q][:, :].rearrange("p (r b c) -> p r b c", r=2, b=N1)
                    cos, sin = (turn[:, part, :, :].rearrange("p (b q) c -> p b q c", q=4)[:, :, q, :].unsqueeze(1)
                                .to_broadcast([P, 2, N1, CH]) for part in range(2))
                    z = zs[:, :, :, :].rearrange("p r (b q) c -> p r b q c", q=4)[:, :, :, q, :]
                    t = tm[:, :, :].rearrange("p r (b q c) -> p r b q c", q=4, c=CH)[:, :, :, q, :]
                    tt(z, bu, cos, MUL)
                    last = tt(t, bu, sin, MUL)
                if first:
                    return
                last.then_inc(v_rot, 1)
                dve.wait_ge(v_rot, at.n * 4 + (c + 1))
                flat = [zs[:, part, :, :].rearrange("p a c -> p (a c)") for part in range(2)]
                tt(flat[0], flat[0], tm[:, 1, :], ADD)
                tt(flat[1], flat[1], tm[:, 0, :], SUB).then_inc(dve_step, 1)
                own.turned_back = own.next()

            def scan(at, own, c):
                dve.wait_ge(dve_step, own.turned_back)
                if c:
                    tt(zs[:, 0, :, 0], zs[:, 0, :, 0], tiny[:, 28, :], ADD)
                    tt(zs[:, 1, :, 0], zs[:, 1, :, 0], tiny[:, 29, :], ADD).then_inc(dve_step, 1)
                    dve.wait_ge(dve_step, own.next())
                flat = decay[:, :, :].rearrange("p a c -> p (a c)")
                for part in range(2):
                    z = zs[:, part, :, :].rearrange("p a c -> p (a c)")
                    last = nc.vector.tensor_tensor_scan(z, flat, z, 0.0, MUL, ADD)
                last.then_inc(dve_step, 1)
                dve.wait_ge(dve_step, own.next())
                z_re, z_im = zs[:, 0, :, CH - 1], zs[:, 1, :, CH - 1]
                tt(tiny[:, 28, :], z_re, tiny[:, 26, :], MUL)
                tt(tiny[:, 30, :], z_im, tiny[:, 27, :], MUL)
                tt(tiny[:, 29, :], z_im, tiny[:, 26, :], MUL)
                tt(tiny[:, 31, :], z_re, tiny[:, 27, :], MUL).then_inc(dve_step, 1)
                dve.wait_ge(dve_step, own.next())
                tt(tiny[:, 28, :], tiny[:, 28, :], tiny[:, 30, :], SUB)
                tt(tiny[:, 29, :], tiny[:, 29, :], tiny[:, 31, :], ADD).then_inc(dve_step, 1)
                own.scanned = own.next()

            def turn_states(at, own, c):
                dve.wait_ge(dve_step, own.scanned)
                if c:
                    dve.wait_ge(pe_y, at.n * 4 + c)
                cos, sin = turn[:, 0, :, :], turn[:, 1, :, :]
                t0 = tm[:, 0, :].rearrange("p (a c) -> p a c", a=PAIRS)
                t1 = tm[:, 1, :].rearrange("p (a c) -> p a c", a=PAIRS)
                tt(xst[:, 0, :, :], zs[:, 0, :, :], cos, MUL)
                tt(t0, zs[:, 1, :, :], sin, MUL)
                tt(xst[:, 1, :, :], zs[:, 1, :, :], cos, MUL)
                tt(t1, zs[:, 0, :, :], sin, MUL).then_inc(dve_step, 1)
                dve.wait_ge(dve_step, own.next())
                tt(xst[:, 0, :, :], xst[:, 0, :, :], t0, SUB)
                tt(xst[:, 1, :, :], xst[:, 1, :, :], t1, ADD).then_inc(v_x, 1)
                dve.wait_ge(v_x, at.n * 4 + (c + 1))

            def ssm_y(at, c):
                dve.wait_ge(pe_y, at.n * 4 + (c + 1))
                tokens = slice(c * CH, c * CH + CH)
                for blk in range(N1):
                    last = stt(u[:, blk, tokens], u[:, blk, tokens], par1("d", blk, blk + 1),
                               mid[2][:, blk * CH:(blk + 1) * CH], MUL, ADD)
                last.then_inc(v_y, 1)

            def scores(at, h):
                dve.wait_ge(pe_s, at.n * 8 + (h + 1))
                stt(prob[:, h, :], mid[3][:, 0:TRI], HD ** -0.5, con1("mask"), MUL, ADD).then_inc(v_mask, 1)

            def maxima(at, own):
                sink = par1("sink")
                dve.wait_ge(v_mask, at.n * 8 + 8)
                nc.vector.tensor_reduce(soft[:, 0, 0, :], prob[:, :, 0:P], AX_X, MAX)
                nc.vector.tensor_reduce(soft[:, 0, 1, :], prob[:, :, P:TRI], AX_X, MAX).then_inc(dve_step, 1)
                dve.wait_ge(dve_step, own.next())
                sinks = sink.unsqueeze(1).to_broadcast([P, 2, HEADS])
                tt(soft[:, 1, :, :], soft[:, 0, :, :], sinks, MAX).then_inc(dve_step, 1)
                dve.wait_ge(dve_step, own.next())
                ts(soft[:, 3, :, :], soft[:, 1, :, :], -1.0, None, MUL)
                tt(soft[:, 4, :, :], sinks, soft[:, 1, :, :], SUB).then_inc(v_max, 1)

            def normalize(at, own):
                dve.wait_ge(a_exp, at.n + 1)
                tt(soft[:, 7, :, :], soft[:, 6, :, :], soft[:, 5, :, :], ADD).then_inc(dve_step, 1)
                dve.wait_ge(dve_step, own.next())
                nc.vector.reciprocal(soft[:, 8, :, :], soft[:, 7, :, :]).then_inc(dve_step, 1)
                dve.wait_ge(dve_step, own.next())
                for r, (a, b) in enumerate(((0, P), (P, TRI))):
                    last = tt(prob[:, :, a:b], prob[:, :, a:b],
                              soft[:, 8, r, :].unsqueeze(2).to_broadcast([P, HEADS, b - a]), MUL)
                last.then_inc(v_p, 1)

            def attended(at, a):
                dve.wait_ge(a_ohi, at.n * 4 + (a + 1))
                tt(o_lo[:, a, :], mid[2][:, T:2 * T], o_hi[:, a, :].bitcast(F32), SUB).then_inc(v_olo, 1)

            def gelu(at):
                dve.wait_ge(a_gelu, at.n * 2 + 2)
                tt(ys_lo[:, :, :], ysg[:, :, :], ys_hi[:, :, :].bitcast(F32), SUB).then_inc(v_yslo, 1)

            def conv_lo(at, b):
                dve.wait_ge(a_chi, at.n * 4 + (b + 1))
                tt(cv_lo[:, b, :], cy[:, b % 2, :], cv_hi[:, b, :].bitcast(F32), SUB).then_inc(v_clo, 1)

            def first_slab(at, own, i):
                split(at, i + AHEAD)
                bank = acc[i % 4]
                if C0 <= i < G0:
                    b, part = (i - C0) // 3, (i - C0) % 3
                    if part == 1:
                        if b:
                            conv_lo(at, b - 1)
                        wait_used(dve, at, i)
                        wait_out(dve, at, i - 1)
                        y = ccx[:, b % 2, :]
                        tt(zpad[:, 8:8 + T], bank[:, 0:T], y, MUL).then_inc(out[i % 4], 1)
                        wait_out(dve, at, i)
                        w = [par1("conv_w", j * N1 + b, j * N1 + b + 1) for j in range(3)]
                        ts(y, zpad[:, 8:8 + T], w[2], None, MUL).then_inc(dve_step, 1)
                        dve.wait_ge(dve_step, own.next())
                        stt(y, zpad[:, 7:7 + T], w[1], y, MUL, ADD).then_inc(dve_step, 1)
                        dve.wait_ge(dve_step, own.next())
                        stt(y, zpad[:, 6:6 + T], w[0], y, MUL, ADD).then_inc(dve_step, 1)
                        dve.wait_ge(dve_step, own.next())
                    elif part == 2:
                        wait_used(dve, at, i)
                        tt(cy[:, b % 2, :], ccx[:, b % 2, :], bank[:, 0:T], MUL).then_inc(out[i % 4], 1)
                elif i == G0:
                    conv_lo(at, N1 - 1)
                elif CO0 <= i < AO0:
                    n = i - CO0
                    wait_used(dve, at, i)
                    if n == 0:
                        for t in range(CO0 - 4, CO0):
                            wait_out(dve, at, t)
                    tt(work[:, 2 * n:2 * n + 2, :], gate[:, 8 + 2 * n:10 + 2 * n, :],
                       bank[:, :].rearrange("p (b t) -> p b t", b=2), MUL).then_inc(out[i % 4], 1)
                elif AO0 <= i < GL0 or SO0 <= i < MX0:
                    n, g = (i - AO0, 0) if i < GL0 else (i - SO0, 16)
                    mine = slice(2 * n, 2 * n + 2)
                    wait_used(dve, at, i)
                    add = branch[:, n % 2, :].rearrange("p (b t) -> p b t", b=2)
                    tt(add, gate[:, g + 2 * n:g + 2 * n + 2, :], bank[:, :].rearrange("p (b t) -> p b t", b=2),
                       MUL).then_inc(out[i % 4], 1)
                    wait_out(dve, at, i)
                    if g == 0:
                        wait_out(dve, at, CO0 + n)
                        tt(work[:, mine, :], work[:, mine, :], add, ADD).then_inc(dve_step, 1)
                        dve.wait_ge(dve_step, own.next())
                    else:
                        tt(work[:, mine, :], work[:, mine, :], add, ADD).then_inc(v_mg, 1)
                        dve.wait_ge(a_mhi, at.n * 4 + (n + 1))
                        tt(h_lo[:, mine, :], work[:, mine, :], h_hi[:, mine, :].bitcast(F32), SUB).then_inc(v_mlo, 1)
                elif GL0 <= i < SO0:
                    n = i - GL0
                    mine = slice(2 * n, 2 * n + 2)
                    wait_out(dve, at, i)
                    tt(yv[:, mine, :], ysg[:, mine, :], glu[:, n, :].rearrange("p (b t) -> p b t", b=2), MUL).then_inc(v_yv, 1)
                    dve.wait_ge(a_yvhi, at.n * 2 + (n + 1))
                    tt(yv_lo[:, mine, :], yv[:, mine, :], yv_hi[:, mine, :].bitcast(F32), SUB).then_inc(v_yvlo, 1)
                elif MX0 <= i:
                    wait_used(dve, at, i)
                    tt(x[:, i - MX0, :], x[:, i - MX0, :], bank[:, 0:T], ADD).then_inc(out[i % 4], 1)

            dve.wait_ge(consts, 32)
            start = Layer(False, 0)
            for slot in range(AHEAD):
                split(start, slot)
            dve.wait_ge(pad_ok, 1)
            with dve.Fori(0, DEPTH) as n:
                at, own = Layer(False, n), Steps(n * V_STEPS1)
                dve.wait_ge(params, n * 16 + 16)
                norm(at, 0, par1("g_mix"), work)
                for task in tasks1():
                    if task[0] == "slab":
                        first_slab(at, own, task[1])
                    elif task[0] == "prep":
                        prep(at, own)
                    elif task[0] == "prep_c":
                        prep_c(at, own)
                    elif task[0] == "double":
                        double(at, own, task[1])
                    elif task[0] == "carry":
                        carry_factors(at, own)
                    elif task[0] == "rope":
                        rope(at, own, task[1])
                    elif task[0] == "rot":
                        rot(at, own, task[1], True)
                    elif task[0] == "rot2":
                        rot(at, own, task[1], False)
                    elif task[0] == "turn":
                        turn_states(at, own, task[1])
                    elif task[0] == "scan":
                        scan(at, own, task[1])
                    elif task[0] == "ssm_y":
                        ssm_y(at, task[1])
                    elif task[0] == "scores":
                        scores(at, task[1])
                    elif task[0] == "softmax":
                        maxima(at, own)
                    elif task[0] == "softnorm":
                        normalize(at, own)
                    elif task[0] == "gelu":
                        gelu(at)
                    elif task[0] == "pv" and task[1] % 2:
                        attended(at, task[1] // 2)
                norm(at, 1, par1("g_ffn"), work)
                ffn(at, False)
                assert own.n == V_STEPS1, own.n

            norm(Middle(), 0, con1("g_mid"), x, last=True)
            dve.wait_ge(consts2, 16)
            ts(above[:, :], con2("tri")[:, 0:P], -1.0, 1e30, ADD, MUL).then_inc(v_above, 1)

            def turned(at, own, i):
                dst = qt if i < K20 else kt
                h = (i - (0 if i < K20 else K20)) // 2
                wait_used(dve, at, i)
                first, second = acc[(i - 1) % 4][:, 0:T], acc[i % 4][:, 0:T]
                t0, t1 = rp[:, 0, 0:T], rp[:, 1, 0:T]
                tt(dst[:, 2 * h, :], first, con2("cos"), MUL)
                tt(t0, second, con2("sin"), MUL)
                tt(dst[:, 2 * h + 1, :], first, con2("sin"), MUL).then_inc(out[(i - 1) % 4], 1)
                tt(t1, second, con2("cos"), MUL).then_inc(out[i % 4], 1)
                wait_out(dve, at, i)
                tt(dst[:, 2 * h, :], dst[:, 2 * h, :], t0, SUB)
                tt(dst[:, 2 * h + 1, :], dst[:, 2 * h + 1, :], t1, ADD).then_inc(v_qk, 1)
                dve.wait_ge(v_qk, at.n * 8 + (i // 2 + 1))

            def conv(at, own, i):
                b = i - X20
                bank, y = acc[i % 4], cv[:, b % 2, :]
                dve.wait_ge(a_cv, at.n * XB + (b + 1))
                for j in (1, 2, 3):
                    w = par2("conv_w", (3 - j) * XB + b, (3 - j) * XB + b + 1)
                    op = stt(y[:, j:T], bank[:, 0:T - j], w, y[:, j:T], MUL, ADD)
                    if j < 3:
                        op.then_inc(dve_step2, 1)
                        dve.wait_ge(dve_step2, own.next())
                op.then_inc(out[i % 4], 1)

            def dt(at, own):
                dve.wait_ge(pe_dt, at.n * 2 + 1)
                tt(dts[:, 0, :, :], mid[0][:, 0:2 * SH].rearrange("p (r h) -> p r h", r=2),
                   par2("dt_b").unsqueeze(1).to_broadcast([P, 2, SH]), ADD).then_inc(dve_step2, 1)
                dve.wait_ge(dve_step2, own.next())
                stt(dts[:, 1, :, :], dts[:, 0, :, :], -1.0, dts[:, 0, :, :], MUL, MAX).then_inc(v_dt, 1)
                dve.wait_ge(a_dt, at.n * 4 + 3)
                e, s, s2, q = (dts[:, k, :, :] for k in (2, 3, 4, 5))
                ts(s, e, 2.0, None, ADD).then_inc(dve_step2, 1)
                dve.wait_ge(dve_step2, own.next())
                nc.vector.reciprocal(s2, s).then_inc(dve_step2, 1)
                dve.wait_ge(dve_step2, own.next())
                tt(s, e, s2, MUL).then_inc(dve_step2, 1)
                dve.wait_ge(dve_step2, own.next())
                tt(s2, s, s, MUL).then_inc(dve_step2, 1)
                dve.wait_ge(dve_step2, own.next())
                ts(q, s2, 1.0 / 17, None, MUL).then_inc(dve_step2, 1)
                for k in range(15, 1, -2):
                    dve.wait_ge(dve_step2, own.next())
                    stt(q, q, 1.0 / k, s2, ADD, MUL).then_inc(dve_step2, 1)
                dve.wait_ge(dve_step2, own.next())
                stt(q, q, 1.0, s, ADD, MUL).then_inc(dve_step2, 1)
                dve.wait_ge(dve_step2, own.next())
                tt(q, q, q, ADD).then_inc(dve_step2, 1)
                dve.wait_ge(dve_step2, own.next())
                stt(dts[:, 6, :, :], dts[:, 0, :, :], 0.0, q, MAX, ADD).then_inc(dve_step2, 1)
                dve.wait_ge(dve_step2, own.next())
                stt(dts[:, 8, :, :], dts[:, 6, :, :], -1.0, dts[:, 7, 0, :].unsqueeze(1).to_broadcast([P, 2, SH]),
                    MUL, MUL).then_inc(v_dt, 1)

            def dt_sums(at):
                dve.wait_ge(pe_dt, at.n * 2 + 2)
                dve.wait_ge(a_dt, at.n * 4 + 4)
                ts(dts[:, 9, :, :], mid[0][:, 2 * SH:4 * SH].rearrange("p (r h) -> p r h", r=2), -1.0, None, MUL)
                tt(at_lo[0:SH, :], mid[0][0:SH, P:P + T], at_hi[0:SH, :].bitcast(F32), SUB).then_inc(v_dt, 1)

            def ret_scores(at, h):
                dve.wait_ge(pe_rs, at.n * 4 + (h + 1))
                if h == 0:
                    dve.wait_ge(decays, at.n * 16 + 16)
                elif h >= 2:
                    dve.wait_ge(pe_ry, at.n * 4 + (h - 1))
                tt(rp[:, h % 2, :], mid[2][:, 0:TRI], rdec[:, h, :], MUL).then_inc(v_rp, 1)

            def roots(at, own, which):
                dve.wait_ge(a_root2, at.n * 2 + which + 1)
                nc.vector.reciprocal(nt[:, :, :], rr[:, :, :]).then_inc(dve_step2, 1)
                dve.wait_ge(dve_step2, own.next())
                tt(rr[:, :, :], ms[:, :, :], nt[:, :, :], MUL).then_inc(dve_step2, 1)
                dve.wait_ge(dve_step2, own.next())
                tt(rr[:, :, :], rr[:, :, :], nt[:, :, :], MUL).then_inc(dve_step2, 1)
                dve.wait_ge(dve_step2, own.next())
                ts(rr[:, :, :], rr[:, :, :], -0.5, 1.5, MUL, ADD).then_inc(dve_step2, 1)
                dve.wait_ge(dve_step2, own.next())
                tt(rr[:, :, :], rr[:, :, :], nt[:, :, :], MUL).then_inc(dve_step2, 1)
                dve.wait_ge(dve_step2, own.next())

            def turned_xs(at, m):
                dve.wait_ge(pe_xt, at.n * 8 + (m + 1))
                for b in range(2):
                    blk = 2 * m + b
                    last = tt(xdt[:, :, blk * P:(blk + 1) * P].rearrange("p r (h c) -> p r h c", h=2),
                              mid[1 + m % 2][:, b * T:(b + 1) * T].rearrange("p (r h c) -> p r h c", r=2, h=2),
                              dts[:, 6, :, 2 * blk:2 * blk + 2].unsqueeze(3).to_broadcast([P, 2, 2, SP_]), MUL)
                last.then_inc(v_xdt, 1)

            def c_times_b(at, g):
                dve.wait_ge(pe_cb, at.n * 4 + (g + 1))
                copy(cbm[:, g, :], mid[0][:, 0:TRI]).then_inc(v_cb, 1)

            def pair(at, b):
                dve.wait_ge(a_l, at.n * 16 + (b + 1))
                if b:
                    dve.wait_ge(pe_y2, at.n * 16 + b)
                else:
                    dve.wait_ge(v_cb, at.n * 4 + 4)
                tt(mt[:, :, :], lseg[:, :, :], cbm[:, b // 4, :].unsqueeze(1).to_broadcast([P, 2, TRI]), MUL).then_inc(v_m, 1)

            def pair_y(at, b):
                dve.wait_ge(pe_y2, at.n * 16 + (b + 1))
                stt(xs[:, b, :], xs[:, b, :], par2("d_skip", b, b + 1), mid[2 + b % 2][:, 0:T],
                    MUL, ADD).then_inc(v_ys, 1)

            def z_norm(at, own, b):
                y = pr[:, b % 2, :]
                stt(y, xs[:, b, :], par2("norm", b, b + 1), rr[:, b // 4, :], MUL, MUL).then_inc(dve_step2, 1)
                dve.wait_ge(dve_step2, own.next())
                copy(s_hi[:, b, :], y).then_inc(dve_step2, 1)
                dve.wait_ge(dve_step2, own.next())
                tt(s_lo[:, b, :], y, s_hi[:, b, :].bitcast(F32), SUB).then_inc(v_slo, 1)

            def second_slab(at, own, i):
                split(at, i + AHEAD)
                bank = acc[i % 4]
                if i < V20:
                    if i % 2:
                        turned(at, own, i)
                elif X20 <= i < GR20:
                    conv(at, own, i)
                elif GR20 <= i < Z20:
                    b = i - GR20
                    y = pr[:, b % 2, :]
                    wait_out(dve, at, i)
                    tt(y, sg[:, b % 2, :], yr[:, b, :], MUL).then_inc(dve_step2, 1)
                    dve.wait_ge(dve_step2, own.next())
                    tt(y, y, rr[:, b // 4, :], MUL).then_inc(dve_step2, 1)
                    dve.wait_ge(dve_step2, own.next())
                    copy(r_hi[:, b, :], y).then_inc(dve_step2, 1)
                    dve.wait_ge(dve_step2, own.next())
                    tt(r_lo[:, b, :], y, r_hi[:, b, :].bitcast(F32), SUB).then_inc(v_flo, 1)
                elif Z20 <= i < RO_S:
                    b = i - Z20
                    wait_out(dve, at, i)
                    dve.wait_ge(v_ys, at.n * 16 + (b + 1))
                    tt(xs[:, b, :], xs[:, b, :], sg[:, b % 2, :], MUL).then_inc(v_z, 1)
                elif RO_S <= i < WO_S:
                    s0, t0 = (RO_S, RO_T) if i < SO_S else (SO_S, SO_T)
                    n, part = (i - s0) // 3, (i - s0) % 3
                    if part == 2:
                        t = t0 + 2 * n + 1
                        wait_used(dve, at, i)
                        wait_out(dve, at, t - 1)
                        if i < SO_S:
                            tt(work[:, n, :], acc[t % 4][:, 0:T], sg[:, n % 2, :], MUL).then_inc(out[t % 4], 1)
                        else:
                            y = pr[:, n % 2, :]
                            tt(y, acc[t % 4][:, 0:T], sg[:, n % 2, :], MUL).then_inc(out[t % 4], 1)
                            wait_out(dve, at, t)
                            wait_out(dve, at, RO_T + 2 * n + 1)
                            tt(work[:, n, :], work[:, n, :], y, ADD).then_inc(dve_step2, 1)
                            dve.wait_ge(dve_step2, own.next())
                            copy(m_hi[:, n, :], work[:, n, :]).then_inc(dve_step2, 1)
                            dve.wait_ge(dve_step2, own.next())
                            tt(m_lo[:, n, :], work[:, n, :], m_hi[:, n, :].bitcast(F32), SUB).then_inc(v_mlo2, 1)
                elif WO_S <= i:
                    t = WO_T + i - WO_S
                    wait_used(dve, at, i)
                    tt(x[:, i - WO_S, :], x[:, i - WO_S, :], acc[t % 4][:, 0:T], ADD).then_inc(out[t % 4], 1)

            with dve.Fori(0, DEPTH) as n:
                at, own = Layer(True, n), Steps(n * V_STEPS2)
                dve.wait_ge(params, n * 16 + (DEPTH * 16 + 16))
                norm(at, 0, par2("g_mix"), work)
                dve.wait_ge(a_dt, at.n * 4 + 1)
                tt(wdt_lo[:, :, :], par2("w_dt").rearrange("p (k h) -> p k h", k=KD), wdt_hi[:, :, :].bitcast(F32),
                   SUB).then_inc(v_dt, 1)
                for task in tasks2():
                    if task[0] == "slab":
                        second_slab(at, own, task[1])
                    elif task[0] == "ret_s":
                        ret_scores(at, task[1])
                    elif task[0] == "ret_m":
                        dve.wait_ge(pe_rm, at.n * 4 + (task[1] + 1))
                        ts(ms[:, task[1], :], mid[3][:, 0:T], EPS, None, ADD).then_inc(v_rm, 1)
                    elif task[0] == "ret_rs":
                        roots(at, own, 0)
                    elif task[0] == "dt":
                        dt(at, own)
                    elif task[0] == "dt_sums":
                        dt_sums(at)
                    elif task[0] == "xdt":
                        turned_xs(at, task[1])
                    elif task[0] == "cb":
                        c_times_b(at, task[1])
                    elif task[0] == "pair":
                        pair(at, task[1])
                    elif task[0] == "pair_y":
                        pair_y(at, task[1])
                    elif task[0] == "z_m":
                        dve.wait_ge(pe_zm, at.n * 4 + (task[1] + 1))
                        ts(ms[:, task[1], :], mid[3][:, 0:T], EPS, None, ADD).then_inc(v_zm, 1)
                    elif task[0] == "z_rs":
                        roots(at, own, 1)
                    elif task[0] == "z_norm":
                        z_norm(at, own, task[1])
                norm(at, 1, par2("g_ffn"), work)
                ffn(at, True)
                assert own.n == V_STEPS2, own.n
            norm(Layer(True, DEPTH), 0, con1("g_final"), work, last=True)


def kernel(x, norm_mix, w_in, b_gate, attn_sinks, w_attn_o, conv_w, w_conv_o, ssm_a_re, ssm_a_im, ssm_b_re, ssm_b_im,
           ssm_c_re, ssm_c_im, ssm_d, ssm_log_dt, w_ssm_glu, w_ssm_o, w_mix_o, norm_ffn, w_ffn_in, w_ffn_out,
           norm_final, norm_mix_w_2, w_in_2, ret_out_2, conv_w_2, conv_b_2, dt_bias_2, a_log_2, d_skip_2, ssd_norm_w_2,
           ssd_out_2, w_o_2, norm_ffn_w_2, w_gate_up_2, w_down_2, final_norm_w_2):
    import numpy as np
    import concourse.bacc as bacc
    from concourse.bass_utils import run_bass_kernel_spmd

    arr = np.asarray
    f32 = np.float32

    def blocks(w, width=P):
        k, n = w.shape
        return w.reshape(k // P, P, n // width, width).transpose(2, 1, 0, 3)

    def columns(v):
        return v.reshape(-1, P).T

    def every(v):
        return np.broadcast_to(v, (P, v.size))

    def slabs8(w):
        return blocks(w).reshape(-1, P, SLAB)

    def slabs4(w):
        return blocks(w, 2 * P).reshape(-1, P, SLAB)

    def long_slabs(w):
        b = blocks(w)
        n, _, k, _ = b.shape
        m = -(-k // KD)
        full = np.zeros((n, P, m * KD, P), f32)
        full[:, :, :k] = b
        return full.reshape(n, P, m, SLAB).transpose(0, 2, 1, 3)

    head_order = np.arange(HEADS).reshape(2, HEADS // 2).T.reshape(-1)
    by_head = (head_order[:, None] * HD + np.arange(HD)).reshape(-1)

    stream = np.zeros((TOTAL + RING, P, SLAB), f32)
    p1_d = np.zeros((DEPTH, P, P1_N), f32)
    p2_d = np.zeros((DEPTH, P, P2_N), f32)
    at = 0

    def push(part):
        nonlocal at
        part = part.reshape(-1, P, SLAB)
        stream[at:at + len(part)] = part
        at += len(part)

    def interleave(*parts):
        parts = [p.reshape(p.shape[0], -1, P, SLAB) for p in parts]
        return np.concatenate(parts, axis=1)

    for n in range(DEPTH):
        q, k, v, cb, cc, cx, u, g = np.split(arr(w_in)[n], np.cumsum([512, 128, 128, 512, 512, 512, 512]), axis=1)
        push(slabs8(u))
        push(slabs8(q[:, by_head]))
        push(slabs8(k))
        push(slabs8(v))
        push(interleave(slabs8(cc), slabs8(cx), slabs8(cb)))
        push(slabs8(g))
        push(slabs4(arr(w_conv_o)[n]))
        push(slabs4(arr(w_attn_o)[n][by_head]))
        push(slabs4(arr(w_ssm_glu)[n]))
        push(slabs4(arr(w_ssm_o)[n]))
        push(slabs8(arr(w_mix_o)[n]))
        fi = arr(w_ffn_in)[n]
        push(interleave(slabs8(fi[:, :FF * P]), slabs8(fi[:, FF * P:])))
        push(long_slabs(arr(w_ffn_out)[n]))
        assert at == (n + 1) * S1

        p = p1_d[n]

        def put(name, value):
            lo, hi = P1[name]
            p[:, lo:hi] = value

        put("g_mix", columns(arr(norm_mix)[n]))
        put("g_ffn", columns(arr(norm_ffn)[n]))
        put("b_gate", columns(arr(b_gate)[n]))
        put("conv_w", columns(arr(conv_w)[n].reshape(-1)))
        put("d", columns(arr(ssm_d)[n]))
        put("sink", every(arr(attn_sinks)[n][head_order]))
        put("a_re", arr(ssm_a_re)[n].reshape(PAIRS, P).T)
        put("a_im", arr(ssm_a_im)[n].reshape(PAIRS, P).T)
        put("log_dt", np.repeat(arr(ssm_log_dt)[n].reshape(PAIRS, 2), 64, axis=1).T)
        for name, b in (("b_re", ssm_b_re), ("b_im", ssm_b_im)):
            b = arr(b)[n].reshape(N1, 4, 2, 64, 16)
            full = np.zeros((4, 2, 16, N1, 2, 64), f32)
            for a in range(2):
                full[:, a, :, :, a, :] = b[:, :, a].transpose(1, 3, 0, 2)
            put(name, full.reshape(P, N1 * P))
        for name, c in (("c_re", ssm_c_re), ("c_im", ssm_c_im)):
            c = arr(c)[n].reshape(PAIRS, 2, 16, 64)
            full = np.zeros((2, 64, PAIRS, 2, 16), f32)
            for a in range(2):
                full[a, :, :, a, :] = c[:, a].transpose(2, 0, 1)
            put(name, full.reshape(P, PAIRS * PC))

    for n in range(DEPTH):
        w = arr(w_in_2)[n]
        q, k, v, g, z, xbc, dt, gate_ret, gate_ssd = np.split(
            w, np.cumsum([1024, 1024, 2048, 2048, 2048, 3072, SH, 1024]), axis=1)
        for part in (q, k, v, xbc, g, z):
            push(slabs8(part))
        push(interleave(slabs8(gate_ret), long_slabs(arr(ret_out_2)[n])))
        push(interleave(slabs8(gate_ssd), long_slabs(arr(ssd_out_2)[n])))
        push(slabs8(arr(w_o_2)[n]))
        gu = arr(w_gate_up_2)[n]
        push(interleave(slabs8(gu[:, :FF * P]), slabs8(gu[:, FF * P:])))
        push(long_slabs(arr(w_down_2)[n]))
        assert at == DEPTH * S1 + (n + 1) * S2

        p = p2_d[n]

        def put2(name, value):
            lo, hi = P2[name]
            p[:, lo:hi] = value

        put2("g_mix", columns(arr(norm_mix_w_2)[n]))
        put2("g_ffn", columns(arr(norm_ffn_w_2)[n]))
        put2("conv_w", columns(arr(conv_w_2)[n].reshape(-1)))
        put2("conv_b", columns(arr(conv_b_2)[n]))
        put2("dt_b", every(arr(dt_bias_2)[n]))
        put2("a_log", every(arr(a_log_2)[n]))
        put2("d_skip", columns(np.repeat(arr(d_skip_2)[n], SP_)))
        put2("norm", columns(arr(ssd_norm_w_2)[n]))
        put2("w_dt", blocks(dt, SH)[0].reshape(P, KD * SH))

    c1_d = np.zeros((P, C1_N), f32)

    def put_c1(name, value):
        lo, hi = C1[name]
        c1_d[:, lo:hi] = value

    put_c1("ones_d", 1.0 / D)
    put_c1("ones_i", 1.0 / 512)
    put_c1("ident", np.eye(P))
    put_c1("g_mid", columns(arr(norm_final)))
    put_c1("g_final", columns(arr(final_norm_w_2)))
    pos = np.arange(T, dtype=f32)
    half = ROT // 2
    inv = (f32(500000.0) ** (-np.arange(0, ROT, 2, dtype=f32) / f32(ROT))).astype(f32)
    ang = (pos[:, None] * inv).astype(f32)
    rope_c, rope_s = np.ones((HD, T), f32), np.zeros((HD, T), f32)
    rope_c[:ROT] = np.tile(np.cos(ang).T, (2, 1))
    rope_s[:ROT] = np.tile(np.sin(ang).T, (2, 1))
    put_c1("rope_c", np.tile(rope_c, (2, 1)))
    put_c1("rope_s", np.tile(rope_s, (2, 1)))
    turn = np.zeros((P, P), f32)
    for base in (0, HD):
        for m in range(half):
            turn[base + m + half, base + m] = -1.0
            turn[base + m, base + m + half] = 1.0
    put_c1("rope_r", turn)
    i, j = np.arange(P)[:, None], np.arange(P)[None]
    put_c1("mask", np.where(np.concatenate([j <= i, j > i, j <= i], axis=1), 0.0, -1e30))

    c2_d = np.zeros((P, C2_N), f32)
    inv = (f32(10000.0) ** (-np.arange(P, dtype=f32) / f32(P))).astype(f32)
    ang = (pos[:, None] * inv).astype(f32)
    tri = np.concatenate([i <= j, np.ones((P, P), bool), i <= j], axis=1)
    c2_d[:, C2["cos"][0]:C2["cos"][1]] = np.cos(ang).T
    c2_d[:, C2["sin"][0]:C2["sin"][1]] = np.sin(ang).T
    c2_d[:, C2["tri"][0]:C2["tri"][1]] = tri
    gap = np.concatenate([j - i, j + P - i, j - i], axis=1)
    log_g = np.log(1.0 - 2.0 ** (-5.0 - np.arange(RH)))
    decay_d = np.where(tri[:, None, :], np.exp(log_g[None, :, None] * np.maximum(gap, 0)[:, None, :]), 0.0)
    decay_d = np.ascontiguousarray((decay_d * 256.0 ** -0.5).astype(f32))

    ins = {"weights_d": stream, "x_d": np.ascontiguousarray(arr(x)[0].T), "p1_d": p1_d, "p2_d": p2_d,
           "c1_d": c1_d, "c2_d": c2_d, "decay_d": decay_d}
    nc = bacc.Bacc("TRN2", target_bir_lowering=False, num_devices=1)
    args = [nc.dram_tensor(name, a.shape, mybir.dt.from_np(a.dtype), kind="ExternalInput").ap() for name, a in ins.items()]
    args.append(nc.dram_tensor("out_d", (D, T), F32, kind="ExternalOutput").ap())
    hybrid_kernel(nc, *args)
    result = run_bass_kernel_spmd(nc, [ins], core_ids=[0])
    return np.ascontiguousarray(result.results[0]["out_d"].T)[None]
```

```python
from contextlib import ExitStack

import concourse.bass as bass
from concourse import mybir

ALU = mybir.AluOpType
ACT = mybir.ActivationFunctionType
AX_X = mybir.AxisListType.X
F32 = mybir.dt.float32
F32R = mybir.dt.float32r
BF16 = mybir.dt.bfloat16

P = 128
T = 256
D = 1024
KD = D // P
DEPTH = 2
EPS = 1e-6
SLAB = 1024
RING = 4
AHEAD = 3
LO_V = 192
FF = 22

HEADS, KV_HEADS, HD = 8, 2, 64
ROT = 16
SCORE_BANKS = 0, 1, 2
ROPE_BANKS = 2, 3, 0

N1 = 512 // P
CH = 64
NCH = T // CH
PAIRS = 16
PC = 32

U0, Q0, K0, V0, C0, G0 = 0, 4, 8, 9, 10, 22
CO0, AO0, GL0, SO0, MX0, FI0 = 46, 50, 54, 56, 60, 68
FO_S1, FO_T1 = 112, 112
S1, T1 = 136, 120
Q20, K20, V20, X20, GR20, Z20 = 0, 8, 16, 32, 56, 72
RO_S, RO_T, SO_S, SO_T = 88, 88, 112, 104
WO_S, WO_T, FI_S2, FI_T2, FO_S2, FO_T2 = 136, 120, 144, 128, 188, 172
S2, T2 = 212, 180
TOTAL = DEPTH * (S1 + S2)

RH = 4
SH, SP_, SG = 32, 64, 4
NI = 16
XB = 24
TRI = 3 * P

P1 = {}
_at = 0
for _name, _n in (("g_mix", KD), ("g_ffn", KD), ("b_gate", 24), ("conv_w", 3 * N1), ("d", N1),
                  ("sink", HEADS), ("a_re", PAIRS), ("a_im", PAIRS), ("log_dt", PAIRS),
                  ("b_re", N1 * P), ("b_im", N1 * P), ("c_re", PAIRS * PC), ("c_im", PAIRS * PC)):
    P1[_name] = (_at, _at + _n)
    _at += _n
P1_N = _at
P2 = {}
_at = 0
for _name, _n in (("g_mix", KD), ("g_ffn", KD), ("conv_w", 4 * XB), ("conv_b", XB), ("dt_b", SH),
                  ("a_log", SH), ("d_skip", NI), ("norm", NI), ("w_dt", KD * SH)):
    P2[_name] = (_at, _at + _n)
    _at += _n
P2_N = _at
C1 = {}
_at = 0
for _name, _n in (("ones_d", P), ("ones_i", P), ("ident", P), ("g_mid", KD), ("g_final", KD),
                  ("rope_c", T), ("rope_s", T), ("rope_r", P), ("mask", TRI)):
    C1[_name] = (_at, _at + _n)
    _at += _n
C1_N = _at
C2 = {}
_at = 0
for _name, _n in (("cos", T), ("sin", T), ("tri", TRI)):
    C2[_name] = (_at, _at + _n)
    _at += _n
C2_N = _at

V_STEPS1 = 72
V_STEPS2 = 150

TWO_PI = 6.283185307179586
TWO_PI_1 = 6.28125
TWO_PI_2 = 0.0019350051879882812
TWO_PI_3 = TWO_PI - TWO_PI_1 - TWO_PI_2
ROUND = 12582912.0
HALF_PI = 1.5707963267948966
PI_F = 3.1415925


def bu_order(c):
    return (0, 1, 2, 3) if c < NCH - 1 else (3, 1, 2, 0)


def tasks1():
    after = {}

    def put(i, *steps):
        after.setdefault(i, []).extend(steps)

    put(1, ("prep",))
    put(2, ("prep_c",))
    for k in range(6):
        put(3 + k, ("double", k))
    put(9, ("carry",))
    for b in range(KV_HEADS * 2 + 1):
        put(9 + b // 3, ("rope", b))
        put(10 + b // 3, ("rope_mul", b))
    put(10, ("vt",))
    put(11, ("vt_copy",))
    put(36, ("pv_lo", 0))
    for c, i in enumerate((11, 20, 30, 41)):
        for j in range(4):
            put(i + 1 + j, ("rot", c, j))
        put(i + (4 if c == NCH - 1 else 5), ("scan", c))
        put(i + 6, ("turn", c))
        put(i + 9, ("cx", c))
        put(i + 10, ("ssm_y", c))
    for c, i in enumerate((11, 20, 30, 41)):
        for j in range(4):
            put(i + j, ("bu", c, j))
    put(52, ("gelu",))
    put(53, ("gelu_lo",))
    for h in range(HEADS):
        i = (15, 17, 24)[h // 3]
        put(i, ("scores", h))
        put(i + (2 if 3 <= h < 6 else 1), ("mask", h))
    put(28, ("maxima",))
    put(29, ("softmax",))
    put(32, ("normalize",))
    for a in range(HEADS // 2):
        put(34 + 2 * a, ("pt", 2 * a), ("pt", 2 * a + 1))
        put(35 + 2 * a, ("pt_copy", 2 * a), ("pt_copy", 2 * a + 1))
    for a in range(HEADS // 2):
        put(35 + 2 * a, ("pv", 2 * a), ("pv", 2 * a + 1))
        put(36 + 2 * a, ("pv_copy", a))
        if a:
            put(37 + 2 * a, ("pv_lo", a))
    return [t for i in range(FI0) for t in [("slab", i)] + after.get(i, [])]


def tasks2():
    out = [("slab", i) for i in range(X20)]
    for i, step in ((7, "softplus"), (7, "dt_act"), (6, "dt_rows"), (4, "dt_copy"), (2, "dt")):
        out.insert(V20 + i, (step,))
    ret = [t for h in range(RH) for t in (("ret_s", h), ("ret_y", h), ("ret_m", h))]
    for n in range(XB):
        out.append(("slab", X20 + n))
        if n % 2 == 1:
            out.append(ret.pop(0))
    out.append(("ret_rs",))
    for b in range(NI):
        out.append(("slab", GR20 + b))
        if b == 3:
            out.append(("dt_sums",))
        if 1 <= b < 9:
            out.append(("xdt", b - 1))
        elif 9 <= b < 9 + SG:
            out.append(("cb", b - 9))
    after = {}
    for b in range(NI):
        i = RO_S + 3 * (b // 2) + b % 2
        after.setdefault(i, []).append(("pair", b))
        after.setdefault(i + 1 + b % 2, []).extend([("pair_y", b), ("z_mul", b)])
        after.setdefault(i + 2 + b % 2, []).append(("z_sq", b))
        if b % 4 == 3:
            after.setdefault(i + 4, []).append(("z_m", b // 4))
    after.setdefault(SO_S + 2, []).append(("z_rs",))
    for m in range(NI // 2):
        after.setdefault(SO_S + 3 + m // 2, []).append(("z_norm", m))
    for i in range(Z20, FI_S2):
        out += [("slab", i)] + after.get(i, [])
    return out


def hybrid_kernel(nc, weights, x_t, p1_d, p2_d, c1_d, c2_d, decay_d, out_t):
    with ExitStack() as ctx:
        top = [16512]

        def place(name, shape, dtype=F32, at=None):
            n = 4
            for v in shape[1:]:
                n *= v
            if at is None:
                at = top[0]
                top[0] += -(-n // 32) * 32
            assert at + n <= nc.sbuf_usable_end, (name, at + n)
            return nc.alloc_sbuf_tensor_at(name, shape, dtype, offset=at)

        w_raw = place("w_raw", [P, RING, SLAB])
        w_hi = place("w_hi", [P, RING, SLAB], F32R)
        w_lo = place("w_lo", [P, RING, SLAB], F32R)
        x = place("x", [P, KD, T])
        h_hi = place("h_hi", [P, KD, T], F32R)
        h_lo = place("h_lo", [P, KD, T], F32R)
        work_at = top[0]
        work = place("work", [P, KD, T])
        norm_at = top[0]
        root = place("root", [P, T])
        rinv = place("rinv", [P, T])
        rtmp = place("rtmp", [P, T])
        zpad_at = top[0]
        zpad = place("zpad", [P, 8 + T])
        sel = place("sel", [P, SH], F32R)
        c1_at = top[0]
        c1 = place("c1", [P, C1_N])
        p_at = top[0]
        p1 = place("p1", [P, P1_N])
        arena = top[0]

        def in_arena(name, at, shape, dtype=F32):
            return place(name, shape, dtype, arena + at)

        f_hi = in_arena("f_hi", 0, [P, FF, T], F32R)
        f_lo = in_arena("f_lo", 22528, [P, FF, T], F32R)
        f_act = in_arena("f_act", 45056, [P, 2, T])
        f_prod = in_arena("f_prod", 47104, [P, 2, T])
        g_hi = in_arena("g_hi", 51200, [P, KD, T], F32R)
        g_lo = in_arena("g_lo", 59392, [P, KD, T], F32R)
        gate = in_arena("gate", 0, [P, 24, T])
        u = in_arena("u", 24576, [P, N1, T])
        qk = in_arena("qk", 28672, [P, 5, T])
        vrow = in_arena("vrow", 33792, [P, 2, P])
        turn = in_arena("turn", 34816, [P, 2, PAIRS, CH])
        decay = in_arena("decay", 43008, [P, PAIRS, CH])
        zs = in_arena("zs", 47104, [P, 2, PAIRS, CH])
        tm = in_arena("tm", 55296, [P, 2, PAIRS * CH])
        xst = in_arena("xst", 63488, [P, 2, PAIRS, CH])
        cab = in_arena("cab", 71680, [P, 2, PAIRS, PC])
        prob = in_arena("prob", 75776, [P, HEADS, TRI])
        probt = in_arena("probt", 88064, [P, 2, TRI])
        vt = in_arena("vt", 88064, [P, T])
        o_hi = in_arena("o_hi", 91136, [P, N1, T], F32R)
        o_lo = in_arena("o_lo", 95232, [P, N1, T], F32R)
        ccx = in_arena("ccx", 99328, [P, 2, T])
        cy = in_arena("cy", 101376, [P, 2, T])
        branch = in_arena("branch", 75776, [P, 2, 2 * T])
        cv_hi = in_arena("cv_hi", 103424, [P, N1, T], F32R)
        cv_lo = in_arena("cv_lo", 107520, [P, N1, T], F32R)
        ysg = in_arena("ysg", 55296, [P, N1, T])
        ys_hi = in_arena("ys_hi", 59392, [P, N1, T], F32R)
        ys_lo = in_arena("ys_lo", 47104, [P, N1, T], F32R)
        glu = in_arena("glu", 51200, [P, 2, 2 * T])
        yv = in_arena("yv", 34816, [P, N1, T])
        yv_hi = in_arena("yv_hi", 38912, [P, N1, T], F32R)
        yv_lo = in_arena("yv_lo", 43008, [P, N1, T], F32R)
        tiny = place("tiny", [P, 40, PAIRS], at=work_at)
        soft = place("soft", [P, 10, 2, HEADS], at=work_at + 4096)
        qt = in_arena("qt", 0, [P, 2 * RH, T])
        kt = in_arena("kt", 8192, [P, 2 * RH, T])
        vr = in_arena("vr", 16384, [P, 2, NI * P])
        r_hi = in_arena("r_hi", 0, [P, NI, T], F32R)
        r_lo = in_arena("r_lo", 16384, [P, NI, T], F32R)
        sgs = in_arena("sgs", 16384, [P, KD, T])
        m_hi = in_arena("m_hi", 0, [P, KD, T], F32R)
        m_lo = in_arena("m_lo", 8192, [P, KD, T], F32R)
        rp = in_arena("rp", 32768, [P, 2, TRI])
        rdec = in_arena("rdec", 35840, [P, RH, TRI])
        lseg = in_arena("lseg", 41984, [P, 2, TRI])
        xs = in_arena("xs", 45056, [P, NI, T])
        xdt = in_arena("xdt", 61440, [P, 2, NI * P])
        sq2 = in_arena("sq2", 61440, [P, 4, T])
        sqz = in_arena("sqz", 35840, [P, 4, T])
        s_hi = in_arena("s_hi", 61440, [P, NI, T], F32R)
        yr = in_arena("yr", 77824, [P, NI, T])
        s_lo = in_arena("s_lo", 77824, [P, NI, T], F32R)
        mt = in_arena("mt", 94208, [P, 2, TRI])
        wdt_hi = in_arena("wdt_hi", 94208, [P, KD, SH], F32R)
        wdt_lo = in_arena("wdt_lo", 95232, [P, KD, SH], F32R)
        nt = in_arena("nt", 65536, [P, 4, T])
        cv = in_arena("cv", 97280, [P, 2, T])
        sums = in_arena("sums", 97280, [P, TRI], F32R)
        dth = in_arena("dth", 99328, [P, T])
        ms = in_arena("ms", 99328, [P, 4, T])
        rr = in_arena("rr", 103424, [P, 4, T])
        sg = in_arena("sg", 107520, [P, 2, T])
        pr = in_arena("pr", 109568, [P, 2, T])
        dts = place("dts", [P, 12, 2, SH], at=norm_at)
        bc = place("bc", [P, 2, SG, T], at=work_at)
        c2 = place("c2", [P, C2_N], at=c1_at + 4 * C1["rope_c"][0])
        p2 = place("p2", [P, P2_N], at=p_at)
        cbm = place("cbm", [P, SG, TRI], at=p_at + 4 * P2_N)
        above_at = c1_at + 4 * (C1["rope_c"][0] + C2_N)
        above = place("above", [P, P], BF16, at=above_at)
        unit = place("unit", [P, P], BF16, at=above_at + 2 * P)
        assert P2_N + SG * TRI <= P1_N and C2_N + P <= C1_N - C1["rope_c"][0]

        def par1(name, a=0, b=None):
            lo, hi = P1[name]
            return p1[:, lo + a:hi if b is None else lo + b]

        def par2(name, a=0, b=None):
            lo, hi = P2[name]
            return p2[:, lo + a:hi if b is None else lo + b]

        def con1(name):
            return c1[:, C1[name][0]:C1[name][1]]

        def con2(name):
            return c2[:, C2[name][0]:C2[name][1]]

        acc = [ctx.enter_context(nc.psum_tensor(f"acc{i}", [P, 512], F32)) for i in range(4)]
        mid = [ctx.enter_context(nc.psum_tensor(f"mid{i}", [P, 512], F32)) for i in range(4)]

        def sem(name):
            return ctx.enter_context(nc.semaphore(name))

        landed = [sem(f"landed{i}") for i in range(RING)]
        hi_done = sem("hi_done")
        lo_v = sem("lo_v")
        lo_g = sem("lo_g")
        used = sem("used")
        out = [sem(f"out{i}") for i in range(4)]
        consts = sem("consts")
        consts2 = sem("consts2")
        decays = sem("decays")
        params = sem("params")
        v_above = sem("v_above")
        pad_ok = sem("pad_ok")
        stored = sem("stored")
        sq_ok = sem("sq_ok")
        mean_ok = sem("mean_ok")
        log_ok = sem("log_ok")
        root_ok = sem("root_ok")
        hf_ok = sem("hf_ok")
        hhi_ok = sem("hhi_ok")
        h_ok = sem("h_ok")
        ff_hi = sem("ff_hi")
        ff_lo = sem("ff_lo")
        v_norm = sem("v_norm")
        gain_hi = sem("gain_hi")
        gain_lo = sem("gain_lo")
        v_gate = sem("v_gate")
        v_prod = sem("v_prod")
        dve_step = sem("dve_step")
        dve_step2 = sem("dve_step2")
        a_prep = sem("a_prep")
        v_prep = sem("v_prep")
        pe_rope = sem("pe_rope")
        v_rope = sem("v_rope")
        pe_bu = sem("pe_bu")
        v_rot = sem("v_rot")
        v_x = sem("v_x")
        pe_y = sem("pe_y")
        v_y = sem("v_y")
        a_gelu = sem("a_gelu")
        v_yslo = sem("v_yslo")
        pe_v = sem("pe_v")
        a_v = sem("a_v")
        pe_s = sem("pe_s")
        v_mask = sem("v_mask")
        v_max = sem("v_max")
        a_exp = sem("a_exp")
        v_p = sem("v_p")
        pe_t = sem("pe_t")
        a_pt = sem("a_pt")
        pe_pv = sem("pe_pv")
        a_ohi = sem("a_ohi")
        v_olo = sem("v_olo")
        a_chi = sem("a_chi")
        v_clo = sem("v_clo")
        v_yv = sem("v_yv")
        a_yvhi = sem("a_yvhi")
        v_yvlo = sem("v_yvlo")
        v_mg = sem("v_mg")
        a_mhi = sem("a_mhi")
        v_mlo = sem("v_mlo")
        a_cv = sem("a_cv")
        a_xs = sem("a_xs")
        pe_rs = sem("pe_rs")
        v_rp = sem("v_rp")
        pe_ry = sem("pe_ry")
        a_yr = sem("a_yr")
        pe_rm = sem("pe_rm")
        v_rm = sem("v_rm")
        a_log2 = sem("a_log2")
        a_root2 = sem("a_root2")
        v_qk = sem("v_qk")
        a_dt = sem("a_dt")
        v_dt = sem("v_dt")
        pe_dt = sem("pe_dt")
        pe_xt = sem("pe_xt")
        v_xdt = sem("v_xdt")
        pe_cb = sem("pe_cb")
        v_cb = sem("v_cb")
        pe_bc = sem("pe_bc")
        a_l = sem("a_l")
        v_m = sem("v_m")
        pe_y2 = sem("pe_y2")
        v_ys = sem("v_ys")
        v_flo = sem("v_flo")
        v_z = sem("v_z")
        a_zsq = sem("a_zsq")
        pe_zm = sem("pe_zm")
        v_zm = sem("v_zm")
        v_slo = sem("v_slo")
        v_mlo2 = sem("v_mlo2")

        block = ctx.enter_context(nc.Block())

        class Layer:

            def __init__(self, second, n):
                self.n = n
                self.slab = n * S2 + DEPTH * S1 if second else n * S1
                self.four = n * (T2 // 4) + DEPTH * (T1 // 4) if second else n * (T1 // 4)
                self.norm = n * 2 + (2 * DEPTH + 1 if second else 0)
                self.split = n + (DEPTH if second else 0)
                self.normed = n + (DEPTH + 1 if second else 0)
                self.ffn = n * FF + (DEPTH * FF if second else 0)

        def wait_used(eng, at, i):
            eng.wait_ge(used, at.slab + (i + 1 + RING))

        def wait_out(eng, at, t):
            eng.wait_ge(out[t % 4], at.four + (t // 4 + 3))

        class Middle:
            norm = 2 * DEPTH
            normed = DEPTH
            four = DEPTH * (T1 // 4)

        def ffn_layout(second):
            return (FI_S2, FI_T2, FO_S2, FO_T2) if second else (FI0, FI0, FO_S1, FO_T1)

        class Later:

            def __init__(self, at, it, slabs, tiles, ffn=0):
                self.n, self.norm, self.split = at.n, at.norm, at.split
                self.slab = at.slab + it * slabs
                self.four = at.four + it * (tiles // 4)
                self.ffn = at.ffn + it * ffn

        @block.sync
        def _(sp):
            def load(s, slot):
                sp.dma_start(w_raw[:, slot, :], weights[bass.ds(s, 1)].rearrange("a p n -> p (a n)")
                             ).then_inc(landed[slot], 16)

            for slot in range(RING):
                load(slot, slot)
            with sp.Fori(1, TOTAL // RING + 1) as it:
                for slot in range(RING):
                    sp.wait_ge(lo_v, it * RING + (slot + 1 - RING))
                    sp.wait_ge(lo_g, it * RING + (slot + 1 - RING))
                    load(it * RING + slot, slot)
            for j in range(4):
                sp.wait_ge(hf_ok, 4 * (2 * DEPTH + 1) + j + 1)
                sp.dma_start(out_t.rearrange("(k p) t -> p k t", p=P)[:, 2 * j:2 * j + 2, :],
                             work[:, 2 * j:2 * j + 2, :]).then_inc(stored, 16)
            sp.wait_ge(stored, 64)
            for slot in range(RING):
                sp.wait_ge(landed[slot], 16 * (TOTAL // RING + 1))

        @block.gpsimd
        def _(pool):
            nc.gpsimd.memset(zpad[:, 0:8], 0.0).then_inc(pad_ok, 1)
            with pool.Fori(0, TOTAL // RING) as it:
                for slot in range(RING):
                    pool.wait_ge(hi_done, it * RING + (slot + 1))
                    nc.gpsimd.tensor_tensor(w_lo[:, slot, LO_V:], w_raw[:, slot, LO_V:],
                                            w_hi[:, slot, LO_V:].bitcast(F32), ALU.subtract).then_inc(lo_g, 1)
            for slot in range(AHEAD):
                pool.wait_ge(hi_done, TOTAL + slot + 1)
                nc.gpsimd.tensor_tensor(w_lo[:, slot, LO_V:], w_raw[:, slot, LO_V:],
                                        w_hi[:, slot, LO_V:].bitcast(F32), ALU.subtract).then_inc(lo_g, 1)

        @block.tensor
        def _(pe):
            mm = nc.tensor.matmul

            def mean(at, which, b):
                pe.wait_ge(sq_ok, (at.norm + which) * KD + (b + 1))
                part = mm(mid[0][:, 0:T], con1("ones_d"), work[:, b, :], start=b == 0, stop=b == KD - 1)
                if b == KD - 1:
                    part.then_inc(mean_ok, 1)

            def norm(at, which):
                for b in range(KD):
                    mean(at, which, b)

            def weights_of(at, i):
                pe.wait_ge(lo_v, at.slab + (i + 1))
                pe.wait_ge(lo_g, at.slab + (i + 1))

            def bank(at, t):
                pe.wait_ge(out[t % 4], at.four + (t // 4 + 2))

            def products(at, i, dst, col, width, ks, hi, lo, first=True, last=True, need=None):
                slot = i % RING
                for j, k in enumerate(ks):
                    if need is not None:
                        need(k)
                    a = j * width + col
                    wh, wl = w_hi[:, slot, a:a + P], w_lo[:, slot, a:a + P]
                    mm(dst, wh, hi[:, k, :], start=first and j == 0, stop=False)
                    mm(dst, wh, lo[:, k, :], start=False, stop=False)
                    done = mm(dst, wl, hi[:, k, :], start=False, stop=last and j == len(ks) - 1)
                return done

            def slab_normed(at, i, t):
                weights_of(at, i)
                bank(at, t)
                slot, dst = i % RING, acc[t % 4][:, 0:T]
                for k in range(KD):
                    a = slice(k * P, k * P + P)
                    pe.wait_ge(hhi_ok, at.split * 4 + (k // 2 + 1))
                    mm(dst, w_hi[:, slot, a], h_hi[:, k, :], start=k == 0, stop=False)
                    mm(dst, w_lo[:, slot, a], h_hi[:, k, :], start=False, stop=False)
                for k in range(KD):
                    pe.wait_ge(h_ok, at.split * 4 + (k // 2 + 1))
                    last = mm(dst, w_hi[:, slot, k * P:k * P + P], h_lo[:, k, :], start=False, stop=k == KD - 1)
                last.then_inc(used, 1)

            def slab_gained(at, i, t):
                weights_of(at, i)
                bank(at, t)
                slot, dst = i % RING, acc[t % 4][:, 0:T]
                for k in range(KD):
                    if k == KD // 2:
                        mean(at, 1, KD - 1)
                    a = slice(k * P, k * P + P)
                    pe.wait_ge(gain_hi, at.split * KD + (k + 1))
                    mm(dst, w_hi[:, slot, a], g_hi[:, k, :], start=k == 0, stop=False)
                    mm(dst, w_lo[:, slot, a], g_hi[:, k, :], start=False, stop=False)
                for k in range(KD):
                    pe.wait_ge(gain_lo, at.split * KD + (k + 1))
                    last = mm(dst, w_hi[:, slot, k * P:k * P + P], g_lo[:, k, :], start=False, stop=k == KD - 1)
                last.then_inc(used, 1)

            def slab_k8(at, i, t, need=None, hi=h_hi, lo=h_lo):
                weights_of(at, i)
                bank(at, t)
                products(at, i, acc[t % 4][:, 0:T], 0, P, range(KD), hi, lo, need=need).then_inc(used, 1)

            def slab_k4(at, i, t, hi, lo):
                weights_of(at, i)
                bank(at, t)
                for b in range(2):
                    done = products(at, i, acc[t % 4][:, b * T:(b + 1) * T], b * P, 2 * P, range(4), hi, lo)
                done.then_inc(used, 1)

            def slabs_long(at, i, t, n, blocks, hi, lo, need=None):
                bank(at, t)
                for m in range(n):
                    weights_of(at, i + m)
                    ks = range(m * KD, min(m * KD + KD, blocks))
                    products(at, i + m, acc[t % 4][:, 0:T], 0, P, ks, hi, lo, m == 0, m == n - 1, need).then_inc(used, 1)

            def slabs_rows(at, i, t):
                weights_of(at, i + 1)
                slots = slice(i % RING, i % RING + 2)
                for r in range(2):
                    bank(at, t + r)
                    dst = acc[(t + r) % 4][:, 0:2 * P]
                    for k in range(KD):
                        wh, wl = w_hi[:, slots, k * P:(k + 1) * P], w_lo[:, slots, k * P:(k + 1) * P]
                        hh, hl = h_hi[:, k, r * P:(r + 1) * P], h_lo[:, k, r * P:(r + 1) * P]
                        mm(dst, hh, wh, start=k == 0, stop=False)
                        mm(dst, hh, wl, start=False, stop=False)
                        done = mm(dst, hl, wh, start=False, stop=k == KD - 1)
                done.then_inc(used, 2)

            def ffn(at, second):
                si, ti, so, to = ffn_layout(second)
                slab_gained(at, si, ti)
                for j in range(1, 4):
                    slab_k8(at, si + j, ti + j, None, g_hi, g_lo)
                with pe.Fori(1, FF // 2) as it:
                    now = Later(at, it, 4, 4)
                    for j in range(4):
                        slab_k8(now, si + j, ti + j, None, g_hi, g_lo)

                def act_ready(k):
                    pe.wait_ge(ff_lo, at.ffn + (k + 1))

                for n in range(KD):
                    slabs_long(at, so + 3 * n, to + n, 3, FF, f_hi, f_lo, act_ready if n == 0 else None)
                    if n:
                        mean(at, 2, n - 1)
                mean(at, 2, KD - 1)

            def s5_in(at, c, j):
                q = bu_order(c)[j]
                if c == 0:
                    if j == 0:
                        for t in range(4):
                            wait_out(pe, at, U0 + t)
                        pe.wait_ge(v_rope, at.n * 5 + 3)
                    elif j == 1:
                        pe.wait_ge(a_v, at.n + 1)
                    elif j == 2:
                        pe.wait_ge(v_rope, at.n * 5 + 5)
                elif q == 3:
                    pe.wait_ge(v_y, at.n * 4 + c)
                elif c < 3:
                    pe.wait_ge(v_mask, at.n * 8 + (6 if c == 1 else 8))
                elif q:
                    pe.wait_ge(a_pt, at.n * 8 + 8)
                else:
                    pe.wait_ge(v_olo, at.n * 4 + 4)
                if c:
                    pe.wait_ge(v_rot, at.n * 16 + 4 * c)
                rows = slice(PC * q, PC * q + PC)
                for part, name in ((0, "b_re"), (1, "b_im")):
                    for blk in range(N1):
                        b = p1[rows, P1[name][0] + blk * P:P1[name][0] + (blk + 1) * P]
                        dst = mid[q][:, (part * N1 + blk) * CH:(part * N1 + blk + 1) * CH]
                        last = mm(dst, b, u[rows, blk, c * CH:(c + 1) * CH], start=True, stop=True,
                                  tile_position=(PC * q, 0))
                last.then_inc(pe_bu, 1)

            def s5_out(at, c):
                pe.wait_ge(v_x, at.n * 4 + (c + 1))
                if c == 0:
                    pe.wait_ge(v_prep, at.n * 3 + 3)
                for blk in range(N1):
                    for q in range(4):
                        pair = blk * 4 + q
                        dst = mid[3][PC * q:PC * q + PC, blk * CH:(blk + 1) * CH]
                        mm(dst, cab[:, 0, pair, :], xst[:, 0, pair, :], start=True, stop=False, tile_position=(0, PC * q))
                        last = mm(dst, cab[:, 1, pair, :], xst[:, 1, pair, :], start=False, stop=True,
                                  tile_position=(0, PC * q))
                last.then_inc(pe_y, 1)

            def rope(at, b):
                wait_out(pe, at, Q0 + b)
                if b >= 3:
                    pe.wait_ge(v_rope, at.n * 5 + (b - 2))
                mm(mid[ROPE_BANKS[b % 3]][:, 0:T], con1("rope_r"), qk[:, b, :],
                   start=True, stop=True).then_inc(pe_rope, 1)

            def value_rows(at):
                wait_out(pe, at, V0)
                for r in range(2):
                    last = nc.tensor.transpose(mid[1][:, r * P:(r + 1) * P], vt[:, r * P:(r + 1) * P], con1("ident"))
                last.then_inc(pe_v, 1)

            def scores(at, h):
                a, g = h // 2, h % 2
                if h in (0, 6):
                    pe.wait_ge(v_rot, at.n * 16 + (6 if h else 3))
                elif 3 <= h < 6:
                    pe.wait_ge(v_mask, at.n * 8 + (h - 2))
                rows = slice(HD * g, HD * g + HD)
                dst = mid[SCORE_BANKS[h % 3]]
                mm(dst[:, 0:P], qk[rows, a, 0:P], qk[rows, 4, 0:P], start=True, stop=True)
                mm(dst[:, P:TRI], qk[rows, a, P:T], qk[rows, 4, :], start=True, stop=True).then_inc(pe_s, 1)

            def turn_probs(at, h):
                if h < 2:
                    pe.wait_ge(v_p, at.n + 1)
                    pe.wait_ge(v_rot, at.n * 16 + 11)
                else:
                    pe.wait_ge(a_pt, at.n * 8 + (h - 1))
                for j in range(3):
                    last = nc.tensor.transpose(mid[1 + h % 2][:, j * P:(j + 1) * P], prob[:, h, j * P:(j + 1) * P], con1("ident"))
                last.then_inc(pe_t, 1)

            def values(at, h):
                a, g = h // 2, h % 2
                pe.wait_ge(a_pt, at.n * 8 + (h + 1))
                if h == 0:
                    pe.wait_ge(a_v, at.n + 1)
                if g == 0 and a > 0:
                    pe.wait_ge(v_olo, at.n * 4 + a)
                rows = slice(HD * g, HD * g + HD)
                mm(mid[0][rows, 0:T], vrow[:, 0, rows], probt[:, h % 2, 0:T], start=True, stop=False,
                   tile_position=(0, HD * g))
                mm(mid[0][rows, P:T], vrow[:, 1, rows], probt[:, h % 2, T:TRI], start=False, stop=True,
                   tile_position=(0, HD * g)).then_inc(pe_pv, 1)

            def first_slab(at, i):
                if i == 0:
                    slab_normed(at, i, i)
                elif i < CO0:
                    slab_k8(at, i, i)
                elif i < AO0:
                    if i == CO0:
                        pe.wait_ge(v_clo, at.n * 4 + 4)
                    slab_k4(at, i, i, cv_hi, cv_lo)
                elif i < GL0:
                    if i == AO0:
                        pe.wait_ge(v_olo, at.n * 4 + 4)
                    slab_k4(at, i, i, o_hi, o_lo)
                elif i < SO0:
                    if i == GL0:
                        pe.wait_ge(v_yslo, at.n + 1)
                    slab_k4(at, i, i, ys_hi, ys_lo)
                elif i < MX0:
                    if i == SO0:
                        pe.wait_ge(v_yvlo, at.n * 2 + 2)
                    slab_k4(at, i, i, yv_hi, yv_lo)
                else:
                    slab_k8(at, i, i, (lambda k: pe.wait_ge(v_mlo, at.n * 4 + (k // 2 + 1))) if i == MX0 else None)
                    if i > MX0:
                        mean(at, 1, i - MX0 - 1)

            pe.sem_inc(used, RING)
            for t in range(4):
                pe.sem_inc(out[t], 2)
            pe.wait_ge(consts, 16 * 2)
            norm(Layer(False, 0), 0)
            with pe.Fori(0, DEPTH) as n:
                at = Layer(False, n)
                for task in tasks1():
                    if task[0] == "slab":
                        first_slab(at, task[1])
                    elif task[0] == "rope":
                        rope(at, task[1])
                    elif task[0] == "bu":
                        s5_in(at, task[1], task[2])
                    elif task[0] == "cx":
                        s5_out(at, task[1])
                    elif task[0] == "vt":
                        value_rows(at)
                    elif task[0] == "scores":
                        scores(at, task[1])
                    elif task[0] == "pt":
                        turn_probs(at, task[1])
                    elif task[0] == "pv":
                        values(at, task[1])
                ffn(at, False)

            def ret_scores(at, h):
                if h == 0:
                    pe.wait_ge(v_qk, at.n * 8 + 8)
                else:
                    pe.wait_ge(v_rp, at.n * 4 + h)
                for d in range(2):
                    mm(mid[2][:, 0:T], kt[:, 2 * h + d, 0:P], qt[:, 2 * h + d, :], start=d == 0, stop=d == 1)
                for d in range(2):
                    last = mm(mid[2][:, T:TRI], kt[:, 2 * h + d, P:T], qt[:, 2 * h + d, P:T], start=d == 0, stop=d == 1)
                last.then_inc(pe_rs, 1)

            def ret_values(at, h):
                pe.wait_ge(v_rp, at.n * 4 + (h + 1))
                if h == 0:
                    for t in range(V20 + 12, V20 + 16):
                        wait_out(pe, at, t)
                for e in range(4):
                    a = (h * 4 + e) * P
                    dst = mid[e // 2]
                    c = (e % 2) * T
                    mm(dst[:, c:c + T], vr[:, 0, a:a + P], rp[:, h % 2, 0:T], start=True, stop=False)
                    last = mm(dst[:, c + P:c + T], vr[:, 1, a:a + P], rp[:, h % 2, T:TRI], start=False, stop=True)
                last.then_inc(pe_ry, 1)

            def ret_mean(at, h):
                pe.wait_ge(a_yr, at.n * 16 + (4 * h + 4))
                if h:
                    pe.wait_ge(v_rm, at.n * 4 + h)
                for e in range(4):
                    last = mm(mid[3][:, 0:T], con1("ones_i"), sq2[:, e, :], start=e == 0, stop=e == 3)
                last.then_inc(pe_rm, 1)

            def dt(at):
                pe.wait_ge(v_dt, at.n * 4 + 1)
                dst = mid[1][0:SH, 0:T]
                for k in range(KD):
                    mm(dst, wdt_hi[:, k, :], h_hi[:, k, :], start=k == 0, stop=False)
                    mm(dst, wdt_hi[:, k, :], h_lo[:, k, :], start=False, stop=False)
                    last = mm(dst, wdt_lo[:, k, :], h_hi[:, k, :], start=False, stop=k == KD - 1)
                last.then_inc(pe_dt, 1)

            def dt_rows(at):
                pe.wait_ge(a_dt, at.n * 5 + 2)
                for r in range(2):
                    last = mm(mid[0][:, r * SH:(r + 1) * SH], dth[0:SH, r * P:(r + 1) * P], con1("ident")[0:SH, 0:SH],
                              start=True, stop=True)
                last.then_inc(pe_dt, 1)

            def dt_sums(at):
                pe.wait_ge(v_dt, at.n * 4 + 3)
                pe.wait_ge(a_yr, at.n * 16 + 16)
                tri = con2("tri")
                la = dts[:, 8, :, :]
                a0 = 2 * SH
                mm(mid[0][:, a0:a0 + SH], tri[:, 0:P], la[:, 0, :], start=True, stop=True)
                mm(mid[0][:, a0 + SH:a0 + 2 * SH], tri[:, P:T], la[:, 0, :], start=True, stop=False)
                mm(mid[0][:, a0 + SH:a0 + 2 * SH], tri[:, T:TRI], la[:, 1, :], start=False, stop=True)
                for k in range(2):
                    rows = slice(SH * k, SH * k + SH)
                    mm(mid[0][rows, P:P + T], la[:, 0, :], tri[:, 0:T], start=True, stop=False, tile_position=(0, SH * k))
                    last = mm(mid[0][rows, T:P + T], la[:, 1, :], tri[:, T:TRI], start=False, stop=True,
                              tile_position=(0, SH * k))
                last.then_inc(pe_dt, 1)

            def turn_xs(at, m):
                pe.wait_ge(a_xs, at.n * XB + (2 * m + 2))
                if m >= 2:
                    pe.wait_ge(v_xdt, at.n * 8 + (m - 1))
                elif m == 1:
                    pe.wait_ge(v_rp, at.n * 4 + 4)
                for b in range(2):
                    for r in range(2):
                        c = (2 * b + r) * P
                        last = nc.tensor.transpose(mid[1 + m % 2][:, c:c + P], xs[:, 2 * m + b, r * P:(r + 1) * P],
                                                   con1("ident"))
                last.then_inc(pe_xt, 1)

            def c_times_b(at, g):
                if g == 0:
                    pe.wait_ge(a_xs, at.n * XB + XB)
                    pe.wait_ge(v_dt, at.n * 4 + 4)
                else:
                    pe.wait_ge(v_cb, at.n * 4 + g)
                mm(mid[0][:, 0:T], bc[:, 0, g, 0:P], bc[:, 1, g, :], start=True, stop=True)
                mm(mid[0][:, T:TRI], bc[:, 0, g, P:T], bc[:, 1, g, P:T], start=True, stop=True).then_inc(pe_cb, 1)

            def sums_of_pair(at, b):
                if b:
                    pe.wait_ge(a_l, at.n * 16 + b)
                else:
                    pe.wait_ge(v_cb, at.n * 4 + 4)
                    pe.wait_ge(v_xdt, at.n * 8 + 8)
                    pe.wait_ge(v_dt, at.n * 4 + 4)
                for n in range(2):
                    pick = sel[0:2 * SH, 2 * b + n:2 * b + n + 1].to_broadcast([2 * SH, P])
                    mm(mid[n][:, 0:TRI], pick, sums[0:2 * SH, :], start=True, stop=False)
                    for lo in (0, T):
                        last = mm(mid[n][:, lo:lo + P], unit[:, :], above[:, :], start=False, stop=lo == T)
                last.then_inc(pe_bc, 1)

            def ssd_values(at, b):
                pe.wait_ge(v_m, at.n * 16 + (b + 1))
                if b >= 2:
                    pe.wait_ge(v_ys, at.n * 16 + (b - 1))
                if b >= 5 and b % 2:
                    pe.wait_ge(v_zm, at.n * 4 + (b - 1) // 4)
                dst = mid[2 + b % 2]
                for n in range(2):
                    h = 2 * b + n
                    rows = slice(SP_ * n, SP_ * n + SP_)
                    mm(dst[rows, 0:T], xdt[:, 0, h * SP_:(h + 1) * SP_], mt[:, n, 0:T], start=True, stop=False,
                       tile_position=(0, SP_ * n))
                    last = mm(dst[rows, P:T], xdt[:, 1, h * SP_:(h + 1) * SP_], mt[:, n, T:TRI],
                              start=False, stop=True, tile_position=(0, SP_ * n))
                last.then_inc(pe_y2, 1)

            def ssd_mean(at, g):
                pe.wait_ge(a_zsq, at.n * 16 + (4 * g + 4))
                if g:
                    pe.wait_ge(v_zm, at.n * 4 + g)
                pe.wait_ge(v_ys, at.n * 16 + (4 * g + 4))
                for e in range(4):
                    last = mm(mid[3][:, 0:T], con1("ones_i"), sqz[:, e, :], start=e == 0, stop=e == 3)
                last.then_inc(pe_zm, 1)

            def second_slab(at, i):
                if i == 0:
                    slab_normed(at, i, i)
                elif V20 <= i < X20:
                    if i % 2 == 0:
                        slabs_rows(at, i, i)
                elif i < RO_S:
                    slab_k8(at, i, i)
                elif i < SO_S:
                    n, part = (i - RO_S) // 3, (i - RO_S) % 3
                    if part == 0:
                        slab_k8(at, i, RO_T + 2 * n)
                    elif part == 1:
                        slabs_long(at, i, RO_T + 2 * n + 1, 2, NI, r_hi, r_lo,
                                   (lambda k: pe.wait_ge(v_flo, at.n * NI + (k + 1))) if n == 0 else None)
                elif i < SO_S + KD:
                    slab_k8(at, i, SO_T + i - SO_S)
                elif i < WO_S:
                    n, part = (i - SO_S - KD) // 2, (i - SO_S) % 2
                    if part == 0:
                        slabs_long(at, i, SO_T + KD + n, 2, NI, s_hi, s_lo,
                                   (lambda k: pe.wait_ge(v_slo, at.n * 8 + (k // 2 + 1))) if n == 0 else None)
                else:
                    slab_k8(at, i, WO_T + i - WO_S,
                            (lambda k: pe.wait_ge(v_mlo2, at.n * 8 + (k + 1))) if i == WO_S else None, m_hi, m_lo)
                    if i > WO_S:
                        mean(at, 1, i - WO_S - 1)

            pe.wait_ge(v_above, 1)
            pe.wait_ge(consts2, 16)
            norm(Layer(True, 0), 0)
            with pe.Fori(0, DEPTH) as n:
                at = Layer(True, n)
                for task in tasks2():
                    if task[0] == "slab":
                        second_slab(at, task[1])
                    elif task[0] == "ret_s":
                        ret_scores(at, task[1])
                    elif task[0] == "ret_y":
                        ret_values(at, task[1])
                    elif task[0] == "ret_m":
                        ret_mean(at, task[1])
                    elif task[0] == "dt":
                        dt(at)
                    elif task[0] == "dt_rows":
                        dt_rows(at)
                    elif task[0] == "dt_sums":
                        dt_sums(at)
                    elif task[0] == "xdt":
                        turn_xs(at, task[1])
                    elif task[0] == "cb":
                        c_times_b(at, task[1])
                    elif task[0] == "pair":
                        sums_of_pair(at, task[1])
                    elif task[0] == "pair_y":
                        ssd_values(at, task[1])
                    elif task[0] == "z_m":
                        ssd_mean(at, task[1])
                ffn(at, True)

        def wait_x(eng, at, second, which, b):
            if which == 0:
                eng.wait_ge(out[b % 4], at.four + (b // 4 + 1))
            elif which == 1:
                wait_out(eng, at, (WO_T if second else MX0) + b)
            else:
                wait_out(eng, at, (FO_T2 if second else FO_T1) + b)

        @block.scalar
        def _(act):
            def split(at, i):
                slot = i % RING
                act.wait_ge(landed[slot], (at.slab // RING + (i // RING + 1)) * 16)
                act.wait_ge(used, at.slab + (i + 1))
                nc.scalar.copy(w_hi[:, slot, :], w_raw[:, slot, :]).then_inc(hi_done, 1)

            def evac(at, i, t, dst, src, func=ACT.Copy, **kw):
                wait_used(act, at, i)
                nc.scalar.activation(dst, src, func, **kw).then_inc(out[t % 4], 1)

            def square(at, second, which, b):
                wait_x(act, at, second, which, b)
                nc.scalar.activation(work[:, b, :], x[:, b, :], ACT.Square).then_inc(sq_ok, 1)

            def gained(at, second, b):
                gain = (par2 if second else par1)("g_ffn", b, b + 1)
                wait_x(act, at, second, 1, b)
                nc.scalar.activation(g_hi[:, b, :], x[:, b, :], ACT.Identity, scale=gain).then_inc(gain_hi, 1)

            def norm(at, which, last=False):
                act.wait_ge(mean_ok, at.norm + (which + 1))
                nc.scalar.activation(root[:, :], mid[0][:, 0:T], ACT.Ln, bias=EPS).then_inc(log_ok, 1)
                act.wait_ge(log_ok, at.norm + (which + 1))
                nc.scalar.activation(rinv[:, :], root[:, :], ACT.Exp, scale=-0.5).then_inc(root_ok, 1)
                if last or which:
                    return
                for j in range(4):
                    act.wait_ge(hf_ok, at.normed * 4 + (j + 1))
                    nc.scalar.copy(h_hi[:, 2 * j:2 * j + 2, :], work[:, 2 * j:2 * j + 2, :]).then_inc(hhi_ok, 1)

            def ffn(at, second):
                si, ti, so, to = ffn_layout(second)
                square(at, second, 1, KD - 1)
                gained(at, second, KD - 1)
                split(at, si + AHEAD)
                norm(at, 1)
                with act.Fori(0, FF // 2) as it:
                    now = Later(at, it, 4, 4, 2)
                    for b in range(2):
                        split(now, si + 2 * b + 1 + AHEAD)
                        act.wait_ge(v_gate, now.ffn + (b + 1))
                        nc.scalar.activation(f_act[:, b, :], f_act[:, b, :], ACT.Silu).then_inc(out[(ti + 2 * b) % 4], 1)
                        split(now, si + 2 * b + 2 + AHEAD)
                for b in range(KD):
                    for j in range(3):
                        if b or j:
                            split(at, so + 3 * b + j + AHEAD)
                    if b:
                        square(at, second, 2, b - 1)
                square(at, second, 2, KD - 1)

            def prep(at):
                act.wait_ge(h_ok, at.split * 4 + 4)
                nc.scalar.activation(tiny[:, 0, :], par1("log_dt"), ACT.Exp).then_inc(a_prep, 1)
                act.wait_ge(v_prep, at.n * 3 + 1)
                nc.scalar.activation(tiny[:, 2, :], tiny[:, 1, :], ACT.Exp).then_inc(a_prep, 1)
                act.wait_ge(v_prep, at.n * 3 + 2)
                nc.scalar.activation(turn[:, 1, :, 0], tiny[:, 5, :], ACT.Sin).then_inc(a_prep, 1)
                nc.scalar.activation(turn[:, 0, :, 0], tiny[:, 6, :], ACT.Sin, bias=HALF_PI).then_inc(a_prep, 1)

            def softmax(at):
                act.wait_ge(v_max, at.n + 1)
                nc.scalar.activation(soft[:, 5, :, :], soft[:, 4, :, :], ACT.Exp)
                for h in range(HEADS):
                    for r, (a, b) in enumerate(((0, P), (P, TRI))):
                        last = nc.scalar.activation(prob[:, h, a:b], prob[:, h, a:b], ACT.Exp, bias=soft[:, 3, r, h:h + 1],
                                                    accum_out=soft[:, 6, r, h:h + 1])
                last.then_inc(a_exp, 1)

            def gelu(at):
                act.wait_ge(v_y, at.n * 4 + 4)
                nc.scalar.activation(ysg[:, :, :], u[:, :, :], ACT.Gelu_apprx_tanh).then_inc(a_gelu, 1)
                act.wait_ge(a_gelu, at.n * 2 + 1)
                nc.scalar.copy(ys_hi[:, :, :], ysg[:, :, :]).then_inc(a_gelu, 1)

            def probs(at, h):
                act.wait_ge(pe_t, at.n * 8 + (h + 1))
                if h >= 2:
                    act.wait_ge(pe_pv, at.n * 8 + (h - 1))
                nc.scalar.copy(probt[:, h % 2, :], mid[1 + h % 2][:, 0:TRI]).then_inc(a_pt, 1)

            def attended(at, a):
                act.wait_ge(pe_pv, at.n * 8 + (2 * a + 2))
                nc.scalar.copy(o_hi[:, a, :], mid[0][:, 0:T]).then_inc(a_ohi, 1)

            def first_slab(at, i):
                split(at, i + AHEAD)
                bank = acc[i % 4]
                if i < Q0:
                    evac(at, i, i, u[:, i, :], bank[:, 0:T])
                elif i < V0:
                    evac(at, i, i, qk[:, i - Q0, :], bank[:, 0:T])
                elif i == V0:
                    evac(at, i, i, vt[:, :], bank[:, 0:T])
                elif i < G0:
                    b, part = (i - C0) // 3, (i - C0) % 3
                    if part == 0:
                        if b >= 2:
                            wait_out(act, at, i - 4)
                        evac(at, i, i, ccx[:, b % 2, :], bank[:, 0:T])
                    if part == 2:
                        wait_out(act, at, i)
                        nc.scalar.copy(cv_hi[:, b, :], cy[:, b % 2, :]).then_inc(a_chi, 1)
                elif i < CO0:
                    evac(at, i, i, gate[:, i - G0, :], bank[:, 0:T], ACT.Sigmoid, bias=par1("b_gate", i - G0, i - G0 + 1))
                elif GL0 <= i < SO0:
                    evac(at, i, i, glu[:, i - GL0, :], bank[:, :], ACT.Sigmoid)
                    act.wait_ge(v_yv, at.n * 2 + (i - GL0 + 1))
                    a = 2 * (i - GL0)
                    nc.scalar.copy(yv_hi[:, a:a + 2, :], yv[:, a:a + 2, :]).then_inc(a_yvhi, 1)
                elif MX0 < i:
                    square(at, False, 1, i - MX0 - 1)
                    gained(at, False, i - MX0 - 1)
                elif SO0 <= i < MX0:
                    act.wait_ge(v_mg, at.n * 4 + (i - SO0 + 1))
                    a = 2 * (i - SO0)
                    nc.scalar.copy(h_hi[:, a:a + 2, :], work[:, a:a + 2, :]).then_inc(a_mhi, 1)

            act.dma_start(x[:, :, :], x_t.rearrange("(k p) t -> p k t", p=P)).then_inc(consts, 16)
            act.dma_start(c1[:, :], c1_d).then_inc(consts, 16)
            start = Layer(False, 0)
            for slot in range(AHEAD):
                split(start, slot)
            act.wait_ge(consts, 32)
            for b in range(KD):
                square(start, False, 0, b)
            with act.Fori(0, DEPTH) as n:
                at = Layer(False, n)
                wait_x(act, at, False, 0, KD - 1)
                act.dma_start(p1[:, :], p1_d[bass.ds(n, 1)].rearrange("a p n -> p (a n)")).then_inc(params, 16)
                norm(at, 0)
                act.wait_ge(params, n * 16 + 16)
                for task in tasks1():
                    if task[0] == "slab":
                        first_slab(at, task[1])
                    elif task[0] == "prep":
                        prep(at)
                    elif task[0] == "vt_copy":
                        act.wait_ge(pe_v, n + 1)
                        nc.scalar.copy(vrow[:, :, :], mid[1][:, 0:T]).then_inc(a_v, 1)
                    elif task[0] == "softmax":
                        softmax(at)
                    elif task[0] == "gelu":
                        gelu(at)
                    elif task[0] == "pt_copy":
                        probs(at, task[1])
                    elif task[0] == "pv_copy":
                        attended(at, task[1])
                ffn(at, False)

            def conv_silu(at, b):
                wait_out(act, at, X20 + b)
                dst = xs[:, b, :] if b < NI else bc[:, (b - NI) // SG, b % SG, :]
                nc.scalar.activation(dst, cv[:, b % 2, :], ACT.Silu).then_inc(a_xs, 1)

            def ret_out(at, h):
                act.wait_ge(pe_ry, at.n * 4 + (h + 1))
                for e in range(2):
                    nc.scalar.copy(yr[:, 4 * h + 2 * e:4 * h + 2 * e + 2, :], mid[e][:, :]).then_inc(a_yr, 1)
                    nc.scalar.activation(sq2[:, 2 * e:2 * e + 2, :], mid[e][:, :], ACT.Square).then_inc(a_yr, 1)

            def roots(at, which, ready, count):
                act.wait_ge(ready, at.n * count + count)
                nc.scalar.activation(nt[:, :, :], ms[:, :, :], ACT.Ln).then_inc(a_log2, 1)
                act.wait_ge(a_log2, at.n * 2 + (which + 1))
                nc.scalar.activation(rr[:, :, :], nt[:, :, :], ACT.Exp, scale=-0.5).then_inc(a_root2, 1)

            def dt_copy(at):
                act.wait_ge(pe_dt, at.n * 3 + 1)
                nc.scalar.copy(dth[0:SH, :], mid[1][0:SH, 0:T]).then_inc(a_dt, 1)

            def dt(at):
                act.wait_ge(v_dt, at.n * 4 + 2)
                nc.scalar.activation(dts[:, 2, :, :], dts[:, 1, :, :], ACT.Exp, scale=-1.0).then_inc(a_dt, 1)
                nc.scalar.activation(dts[:, 7, 0, :], par2("a_log"), ACT.Exp).then_inc(a_dt, 1)

            def dt_sums(at):
                act.wait_ge(pe_dt, at.n * 3 + 3)
                act.wait_ge(a_xs, at.n * XB + XB)
                nc.scalar.copy(sums[0:2 * SH, 0:T], mid[0][0:2 * SH, P:P + T])
                nc.scalar.copy(sums[0:2 * SH, T:TRI], mid[0][0:2 * SH, T:P + T]).then_inc(a_dt, 1)

            def pair(at, b):
                act.wait_ge(pe_bc, at.n * 16 + (b + 1))
                if b:
                    act.wait_ge(v_m, at.n * 16 + b)
                else:
                    act.wait_ge(v_dt, at.n * 4 + 4)
                for n in range(2):
                    h = 2 * b + n
                    nc.scalar.activation(lseg[:, n, 0:T], mid[n][:, 0:T], ACT.Exp, bias=dts[:, 9, 0, h:h + 1])
                    last = nc.scalar.activation(lseg[:, n, T:TRI], mid[n][:, T:TRI], ACT.Exp, bias=dts[:, 9, 1, h:h + 1])
                last.then_inc(a_l, 1)

            def z_square(at, b):
                act.wait_ge(v_z, at.n * 16 + (b + 1))
                if b >= 4:
                    act.wait_ge(pe_zm, at.n * 4 + b // 4)
                nc.scalar.activation(sqz[:, b % 4, :], xs[:, b, :], ACT.Square).then_inc(a_zsq, 1)

            def second_slab(at, i):
                split(at, i + AHEAD)
                if V20 <= i < X20:
                    r = i % 2
                    j = (i - r - V20) * P
                    evac(at, i - r + 1, i, vr[:, r, j:j + 2 * P], acc[i % 4][:, 0:2 * P])
                elif X20 <= i < GR20:
                    b = i - X20
                    evac_conv = par2("conv_w", 3 * XB + b, 3 * XB + b + 1)
                    wait_used(act, at, i)
                    if b >= 2:
                        act.wait_ge(a_xs, at.n * XB + (b - 1))
                    nc.scalar.activation(cv[:, b % 2, :], acc[i % 4][:, 0:T], ACT.Identity, scale=evac_conv,
                                         bias=par2("conv_b", b, b + 1)).then_inc(a_cv, 1)
                    if b:
                        conv_silu(at, b - 1)
                    if b == XB - 1:
                        conv_silu(at, b)
                elif GR20 <= i < Z20:
                    b = i - GR20
                    if b >= 2:
                        act.wait_ge(v_flo, at.n * 16 + (b - 1))
                    evac(at, i, i, sg[:, b % 2, :], acc[i % 4][:, 0:T], ACT.Silu)
                elif Z20 <= i < RO_S:
                    b = i - Z20
                    act.wait_ge(v_flo, at.n * 16 + (b + 1))
                    evac(at, i, i, yr[:, b, :], acc[i % 4][:, 0:T], ACT.Silu)
                elif RO_S <= i < SO_S and (i - RO_S) % 3 == 0:
                    n = (i - RO_S) // 3
                    t = RO_T + 2 * n
                    if n >= 2:
                        wait_out(act, at, t - 3)
                    else:
                        act.wait_ge(v_flo, at.n * 16 + (15 + n))
                    evac(at, i, t, sg[:, n % 2, :], acc[t % 4][:, 0:T], ACT.Sigmoid)
                elif SO_S <= i < SO_S + KD:
                    n = i - SO_S
                    evac(at, i, SO_T + n, sgs[:, n, :], acc[(SO_T + n) % 4][:, 0:T], ACT.Sigmoid)
                elif WO_S < i:
                    square(at, True, 1, i - WO_S - 1)
                    gained(at, True, i - WO_S - 1)

            norm(Middle(), 0, last=True)
            act.dma_start(c2[:, :], c2_d).then_inc(consts2, 16)
            act.wait_ge(hf_ok, 4 * (DEPTH + 1))
            for b in range(KD):
                square(Layer(True, 0), True, 0, b)
            with act.Fori(0, DEPTH) as n:
                at = Layer(True, n)
                wait_x(act, at, True, 0, KD - 1)
                act.dma_start(p2[:, :], p2_d[bass.ds(n, 1)].rearrange("a p n -> p (a n)")).then_inc(params, 16)
                act.dma_start(rdec[:, :, :], decay_d).then_inc(decays, 16)
                norm(at, 0)
                act.wait_ge(params, n * 16 + (DEPTH * 16 + 16))
                nc.scalar.copy(wdt_hi[:, :, :], par2("w_dt").rearrange("p (k h) -> p k h", k=KD)).then_inc(a_dt, 1)
                for task in tasks2():
                    if task[0] == "slab":
                        second_slab(at, task[1])
                    elif task[0] == "ret_y":
                        ret_out(at, task[1])
                    elif task[0] == "ret_rs":
                        roots(at, 0, v_rm, 4)
                    elif task[0] == "dt_copy":
                        dt_copy(at)
                    elif task[0] == "dt_act":
                        dt(at)
                    elif task[0] == "dt_sums":
                        dt_sums(at)
                    elif task[0] == "pair":
                        pair(at, task[1])
                    elif task[0] == "z_sq":
                        z_square(at, task[1])
                    elif task[0] == "z_rs":
                        roots(at, 1, v_zm, 4)
                ffn(at, True)
            norm(Layer(True, DEPTH), 0, last=True)

        @block.vector
        def _(dve):
            tt, ts, stt = nc.vector.tensor_tensor, nc.vector.tensor_scalar, nc.vector.scalar_tensor_tensor
            copy = nc.vector.tensor_copy
            ADD, SUB, MUL, MAX, MIN = ALU.add, ALU.subtract, ALU.mult, ALU.max, ALU.min

            class Steps:

                def __init__(self, base):
                    self.base, self.n = base, 0
                    self.turned_back = self.scanned = None

                def next(self):
                    self.n += 1
                    return self.base + self.n

            def split(at, i):
                slot = i % RING
                dve.wait_ge(hi_done, at.slab + (i + 1))
                tt(w_lo[:, slot, 0:LO_V], w_raw[:, slot, 0:LO_V], w_hi[:, slot, 0:LO_V].bitcast(F32), SUB).then_inc(lo_v, 1)

            def gained(at, second, b):
                gain = (par2 if second else par1)("g_ffn", b, b + 1)
                wait_x(dve, at, second, 1, b)
                dve.wait_ge(gain_hi, at.split * KD + (b + 1))
                stt(g_lo[:, b, :], x[:, b, :], gain, g_hi[:, b, :].bitcast(F32), MUL, SUB).then_inc(gain_lo, 1)

            def root_of(at, which):
                step = (at.norm + which) * 3
                dve.wait_ge(root_ok, at.norm + (which + 1))
                stt(rtmp[:, :], mid[0][:, 0:T], EPS, rinv[:, :], ADD, MUL).then_inc(v_norm, 1)
                dve.wait_ge(v_norm, step + 1)
                stt(rtmp[:, :], rtmp[:, :], -0.5, rinv[:, :], MUL, MUL).then_inc(v_norm, 1)
                dve.wait_ge(v_norm, step + 2)
                stt(rinv[:, :], rtmp[:, :], 1.5, rinv[:, :], ADD, MUL).then_inc(v_norm, 1)

            def wait_root(at, which):
                dve.wait_ge(v_norm, (at.norm + which) * 3 + 3)

            def norm(at, gain, dst, last=False):
                root_of(at, 0)
                wait_root(at, 0)
                for j in range(4):
                    stt(dst[:, 2 * j, :], x[:, 2 * j, :], gain[:, 2 * j:2 * j + 1], rinv[:, :], MUL, MUL)
                    stt(dst[:, 2 * j + 1, :], x[:, 2 * j + 1, :], gain[:, 2 * j + 1:2 * j + 2], rinv[:, :], MUL, MUL).then_inc(hf_ok, 1)
                if last:
                    return
                for j in range(4):
                    dve.wait_ge(hhi_ok, at.split * 4 + (j + 1))
                    a = slice(2 * j, 2 * j + 2)
                    tt(h_lo[:, a, :], work[:, a, :], h_hi[:, a, :].bitcast(F32), SUB).then_inc(h_ok, 1)

            def ffn(at, second):
                si, ti, so, to = ffn_layout(second)
                gained(at, second, KD - 1)
                split(at, si + AHEAD)
                root_of(at, 1)
                with dve.Fori(0, FF // 2) as it:
                    now = Later(at, it, 4, 4, 2)
                    for b in range(2):
                        gate_slab, t = si + 2 * b, ti + 2 * b + 1
                        if b == 0:
                            wait_root(at, 1)
                        wait_used(dve, now, gate_slab)
                        wait_out(dve, now, t - 4)
                        tt(f_act[:, b, :], acc[(t - 1) % 4][:, 0:T], rinv[:, :], MUL).then_inc(v_gate, 1)
                        split(now, gate_slab + 1 + AHEAD)
                        wait_used(dve, now, gate_slab + 1)
                        wait_out(dve, now, t - 1)
                        tt(f_prod[:, b, :], f_act[:, b, :], acc[t % 4][:, 0:T], MUL).then_inc(out[t % 4], 1)
                        wait_out(dve, now, t)
                        tt(f_prod[:, b, :], f_prod[:, b, :], rinv[:, :], MUL).then_inc(v_prod, 1)
                        split(now, gate_slab + 2 + AHEAD)
                        dve.wait_ge(v_prod, now.ffn + (b + 1))
                        k = bass.ds(it * 2 + b, 1)
                        copy(f_hi[:, k, :], f_prod[:, b:b + 1, :]).then_inc(ff_hi, 1)
                        dve.wait_ge(ff_hi, now.ffn + (b + 1))
                        tt(f_lo[:, k, :], f_prod[:, b:b + 1, :], f_hi[:, k, :].bitcast(F32), SUB).then_inc(ff_lo, 1)
                for n in range(KD):
                    for m in range(3):
                        if n or m:
                            split(at, so + 3 * n + m + AHEAD)
                    wait_used(dve, at, so + 3 * n + 2)
                    tt(x[:, n, :], x[:, n, :], acc[(to + n) % 4][:, 0:T], ADD).then_inc(out[(to + n) % 4], 1)

            def prep(at, own):
                a_re, a_im = par1("a_re"), par1("a_im")
                dve.wait_ge(a_prep, at.n * 4 + 1)
                tt(tiny[:, 1, :], a_re, tiny[:, 0, :], MUL).then_inc(v_prep, 1)
                tt(tiny[:, 3, :], a_im, tiny[:, 0, :], MUL).then_inc(dve_step, 1)
                dve.wait_ge(dve_step, own.next())
                ts(tiny[:, 4, :], tiny[:, 3, :], 1.0 / TWO_PI, ROUND, MUL, ADD).then_inc(dve_step, 1)
                dve.wait_ge(dve_step, own.next())
                ts(tiny[:, 7, :], tiny[:, 4, :], -ROUND, None, ADD).then_inc(dve_step, 1)
                a = 3
                for part, b in ((TWO_PI_1, 8), (TWO_PI_2, 9), (TWO_PI_3, 10)):
                    dve.wait_ge(dve_step, own.next())
                    stt(tiny[:, b, :], tiny[:, 7, :], -part, tiny[:, a, :], MUL, ADD).then_inc(dve_step, 1)
                    a = b
                dve.wait_ge(dve_step, own.next())
                ts(tiny[:, 5, :], tiny[:, 10, :], PI_F, -PI_F, MIN, MAX).then_inc(dve_step, 1)
                dve.wait_ge(dve_step, own.next())
                stt(tiny[:, 6, :], tiny[:, 5, :], -1.0, tiny[:, 5, :], MUL, MIN).then_inc(v_prep, 1)

            def prep_c(at, own):
                a_re, a_im, r = par1("a_re"), par1("a_im"), tiny[:, 2, :]
                dve.wait_ge(a_prep, at.n * 4 + 4)
                tt(tiny[:, 11, :], r, turn[:, 0, :, 0], MUL)
                tt(tiny[:, 12, :], r, turn[:, 1, :, 0], MUL)
                tt(tiny[:, 13, :], a_re, a_re, MUL)
                tt(tiny[:, 14, :], a_im, a_im, MUL)
                nc.vector.memset(decay[:, :, 0:1], 0.0)
                copy(decay[:, :, 1:CH], r.unsqueeze(2).to_broadcast([P, PAIRS, CH - 1])).then_inc(dve_step, 1)
                dve.wait_ge(dve_step, own.next())
                ts(tiny[:, 15, :], tiny[:, 11, :], -1.0, None, ADD)
                tt(tiny[:, 16, :], tiny[:, 13, :], tiny[:, 14, :], ADD).then_inc(dve_step, 1)
                dve.wait_ge(dve_step, own.next())
                nc.vector.reciprocal(tiny[:, 17, :], tiny[:, 16, :])
                tt(tiny[:, 18, :], tiny[:, 15, :], a_re, MUL)
                tt(tiny[:, 19, :], tiny[:, 12, :], a_im, MUL)
                tt(tiny[:, 20, :], tiny[:, 12, :], a_re, MUL)
                tt(tiny[:, 21, :], tiny[:, 15, :], a_im, MUL).then_inc(dve_step, 1)
                dve.wait_ge(dve_step, own.next())
                tt(tiny[:, 22, :], tiny[:, 18, :], tiny[:, 19, :], ADD)
                tt(tiny[:, 23, :], tiny[:, 20, :], tiny[:, 21, :], SUB).then_inc(dve_step, 1)
                dve.wait_ge(dve_step, own.next())
                tt(tiny[:, 24, :], tiny[:, 22, :], tiny[:, 17, :], MUL)
                tt(tiny[:, 25, :], tiny[:, 23, :], tiny[:, 17, :], MUL).then_inc(dve_step, 1)
                dve.wait_ge(dve_step, own.next())
                c_re = par1("c_re").rearrange("p (a c) -> p a c", a=PAIRS)
                c_im = par1("c_im").rearrange("p (a c) -> p a c", a=PAIRS)
                f_re = tiny[:, 24, :].unsqueeze(2).to_broadcast([P, PAIRS, PC])
                f_im = tiny[:, 25, :].unsqueeze(2).to_broadcast([P, PAIRS, PC])
                t0 = tm[:, 0, 0:PAIRS * PC].rearrange("p (a c) -> p a c", a=PAIRS)
                t1 = tm[:, 1, 0:PAIRS * PC].rearrange("p (a c) -> p a c", a=PAIRS)
                tt(cab[:, 0, :, :], c_re, f_re, MUL)
                tt(t0, c_im, f_im, MUL)
                tt(cab[:, 1, :, :], c_re, f_im, MUL)
                tt(t1, c_im, f_re, MUL).then_inc(dve_step, 1)
                dve.wait_ge(dve_step, own.next())
                tt(cab[:, 0, :, :], cab[:, 0, :, :], t0, SUB)
                stt(cab[:, 1, :, :], cab[:, 1, :, :], -1.0, t1, MUL, SUB).then_inc(v_prep, 1)

            def double(at, own, k):
                n = 1 << k
                if k == 0:
                    dve.wait_ge(v_prep, at.n * 3 + 3)
                cos, sin = turn[:, 0, :, 0:n], turn[:, 1, :, 0:n]
                cos_n = turn[:, 0, :, n - 1:n].to_broadcast([P, PAIRS, n])
                sin_n = turn[:, 1, :, n - 1:n].to_broadcast([P, PAIRS, n])
                t0 = tm[:, 0, 0:PAIRS * n].rearrange("p (a c) -> p a c", a=PAIRS)
                t1 = tm[:, 1, 0:PAIRS * n].rearrange("p (a c) -> p a c", a=PAIRS)
                tt(turn[:, 0, :, n:2 * n], cos, cos_n, MUL)
                tt(t0, sin, sin_n, MUL)
                tt(turn[:, 1, :, n:2 * n], sin, cos_n, MUL)
                tt(t1, cos, sin_n, MUL).then_inc(dve_step, 1)
                dve.wait_ge(dve_step, own.next())
                tt(turn[:, 0, :, n:2 * n], turn[:, 0, :, n:2 * n], t0, SUB)
                tt(turn[:, 1, :, n:2 * n], turn[:, 1, :, n:2 * n], t1, ADD).then_inc(dve_step, 1)
                dve.wait_ge(dve_step, own.next())

            def carry_factors(at, own):
                tt(tiny[:, 26, :], tiny[:, 2, :], turn[:, 0, :, CH - 1], MUL)
                tt(tiny[:, 27, :], tiny[:, 2, :], turn[:, 1, :, CH - 1], MUL).then_inc(dve_step, 1)
                dve.wait_ge(dve_step, own.next())

            def rope(at, own, b):
                dve.wait_ge(pe_rope, at.n * 5 + (b + 1))
                tt(prob[:, b, 0:T], mid[ROPE_BANKS[b % 3]][:, 0:T], con1("rope_s"), MUL)
                tt(qk[:, b, :], qk[:, b, :], con1("rope_c"), MUL).then_inc(dve_step, 1)
                dve.wait_ge(dve_step, own.next())
                tt(qk[:, b, :], qk[:, b, :], prob[:, b, 0:T], ADD).then_inc(v_rope, 1)

            def rot(at, own, c, j):
                q = bu_order(c)[j]
                dve.wait_ge(pe_bu, at.n * 16 + (4 * c + j + 1))
                bu = mid[q][:, :].rearrange("p (r b c) -> p r b c", r=2, b=N1)
                cos, sin = (turn[:, part, :, :].rearrange("p (b q) c -> p b q c", q=4)[:, :, q, :].unsqueeze(1)
                            .to_broadcast([P, 2, N1, CH]) for part in range(2))
                z = zs[:, :, :, :].rearrange("p r (b q) c -> p r b q c", q=4)[:, :, :, q, :]
                t = tm[:, :, :].rearrange("p r (b q c) -> p r b q c", q=4, c=CH)[:, :, :, q, :]
                tt(z, bu, cos, MUL)
                tt(t, bu, sin, MUL).then_inc(v_rot, 1)
                if j < 3:
                    return
                dve.wait_ge(v_rot, at.n * 16 + (4 * c + 4))
                flat = [zs[:, part, :, :].rearrange("p a c -> p (a c)") for part in range(2)]
                tt(flat[0], flat[0], tm[:, 1, :], ADD)
                tt(flat[1], flat[1], tm[:, 0, :], SUB).then_inc(dve_step, 1)
                own.turned_back = own.next()

            def scan(at, own, c):
                dve.wait_ge(dve_step, own.turned_back)
                if c:
                    tt(zs[:, 0, :, 0], zs[:, 0, :, 0], tiny[:, 28, :], ADD)
                    tt(zs[:, 1, :, 0], zs[:, 1, :, 0], tiny[:, 29, :], ADD).then_inc(dve_step, 1)
                    dve.wait_ge(dve_step, own.next())
                flat = decay[:, :, :].rearrange("p a c -> p (a c)")
                for part in range(2):
                    z = zs[:, part, :, :].rearrange("p a c -> p (a c)")
                    last = nc.vector.tensor_tensor_scan(z, flat, z, 0.0, MUL, ADD)
                last.then_inc(dve_step, 1)
                own.scanned = own.next()
                if c == NCH - 1:
                    return
                dve.wait_ge(dve_step, own.scanned)
                z_re, z_im = zs[:, 0, :, CH - 1], zs[:, 1, :, CH - 1]
                tt(tiny[:, 28, :], z_re, tiny[:, 26, :], MUL)
                tt(tiny[:, 30, :], z_im, tiny[:, 27, :], MUL)
                tt(tiny[:, 29, :], z_im, tiny[:, 26, :], MUL)
                tt(tiny[:, 31, :], z_re, tiny[:, 27, :], MUL).then_inc(dve_step, 1)
                dve.wait_ge(dve_step, own.next())
                tt(tiny[:, 28, :], tiny[:, 28, :], tiny[:, 30, :], SUB)
                tt(tiny[:, 29, :], tiny[:, 29, :], tiny[:, 31, :], ADD).then_inc(dve_step, 1)
                own.scanned = own.next()

            def turn_states(at, own, c):
                dve.wait_ge(dve_step, own.scanned)
                if c:
                    dve.wait_ge(pe_y, at.n * 4 + c)
                cos, sin = turn[:, 0, :, :], turn[:, 1, :, :]
                t0 = tm[:, 0, :].rearrange("p (a c) -> p a c", a=PAIRS)
                t1 = tm[:, 1, :].rearrange("p (a c) -> p a c", a=PAIRS)
                tt(xst[:, 0, :, :], zs[:, 0, :, :], cos, MUL)
                tt(t0, zs[:, 1, :, :], sin, MUL)
                tt(xst[:, 1, :, :], zs[:, 1, :, :], cos, MUL)
                tt(t1, zs[:, 0, :, :], sin, MUL).then_inc(dve_step, 1)
                dve.wait_ge(dve_step, own.next())
                tt(xst[:, 0, :, :], xst[:, 0, :, :], t0, SUB)
                tt(xst[:, 1, :, :], xst[:, 1, :, :], t1, ADD).then_inc(v_x, 1)
                dve.wait_ge(v_x, at.n * 4 + (c + 1))

            def ssm_y(at, c):
                dve.wait_ge(pe_y, at.n * 4 + (c + 1))
                tokens = slice(c * CH, c * CH + CH)
                for blk in range(N1):
                    last = stt(u[:, blk, tokens], u[:, blk, tokens], par1("d", blk, blk + 1),
                               mid[3][:, blk * CH:(blk + 1) * CH], MUL, ADD)
                last.then_inc(v_y, 1)

            def scores(at, h):
                dve.wait_ge(pe_s, at.n * 8 + (h + 1))
                stt(prob[:, h, :], mid[SCORE_BANKS[h % 3]][:, 0:TRI], HD ** -0.5, con1("mask"), MUL, ADD).then_inc(v_mask, 1)

            def maxima(at, own):
                sink = par1("sink")
                dve.wait_ge(v_mask, at.n * 8 + 8)
                nc.vector.tensor_reduce(soft[:, 0, 0, :], prob[:, :, 0:P], AX_X, MAX)
                nc.vector.tensor_reduce(soft[:, 0, 1, :], prob[:, :, P:TRI], AX_X, MAX).then_inc(dve_step, 1)
                dve.wait_ge(dve_step, own.next())
                sinks = sink.unsqueeze(1).to_broadcast([P, 2, HEADS])
                tt(soft[:, 1, :, :], soft[:, 0, :, :], sinks, MAX).then_inc(dve_step, 1)
                dve.wait_ge(dve_step, own.next())
                ts(soft[:, 3, :, :], soft[:, 1, :, :], -1.0, None, MUL)
                tt(soft[:, 4, :, :], sinks, soft[:, 1, :, :], SUB).then_inc(v_max, 1)

            def normalize(at, own):
                dve.wait_ge(a_exp, at.n + 1)
                tt(soft[:, 7, :, :], soft[:, 6, :, :], soft[:, 5, :, :], ADD).then_inc(dve_step, 1)
                dve.wait_ge(dve_step, own.next())
                nc.vector.reciprocal(soft[:, 8, :, :], soft[:, 7, :, :]).then_inc(dve_step, 1)
                dve.wait_ge(dve_step, own.next())
                for r, (a, b) in enumerate(((0, P), (P, TRI))):
                    last = tt(prob[:, :, a:b], prob[:, :, a:b],
                              soft[:, 8, r, :].unsqueeze(2).to_broadcast([P, HEADS, b - a]), MUL)
                last.then_inc(v_p, 1)

            def attended(at, a):
                dve.wait_ge(a_ohi, at.n * 4 + (a + 1))
                tt(o_lo[:, a, :], mid[0][:, 0:T], o_hi[:, a, :].bitcast(F32), SUB).then_inc(v_olo, 1)

            def gelu(at):
                dve.wait_ge(a_gelu, at.n * 2 + 2)
                tt(ys_lo[:, :, :], ysg[:, :, :], ys_hi[:, :, :].bitcast(F32), SUB).then_inc(v_yslo, 1)

            def conv_lo(at, b):
                dve.wait_ge(a_chi, at.n * 4 + (b + 1))
                tt(cv_lo[:, b, :], cy[:, b % 2, :], cv_hi[:, b, :].bitcast(F32), SUB).then_inc(v_clo, 1)

            def first_slab(at, own, i):
                split(at, i + AHEAD)
                bank = acc[i % 4]
                if C0 <= i < G0:
                    b, part = (i - C0) // 3, (i - C0) % 3
                    if part == 1:
                        if b:
                            conv_lo(at, b - 1)
                        wait_used(dve, at, i)
                        wait_out(dve, at, i - 1)
                        y = ccx[:, b % 2, :]
                        tt(zpad[:, 8:8 + T], bank[:, 0:T], y, MUL).then_inc(out[i % 4], 1)
                        wait_out(dve, at, i)
                        w = [par1("conv_w", j * N1 + b, j * N1 + b + 1) for j in range(3)]
                        ts(y, zpad[:, 8:8 + T], w[2], None, MUL).then_inc(dve_step, 1)
                        dve.wait_ge(dve_step, own.next())
                        stt(y, zpad[:, 7:7 + T], w[1], y, MUL, ADD).then_inc(dve_step, 1)
                        dve.wait_ge(dve_step, own.next())
                        stt(y, zpad[:, 6:6 + T], w[0], y, MUL, ADD).then_inc(dve_step, 1)
                        dve.wait_ge(dve_step, own.next())
                    elif part == 2:
                        wait_used(dve, at, i)
                        tt(cy[:, b % 2, :], ccx[:, b % 2, :], bank[:, 0:T], MUL).then_inc(out[i % 4], 1)
                elif i == G0:
                    conv_lo(at, N1 - 1)
                elif CO0 <= i < AO0:
                    n = i - CO0
                    wait_used(dve, at, i)
                    if n == 0:
                        dve.wait_ge(dve_step, own.scanned)
                        for t in range(CO0 - 4, CO0):
                            wait_out(dve, at, t)
                    tt(work[:, 2 * n:2 * n + 2, :], gate[:, 8 + 2 * n:10 + 2 * n, :],
                       bank[:, :].rearrange("p (b t) -> p b t", b=2), MUL).then_inc(out[i % 4], 1)
                elif AO0 <= i < GL0 or SO0 <= i < MX0:
                    n, g = (i - AO0, 0) if i < GL0 else (i - SO0, 16)
                    mine = slice(2 * n, 2 * n + 2)
                    wait_used(dve, at, i)
                    add = branch[:, n % 2, :].rearrange("p (b t) -> p b t", b=2)
                    tt(add, gate[:, g + 2 * n:g + 2 * n + 2, :], bank[:, :].rearrange("p (b t) -> p b t", b=2),
                       MUL).then_inc(out[i % 4], 1)
                    wait_out(dve, at, i)
                    if g == 0:
                        wait_out(dve, at, CO0 + n)
                        tt(work[:, mine, :], work[:, mine, :], add, ADD).then_inc(dve_step, 1)
                        dve.wait_ge(dve_step, own.next())
                    else:
                        tt(work[:, mine, :], work[:, mine, :], add, ADD).then_inc(v_mg, 1)
                        dve.wait_ge(a_mhi, at.n * 4 + (n + 1))
                        tt(h_lo[:, mine, :], work[:, mine, :], h_hi[:, mine, :].bitcast(F32), SUB).then_inc(v_mlo, 1)
                elif GL0 <= i < SO0:
                    n = i - GL0
                    mine = slice(2 * n, 2 * n + 2)
                    wait_out(dve, at, i)
                    tt(yv[:, mine, :], ysg[:, mine, :], glu[:, n, :].rearrange("p (b t) -> p b t", b=2), MUL).then_inc(v_yv, 1)
                    dve.wait_ge(a_yvhi, at.n * 2 + (n + 1))
                    tt(yv_lo[:, mine, :], yv[:, mine, :], yv_hi[:, mine, :].bitcast(F32), SUB).then_inc(v_yvlo, 1)
                elif MX0 <= i:
                    wait_used(dve, at, i)
                    tt(x[:, i - MX0, :], x[:, i - MX0, :], bank[:, 0:T], ADD).then_inc(out[i % 4], 1)
                    if i > MX0:
                        gained(at, False, i - MX0 - 1)

            dve.wait_ge(consts, 32)
            start = Layer(False, 0)
            for slot in range(AHEAD):
                split(start, slot)
            dve.wait_ge(pad_ok, 1)
            with dve.Fori(0, DEPTH) as n:
                at, own = Layer(False, n), Steps(n * V_STEPS1)
                dve.wait_ge(params, n * 16 + 16)
                norm(at, par1("g_mix"), work)
                for task in tasks1():
                    if task[0] == "slab":
                        first_slab(at, own, task[1])
                    elif task[0] == "prep":
                        prep(at, own)
                    elif task[0] == "prep_c":
                        prep_c(at, own)
                    elif task[0] == "double":
                        double(at, own, task[1])
                    elif task[0] == "carry":
                        carry_factors(at, own)
                    elif task[0] == "rope_mul":
                        rope(at, own, task[1])
                    elif task[0] == "rot":
                        rot(at, own, task[1], task[2])
                    elif task[0] == "turn":
                        turn_states(at, own, task[1])
                    elif task[0] == "scan":
                        scan(at, own, task[1])
                    elif task[0] == "ssm_y":
                        ssm_y(at, task[1])
                    elif task[0] == "mask":
                        scores(at, task[1])
                    elif task[0] == "maxima":
                        maxima(at, own)
                    elif task[0] == "normalize":
                        normalize(at, own)
                    elif task[0] == "gelu_lo":
                        gelu(at)
                    elif task[0] == "pv_lo":
                        attended(at, task[1])
                ffn(at, False)
                assert own.n == V_STEPS1, own.n

            norm(Middle(), con1("g_mid"), x, last=True)
            dve.wait_ge(consts2, 16)
            copy(unit[:, :], con1("ident"))
            tt(sel[0:2 * SH, :], con1("ident")[0:2 * SH, 0:SH], con1("ident")[0:2 * SH, SH:2 * SH], ADD)
            ts(above[:, :], con2("tri")[:, 0:P], -1.0, 1e30, ADD, MUL).then_inc(v_above, 1)

            def turned(at, own, i):
                dst = qt if i < K20 else kt
                h = (i - (0 if i < K20 else K20)) // 2
                wait_used(dve, at, i)
                first, second = acc[(i - 1) % 4][:, 0:T], acc[i % 4][:, 0:T]
                t0, t1 = rp[:, 0, 0:T], rp[:, 1, 0:T]
                tt(dst[:, 2 * h, :], first, con2("cos"), MUL)
                tt(t0, second, con2("sin"), MUL)
                tt(dst[:, 2 * h + 1, :], first, con2("sin"), MUL).then_inc(out[(i - 1) % 4], 1)
                tt(t1, second, con2("cos"), MUL).then_inc(out[i % 4], 1)
                wait_out(dve, at, i)
                tt(dst[:, 2 * h, :], dst[:, 2 * h, :], t0, SUB)
                tt(dst[:, 2 * h + 1, :], dst[:, 2 * h + 1, :], t1, ADD).then_inc(v_qk, 1)
                dve.wait_ge(v_qk, at.n * 8 + (i // 2 + 1))

            def conv(at, own, i):
                b = i - X20
                bank, y = acc[i % 4], cv[:, b % 2, :]
                dve.wait_ge(a_cv, at.n * XB + (b + 1))
                for j in (1, 2, 3):
                    w = par2("conv_w", (3 - j) * XB + b, (3 - j) * XB + b + 1)
                    op = stt(y[:, j:T], bank[:, 0:T - j], w, y[:, j:T], MUL, ADD)
                    if j < 3:
                        op.then_inc(dve_step2, 1)
                        dve.wait_ge(dve_step2, own.next())
                op.then_inc(out[i % 4], 1)

            def dt(at, own):
                dve.wait_ge(pe_dt, at.n * 3 + 2)
                tt(dts[:, 0, :, :], mid[0][:, 0:2 * SH].rearrange("p (r h) -> p r h", r=2),
                   par2("dt_b").unsqueeze(1).to_broadcast([P, 2, SH]), ADD).then_inc(dve_step2, 1)
                dve.wait_ge(dve_step2, own.next())
                stt(dts[:, 1, :, :], dts[:, 0, :, :], -1.0, dts[:, 0, :, :], MUL, MAX).then_inc(v_dt, 1)
                dve.wait_ge(a_dt, at.n * 5 + 4)
                e, s, s2, q = (dts[:, k, :, :] for k in (2, 3, 4, 5))
                ts(s, e, 2.0, None, ADD).then_inc(dve_step2, 1)
                dve.wait_ge(dve_step2, own.next())
                nc.vector.reciprocal(s2, s).then_inc(dve_step2, 1)
                dve.wait_ge(dve_step2, own.next())
                tt(s, e, s2, MUL).then_inc(dve_step2, 1)
                dve.wait_ge(dve_step2, own.next())
                tt(s2, s, s, MUL).then_inc(dve_step2, 1)
                dve.wait_ge(dve_step2, own.next())
                ts(q, s2, 1.0 / 17, None, MUL).then_inc(dve_step2, 1)
                for k in range(15, 1, -2):
                    dve.wait_ge(dve_step2, own.next())
                    stt(q, q, 1.0 / k, s2, ADD, MUL).then_inc(dve_step2, 1)
                dve.wait_ge(dve_step2, own.next())
                stt(q, q, 1.0, s, ADD, MUL).then_inc(dve_step2, 1)
                dve.wait_ge(dve_step2, own.next())
                tt(q, q, q, ADD).then_inc(dve_step2, 1)
                dve.wait_ge(dve_step2, own.next())
                stt(dts[:, 6, :, :], dts[:, 0, :, :], 0.0, q, MAX, ADD).then_inc(dve_step2, 1)
                dve.wait_ge(dve_step2, own.next())
                stt(dts[:, 8, :, :], dts[:, 6, :, :], -1.0, dts[:, 7, 0, :].unsqueeze(1).to_broadcast([P, 2, SH]),
                    MUL, MUL).then_inc(v_dt, 1)

            def dt_sums(at):
                dve.wait_ge(pe_dt, at.n * 3 + 3)
                dve.wait_ge(a_dt, at.n * 5 + 5)
                ts(dts[:, 9, :, :], mid[0][:, 2 * SH:4 * SH].rearrange("p (r h) -> p r h", r=2), -1.0, None, MUL)
                lo = sums[SH:2 * SH, :]
                tt(lo[:, 0:T], mid[0][SH:2 * SH, P:P + T], lo[:, 0:T].bitcast(F32), SUB)
                tt(lo[:, T:TRI], mid[0][SH:2 * SH, T:P + T], lo[:, T:TRI].bitcast(F32), SUB).then_inc(v_dt, 1)

            def ret_scores(at, h):
                dve.wait_ge(pe_rs, at.n * 4 + (h + 1))
                if h == 0:
                    dve.wait_ge(decays, at.n * 16 + 16)
                elif h >= 2:
                    dve.wait_ge(pe_ry, at.n * 4 + (h - 1))
                tt(rp[:, h % 2, :], mid[2][:, 0:TRI], rdec[:, h, :], MUL).then_inc(v_rp, 1)

            def roots(at, own, which):
                dve.wait_ge(a_root2, at.n * 2 + (which + 1))
                tt(nt[:, :, :], ms[:, :, :], rr[:, :, :], MUL).then_inc(dve_step2, 1)
                dve.wait_ge(dve_step2, own.next())
                stt(nt[:, :, :], nt[:, :, :], -0.5, rr[:, :, :], MUL, MUL).then_inc(dve_step2, 1)
                dve.wait_ge(dve_step2, own.next())
                stt(rr[:, :, :], nt[:, :, :], 1.5, rr[:, :, :], ADD, MUL).then_inc(dve_step2, 1)
                dve.wait_ge(dve_step2, own.next())

            def turned_xs(at, m):
                dve.wait_ge(pe_xt, at.n * 8 + (m + 1))
                for b in range(2):
                    blk = 2 * m + b
                    last = tt(xdt[:, :, blk * P:(blk + 1) * P].rearrange("p r (h c) -> p r h c", h=2),
                              mid[1 + m % 2][:, b * T:(b + 1) * T].rearrange("p (r h c) -> p r h c", r=2, h=2),
                              dts[:, 6, :, 2 * blk:2 * blk + 2].unsqueeze(3).to_broadcast([P, 2, 2, SP_]), MUL)
                last.then_inc(v_xdt, 1)

            def c_times_b(at, g):
                dve.wait_ge(pe_cb, at.n * 4 + (g + 1))
                copy(cbm[:, g, :], mid[0][:, 0:TRI]).then_inc(v_cb, 1)

            def pair(at, b):
                dve.wait_ge(a_l, at.n * 16 + (b + 1))
                if b:
                    dve.wait_ge(pe_y2, at.n * 16 + b)
                else:
                    dve.wait_ge(v_cb, at.n * 4 + 4)
                tt(mt[:, :, :], lseg[:, :, :], cbm[:, b // 4, :].unsqueeze(1).to_broadcast([P, 2, TRI]), MUL).then_inc(v_m, 1)

            def pair_y(at, b):
                dve.wait_ge(pe_y2, at.n * 16 + (b + 1))
                stt(xs[:, b, :], xs[:, b, :], par2("d_skip", b, b + 1), mid[2 + b % 2][:, 0:T],
                    MUL, ADD).then_inc(v_ys, 1)

            def z_mul(at, b):
                wait_out(dve, at, Z20 + b)
                dve.wait_ge(v_ys, at.n * 16 + (b + 1))
                tt(xs[:, b, :], xs[:, b, :], yr[:, b, :], MUL).then_inc(v_z, 1)

            def z_norm(at, own, m):
                both = slice(2 * m, 2 * m + 2)
                if m:
                    dve.wait_ge(v_slo, at.n * 8 + m)
                for b in range(2):
                    blk = 2 * m + b
                    last = stt(pr[:, b, :], xs[:, blk, :], par2("norm", blk, blk + 1), rr[:, blk // 4, :], MUL, MUL)
                last.then_inc(dve_step2, 1)
                dve.wait_ge(dve_step2, own.next())
                copy(s_hi[:, both, :], pr[:, :, :]).then_inc(dve_step2, 1)
                dve.wait_ge(dve_step2, own.next())
                tt(s_lo[:, both, :], pr[:, :, :], s_hi[:, both, :].bitcast(F32), SUB).then_inc(v_slo, 1)

            def second_slab(at, own, i):
                split(at, i + AHEAD)
                bank = acc[i % 4]
                if i < V20:
                    if i % 2:
                        turned(at, own, i)
                elif X20 <= i < GR20:
                    conv(at, own, i)
                elif GR20 <= i < Z20:
                    b = i - GR20
                    y = pr[:, b % 2, :]
                    wait_out(dve, at, i)
                    tt(y, sg[:, b % 2, :], yr[:, b, :], MUL).then_inc(dve_step2, 1)
                    dve.wait_ge(dve_step2, own.next())
                    tt(y, y, rr[:, b // 4, :], MUL).then_inc(dve_step2, 1)
                    dve.wait_ge(dve_step2, own.next())
                    copy(r_hi[:, b, :], y).then_inc(dve_step2, 1)
                    dve.wait_ge(dve_step2, own.next())
                    tt(r_lo[:, b, :], y, r_hi[:, b, :].bitcast(F32), SUB).then_inc(v_flo, 1)
                elif RO_S <= i < SO_S:
                    n, part = (i - RO_S) // 3, (i - RO_S) % 3
                    if part == 2:
                        t = RO_T + 2 * n + 1
                        wait_used(dve, at, i)
                        wait_out(dve, at, t - 1)
                        tt(work[:, n, :], acc[t % 4][:, 0:T], sg[:, n % 2, :], MUL).then_inc(out[t % 4], 1)
                elif SO_S + KD <= i < WO_S:
                    n, part = (i - SO_S - KD) // 2, (i - SO_S) % 2
                    if part == 1:
                        t = SO_T + KD + n
                        y = pr[:, n % 2, :]
                        wait_used(dve, at, i)
                        wait_out(dve, at, SO_T + n)
                        tt(y, acc[t % 4][:, 0:T], sgs[:, n, :], MUL).then_inc(out[t % 4], 1)
                        wait_out(dve, at, t)
                        wait_out(dve, at, RO_T + 2 * n + 1)
                        tt(work[:, n, :], work[:, n, :], y, ADD).then_inc(dve_step2, 1)
                        dve.wait_ge(dve_step2, own.next())
                        copy(m_hi[:, n, :], work[:, n, :]).then_inc(dve_step2, 1)
                        dve.wait_ge(dve_step2, own.next())
                        tt(m_lo[:, n, :], work[:, n, :], m_hi[:, n, :].bitcast(F32), SUB).then_inc(v_mlo2, 1)
                elif WO_S <= i:
                    t = WO_T + i - WO_S
                    wait_used(dve, at, i)
                    tt(x[:, i - WO_S, :], x[:, i - WO_S, :], acc[t % 4][:, 0:T], ADD).then_inc(out[t % 4], 1)
                    if i > WO_S:
                        gained(at, True, i - WO_S - 1)

            with dve.Fori(0, DEPTH) as n:
                at, own = Layer(True, n), Steps(n * V_STEPS2)
                dve.wait_ge(params, n * 16 + (DEPTH * 16 + 16))
                norm(at, par2("g_mix"), work)
                dve.wait_ge(a_dt, at.n * 5 + 1)
                tt(wdt_lo[:, :, :], par2("w_dt").rearrange("p (k h) -> p k h", k=KD), wdt_hi[:, :, :].bitcast(F32),
                   SUB).then_inc(v_dt, 1)
                for task in tasks2():
                    if task[0] == "slab":
                        second_slab(at, own, task[1])
                    elif task[0] == "ret_s":
                        ret_scores(at, task[1])
                    elif task[0] == "ret_m":
                        dve.wait_ge(pe_rm, at.n * 4 + (task[1] + 1))
                        ts(ms[:, task[1], :], mid[3][:, 0:T], EPS, None, ADD).then_inc(v_rm, 1)
                    elif task[0] == "ret_rs":
                        roots(at, own, 0)
                    elif task[0] == "softplus":
                        dt(at, own)
                    elif task[0] == "dt_sums":
                        dt_sums(at)
                    elif task[0] == "xdt":
                        turned_xs(at, task[1])
                    elif task[0] == "cb":
                        c_times_b(at, task[1])
                    elif task[0] == "pair":
                        pair(at, task[1])
                    elif task[0] == "pair_y":
                        pair_y(at, task[1])
                    elif task[0] == "z_m":
                        dve.wait_ge(pe_zm, at.n * 4 + (task[1] + 1))
                        ts(ms[:, task[1], :], mid[3][:, 0:T], EPS, None, ADD).then_inc(v_zm, 1)
                    elif task[0] == "z_rs":
                        roots(at, own, 1)
                    elif task[0] == "z_mul":
                        z_mul(at, task[1])
                    elif task[0] == "z_norm":
                        z_norm(at, own, task[1])
                ffn(at, True)
                assert own.n == V_STEPS2, own.n
            norm(Layer(True, DEPTH), con1("g_final"), work, last=True)


def kernel(x, norm_mix, w_in, b_gate, attn_sinks, w_attn_o, conv_w, w_conv_o, ssm_a_re, ssm_a_im, ssm_b_re, ssm_b_im,
           ssm_c_re, ssm_c_im, ssm_d, ssm_log_dt, w_ssm_glu, w_ssm_o, w_mix_o, norm_ffn, w_ffn_in, w_ffn_out,
           norm_final, norm_mix_w_2, w_in_2, ret_out_2, conv_w_2, conv_b_2, dt_bias_2, a_log_2, d_skip_2, ssd_norm_w_2,
           ssd_out_2, w_o_2, norm_ffn_w_2, w_gate_up_2, w_down_2, final_norm_w_2):
    import numpy as np
    import concourse.bacc as bacc
    from concourse.bass_utils import run_bass_kernel_spmd

    arr = np.asarray
    f32 = np.float32

    def blocks(w, width=P):
        k, n = w.shape
        return w.reshape(k // P, P, n // width, width).transpose(2, 1, 0, 3)

    def columns(v):
        return v.reshape(-1, P).T

    def every(v):
        return np.broadcast_to(v, (P, v.size))

    def slabs8(w):
        return blocks(w).reshape(-1, P, SLAB)

    def slabs4(w):
        return blocks(w, 2 * P).reshape(-1, P, SLAB)

    def long_slabs(w):
        b = blocks(w)
        n, _, k, _ = b.shape
        m = -(-k // KD)
        full = np.zeros((n, P, m * KD, P), f32)
        full[:, :, :k] = b
        return full.reshape(n, P, m, SLAB).transpose(0, 2, 1, 3)

    head_order = np.arange(HEADS).reshape(2, HEADS // 2).T.reshape(-1)
    by_head = (head_order[:, None] * HD + np.arange(HD)).reshape(-1)

    stream = np.zeros((TOTAL + RING, P, SLAB), f32)
    p1_d = np.zeros((DEPTH, P, P1_N), f32)
    p2_d = np.zeros((DEPTH, P, P2_N), f32)
    at = 0

    def push(part):
        nonlocal at
        part = part.reshape(-1, P, SLAB)
        stream[at:at + len(part)] = part
        at += len(part)

    def interleave(*parts):
        parts = [p.reshape(p.shape[0], -1, P, SLAB) for p in parts]
        return np.concatenate(parts, axis=1)

    for n in range(DEPTH):
        q, k, v, cb, cc, cx, u, g = np.split(arr(w_in)[n], np.cumsum([512, 128, 128, 512, 512, 512, 512]), axis=1)
        push(slabs8(u))
        push(slabs8(q[:, by_head]))
        push(slabs8(k))
        push(slabs8(v))
        push(interleave(slabs8(cc), slabs8(cx), slabs8(cb)))
        push(slabs8(g))
        push(slabs4(arr(w_conv_o)[n]))
        push(slabs4(arr(w_attn_o)[n][by_head]))
        push(slabs4(arr(w_ssm_glu)[n]))
        push(slabs4(arr(w_ssm_o)[n]))
        push(slabs8(arr(w_mix_o)[n]))
        fi = arr(w_ffn_in)[n]
        push(interleave(slabs8(fi[:, :FF * P]), slabs8(fi[:, FF * P:])))
        push(long_slabs(arr(w_ffn_out)[n]))
        assert at == (n + 1) * S1

        p = p1_d[n]

        def put(name, value):
            lo, hi = P1[name]
            p[:, lo:hi] = value

        put("g_mix", columns(arr(norm_mix)[n]))
        put("g_ffn", columns(arr(norm_ffn)[n]))
        put("b_gate", columns(arr(b_gate)[n]))
        put("conv_w", columns(arr(conv_w)[n].reshape(-1)))
        put("d", columns(arr(ssm_d)[n]))
        put("sink", every(arr(attn_sinks)[n][head_order]))
        put("a_re", arr(ssm_a_re)[n].reshape(PAIRS, P).T)
        put("a_im", arr(ssm_a_im)[n].reshape(PAIRS, P).T)
        put("log_dt", np.repeat(arr(ssm_log_dt)[n].reshape(PAIRS, 2), 64, axis=1).T)
        for name, b in (("b_re", ssm_b_re), ("b_im", ssm_b_im)):
            b = arr(b)[n].reshape(N1, 4, 2, 64, 16)
            full = np.zeros((4, 2, 16, N1, 2, 64), f32)
            for a in range(2):
                full[:, a, :, :, a, :] = b[:, :, a].transpose(1, 3, 0, 2)
            put(name, full.reshape(P, N1 * P))
        for name, c in (("c_re", ssm_c_re), ("c_im", ssm_c_im)):
            c = arr(c)[n].reshape(PAIRS, 2, 16, 64)
            full = np.zeros((2, 64, PAIRS, 2, 16), f32)
            for a in range(2):
                full[a, :, :, a, :] = c[:, a].transpose(2, 0, 1)
            put(name, full.reshape(P, PAIRS * PC))

    for n in range(DEPTH):
        w = arr(w_in_2)[n]
        q, k, v, g, z, xbc, dt, gate_ret, gate_ssd = np.split(
            w, np.cumsum([1024, 1024, 2048, 2048, 2048, 3072, SH, 1024]), axis=1)
        for part in (q, k, v, xbc, g, z):
            push(slabs8(part))
        push(interleave(slabs8(gate_ret), long_slabs(arr(ret_out_2)[n])))
        push(slabs8(gate_ssd))
        push(long_slabs(arr(ssd_out_2)[n]))
        push(slabs8(arr(w_o_2)[n]))
        gu = arr(w_gate_up_2)[n]
        push(interleave(slabs8(gu[:, :FF * P]), slabs8(gu[:, FF * P:])))
        push(long_slabs(arr(w_down_2)[n]))
        assert at == DEPTH * S1 + (n + 1) * S2

        p = p2_d[n]

        def put2(name, value):
            lo, hi = P2[name]
            p[:, lo:hi] = value

        put2("g_mix", columns(arr(norm_mix_w_2)[n]))
        put2("g_ffn", columns(arr(norm_ffn_w_2)[n]))
        put2("conv_w", columns(arr(conv_w_2)[n].reshape(-1)))
        put2("conv_b", columns(arr(conv_b_2)[n]))
        put2("dt_b", every(arr(dt_bias_2)[n]))
        put2("a_log", every(arr(a_log_2)[n]))
        put2("d_skip", columns(np.repeat(arr(d_skip_2)[n], SP_)))
        put2("norm", columns(arr(ssd_norm_w_2)[n]))
        put2("w_dt", blocks(dt, SH)[0].reshape(P, KD * SH))

    c1_d = np.zeros((P, C1_N), f32)

    def put_c1(name, value):
        lo, hi = C1[name]
        c1_d[:, lo:hi] = value

    put_c1("ones_d", 1.0 / D)
    put_c1("ones_i", 1.0 / 512)
    put_c1("ident", np.eye(P))
    put_c1("g_mid", columns(arr(norm_final)))
    put_c1("g_final", columns(arr(final_norm_w_2)))
    pos = np.arange(T, dtype=f32)
    half = ROT // 2
    inv = (f32(500000.0) ** (-np.arange(0, ROT, 2, dtype=f32) / f32(ROT))).astype(f32)
    ang = (pos[:, None] * inv).astype(f32)
    rope_c, rope_s = np.ones((HD, T), f32), np.zeros((HD, T), f32)
    rope_c[:ROT] = np.tile(np.cos(ang).T, (2, 1))
    rope_s[:ROT] = np.tile(np.sin(ang).T, (2, 1))
    put_c1("rope_c", np.tile(rope_c, (2, 1)))
    put_c1("rope_s", np.tile(rope_s, (2, 1)))
    turn = np.zeros((P, P), f32)
    for base in (0, HD):
        for m in range(half):
            turn[base + m + half, base + m] = -1.0
            turn[base + m, base + m + half] = 1.0
    put_c1("rope_r", turn)
    i, j = np.arange(P)[:, None], np.arange(P)[None]
    put_c1("mask", np.where(np.concatenate([j <= i, j > i, j <= i], axis=1), 0.0, -1e30))

    c2_d = np.zeros((P, C2_N), f32)
    inv = (f32(10000.0) ** (-np.arange(P, dtype=f32) / f32(P))).astype(f32)
    ang = (pos[:, None] * inv).astype(f32)
    tri = np.concatenate([i <= j, np.ones((P, P), bool), i <= j], axis=1)
    c2_d[:, C2["cos"][0]:C2["cos"][1]] = np.cos(ang).T
    c2_d[:, C2["sin"][0]:C2["sin"][1]] = np.sin(ang).T
    c2_d[:, C2["tri"][0]:C2["tri"][1]] = tri
    gap = np.concatenate([j - i, j + P - i, j - i], axis=1)
    log_g = np.log(1.0 - 2.0 ** (-5.0 - np.arange(RH)))
    decay_d = np.where(tri[:, None, :], np.exp(log_g[None, :, None] * np.maximum(gap, 0)[:, None, :]), 0.0)
    decay_d = np.ascontiguousarray((decay_d * 256.0 ** -0.5).astype(f32))

    ins = {"weights_d": stream, "x_d": np.ascontiguousarray(arr(x)[0].T), "p1_d": p1_d, "p2_d": p2_d,
           "c1_d": c1_d, "c2_d": c2_d, "decay_d": decay_d}
    nc = bacc.Bacc("TRN2", target_bir_lowering=False, num_devices=1)
    args = [nc.dram_tensor(name, a.shape, mybir.dt.from_np(a.dtype), kind="ExternalInput").ap() for name, a in ins.items()]
    args.append(nc.dram_tensor("out_d", (D, T), F32, kind="ExternalOutput").ap())
    hybrid_kernel(nc, *args)
    result = run_bass_kernel_spmd(nc, [ins], core_ids=[0])
    return np.ascontiguousarray(result.results[0]["out_d"].T)[None]
```
